# Optimizing a Trainium2 kernel written in Bass

```python
import math
import jax
import jax.numpy as jnp
from jax import lax
import numpy as np

D_MODEL = 1024
BATCH = 1
SEQ = 256
DEPTH = 2

CHUNK = 64
D_MIX = D_MODEL
D_SSM = D_MIX // 2
SSM_GROUP_DIM = 16
SSM_GROUPS = D_SSM // SSM_GROUP_DIM
SSM_STATE = 64
D_ATTN = D_MIX - D_SSM
HEAD_DIM = 64
N_HEADS = D_ATTN // HEAD_DIM
N_KV_HEADS = 2
GQA_GROUP = N_HEADS // N_KV_HEADS
WINDOW = 128
WINDOW_CHUNKS = WINDOW // CHUNK
D_IN = D_SSM + D_ATTN + 2 * N_KV_HEADS * HEAD_DIM
D_FF = 2816
N_EXPERTS = 8
TOP_K = 2
D_FF_EXPERT = 3584
MOE_BLOCK = 128
N_DENSE = (DEPTH + 1) // 2
N_MOE = DEPTH // 2
RMS_EPS = 1e-6
NEG_INF = -1e30

kernel_name = "hybrid_s5_swa_sink_moe_adaln_trunk"

def rms_norm(x, g):
    xf = x.astype(jnp.float32)
    y = xf * lax.rsqrt(jnp.mean(xf * xf, axis=-1, keepdims=True) + RMS_EPS)
    return (y * g.astype(jnp.float32)).astype(x.dtype)

def modulate(h, shift, scale):
    return h * (1.0 + scale[:, None, :]) + shift[:, None, :]

def s5_mixer(u, lam_re, lam_im, b_re, b_im, c_re, c_im, d_skip, log_step, w_glu):
    bsz, L, _ = u.shape
    uf = u.astype(jnp.float32).reshape(bsz, L, SSM_GROUPS, SSM_GROUP_DIM)
    lam = lax.complex(lam_re.astype(jnp.float32), lam_im.astype(jnp.float32))
    step = jnp.exp(log_step.astype(jnp.float32))[:, None]
    lam_bar = jnp.exp(lam * step)
    b = lax.complex(b_re.astype(jnp.float32), b_im.astype(jnp.float32))
    b_bar = ((lam_bar - 1.0) / lam)[..., None] * b
    bu = jnp.einsum('gph,blgh->blgp', b_bar, uf.astype(jnp.complex64))
    a = jnp.broadcast_to(lam_bar, (1, L) + lam_bar.shape)

    def combine(e1, e2):
        a1, s1 = e1
        a2, s2 = e2
        return a1 * a2, a2 * s1 + s2

    _, states = lax.associative_scan(combine, (a, bu), axis=1)
    c = lax.complex(c_re.astype(jnp.float32), c_im.astype(jnp.float32))
    y = jnp.einsum('ghp,blgp->blgh', c, states).real
    y = y + d_skip.astype(jnp.float32).reshape(SSM_GROUPS, SSM_GROUP_DIM) * uf
    y = jax.nn.gelu(y.reshape(bsz, L, D_SSM))
    y = y * jax.nn.sigmoid(y @ w_glu.astype(jnp.float32))
    return y.astype(u.dtype)

def shift_chunks(t, s):
    if s == 0:
        return t
    return jnp.concatenate([jnp.zeros_like(t[:, :s]), t[:, :-s]], axis=1)

def swa_sink_attention(q, k, v, sinks):
    bsz, L, _ = q.shape
    nc = L // CHUNK
    qc = q.reshape(bsz, nc, CHUNK, N_KV_HEADS, GQA_GROUP, HEAD_DIM)
    kc = k.reshape(bsz, nc, CHUNK, N_KV_HEADS, HEAD_DIM)
    vc = v.reshape(bsz, nc, CHUNK, N_KV_HEADS, HEAD_DIM)
    shifts = list(reversed(range(WINDOW_CHUNKS)))
    kb = jnp.concatenate([shift_chunks(kc, s) for s in shifts], axis=2)
    vb = jnp.concatenate([shift_chunks(vc, s) for s in shifts], axis=2)
    scores = jnp.einsum('bcqkgd,bcjkd->bckgqj', qc, kb).astype(jnp.float32)
    scores = scores * (1.0 / math.sqrt(HEAD_DIM))
    chunk_idx = jnp.arange(nc)[:, None]
    key_shift = jnp.repeat(jnp.array(shifts, dtype=jnp.int32), CHUNK)[None, :]
    valid = chunk_idx - key_shift >= 0
    scores = jnp.where(valid[None, :, None, None, None, :], scores, NEG_INF)
    sink = sinks.astype(jnp.float32).reshape(N_KV_HEADS, GQA_GROUP)[None, None, :, :, None, None]
    sink = jnp.broadcast_to(sink, scores.shape[:-1] + (1,))
    probs = jax.nn.softmax(jnp.concatenate([scores, sink], axis=-1), axis=-1)[..., :-1]
    out = jnp.einsum('bckgqj,bcjkd->bcqkgd', probs.astype(vb.dtype), vb)
    return out.reshape(bsz, L, D_ATTN)

def dense_swiglu(h, w_gate, w_up, w_down):
    return (jax.nn.silu(h @ w_gate) * (h @ w_up)) @ w_down

def moe_swiglu(h, w_router, w_gate, w_up, w_down):
    bsz, L, d = h.shape
    T = bsz * L
    A = T * TOP_K
    R = A + N_EXPERTS * MOE_BLOCK
    n_blocks = R // MOE_BLOCK
    hf = h.reshape(T, d)
    logits = (hf @ w_router).astype(jnp.float32)
    top_vals, top_idx = lax.top_k(logits, TOP_K)
    gates = jax.nn.softmax(top_vals, axis=-1)
    flat_e = top_idx.reshape(-1)
    order = jnp.argsort(flat_e)
    sorted_e = flat_e[order]
    tok = order // TOP_K
    w_sorted = gates.reshape(-1)[order]
    sizes = jnp.bincount(flat_e, length=N_EXPERTS).astype(jnp.int32)
    starts = jnp.cumsum(sizes) - sizes
    padded = ((sizes + MOE_BLOCK - 1) // MOE_BLOCK) * MOE_BLOCK
    padded_ends = jnp.cumsum(padded)
    padded_starts = padded_ends - padded
    rank = jnp.arange(A, dtype=jnp.int32) - starts[sorted_e]
    dest = padded_starts[sorted_e] + rank
    xs_buf = jnp.zeros((R, d), hf.dtype).at[dest].set(hf[tok])
    block_starts = jnp.arange(n_blocks, dtype=jnp.int32) * MOE_BLOCK
    block_e = jnp.clip(jnp.searchsorted(padded_ends, block_starts, side='right'), 0, N_EXPERTS - 1)

    def expert_block(args):
        xb, e = args
        return (jax.nn.silu(xb @ w_gate[e]) * (xb @ w_up[e])) @ w_down[e]

    ys_buf = lax.map(expert_block, (xs_buf.reshape(n_blocks, MOE_BLOCK, d), block_e))
    ys = ys_buf.reshape(R, d)[dest] * w_sorted[:, None].astype(hf.dtype)
    out = jnp.zeros((T, d), hf.dtype).at[tok].add(ys)
    return out.reshape(bsz, L, d)

def setup_inputs(seed: int = 0) -> dict:
    key = jax.random.key(seed)
    ks = jax.random.split(key, 32)
    f32 = jnp.float32

    def nrm(k, shape, scale):
        return jax.random.normal(k, shape, f32) * scale

    def gain(k, shape):
        return 1.0 + 0.02 * jax.random.normal(k, shape, f32)

    inputs = {}
    inputs["x"] = nrm(ks[0], (BATCH, SEQ, D_MODEL), 1.0)
    inputs["c"] = nrm(ks[1], (BATCH, D_MODEL), 1.0)
    inputs["norm_mix_g"] = gain(ks[2], (DEPTH, D_MODEL))
    inputs["norm_ffn_g"] = gain(ks[3], (DEPTH, D_MODEL))
    inputs["w_ada"] = nrm(ks[4], (DEPTH, D_MODEL, 6 * D_MODEL), 0.5 * D_MODEL ** -0.5)
    inputs["b_ada"] = nrm(ks[5], (DEPTH, 6 * D_MODEL), 0.02)
    inputs["w_in"] = nrm(ks[6], (DEPTH, D_MODEL, D_IN), D_MODEL ** -0.5)
    inputs["ssm_lam_re"] = -0.5 + 0.01 * jax.random.normal(ks[7], (DEPTH, SSM_GROUPS, SSM_STATE), f32)
    inputs["ssm_lam_im"] = (math.pi * jnp.arange(SSM_STATE, dtype=f32))[None, None, :] \
        + 0.01 * jax.random.normal(ks[8], (DEPTH, SSM_GROUPS, SSM_STATE), f32)
    inputs["ssm_b_re"] = nrm(ks[9], (DEPTH, SSM_GROUPS, SSM_STATE, SSM_GROUP_DIM), (2 * SSM_GROUP_DIM) ** -0.5)
    inputs["ssm_b_im"] = nrm(ks[10], (DEPTH, SSM_GROUPS, SSM_STATE, SSM_GROUP_DIM), (2 * SSM_GROUP_DIM) ** -0.5)
    inputs["ssm_c_re"] = nrm(ks[11], (DEPTH, SSM_GROUPS, SSM_GROUP_DIM, SSM_STATE), SSM_STATE ** -0.5)
    inputs["ssm_c_im"] = nrm(ks[12], (DEPTH, SSM_GROUPS, SSM_GROUP_DIM, SSM_STATE), SSM_STATE ** -0.5)
    inputs["ssm_d"] = nrm(ks[13], (DEPTH, D_SSM), 1.0)
    inputs["ssm_log_step"] = jax.random.uniform(ks[14], (DEPTH, SSM_GROUPS), f32,
                                                math.log(1e-3), math.log(1e-1))
    inputs["ssm_w_glu"] = nrm(ks[15], (DEPTH, D_SSM, D_SSM), D_SSM ** -0.5)
    inputs["attn_sinks"] = nrm(ks[16], (DEPTH, N_HEADS), 0.5)
    inputs["out_norm_ssm_g"] = gain(ks[17], (DEPTH, D_SSM))
    inputs["out_norm_attn_g"] = gain(ks[18], (DEPTH, D_ATTN))
    inputs["w_out"] = nrm(ks[19], (DEPTH, D_MIX, D_MODEL), D_MIX ** -0.5)
    inputs["ffn_w_gate"] = nrm(ks[20], (N_DENSE, D_MODEL, D_FF), D_MODEL ** -0.5)
    inputs["ffn_w_up"] = nrm(ks[21], (N_DENSE, D_MODEL, D_FF), D_MODEL ** -0.5)
    inputs["ffn_w_down"] = nrm(ks[22], (N_DENSE, D_FF, D_MODEL), D_FF ** -0.5)
    inputs["moe_w_router"] = nrm(ks[23], (N_MOE, D_MODEL, N_EXPERTS), D_MODEL ** -0.5)
    inputs["moe_w_gate"] = nrm(ks[24], (N_MOE, N_EXPERTS, D_MODEL, D_FF_EXPERT), D_MODEL ** -0.5)
    inputs["moe_w_up"] = nrm(ks[25], (N_MOE, N_EXPERTS, D_MODEL, D_FF_EXPERT), D_MODEL ** -0.5)
    inputs["moe_w_down"] = nrm(ks[26], (N_MOE, N_EXPERTS, D_FF_EXPERT, D_MODEL), D_FF_EXPERT ** -0.5)
    inputs["final_norm_g"] = gain(ks[27], (D_MODEL,))
    return inputs

def reference(x, c, norm_mix_g, norm_ffn_g, w_ada, b_ada, w_in, ssm_lam_re, ssm_lam_im,
              ssm_b_re, ssm_b_im, ssm_c_re, ssm_c_im, ssm_d, ssm_log_step, ssm_w_glu,
              attn_sinks, out_norm_ssm_g, out_norm_attn_g, w_out, ffn_w_gate, ffn_w_up,
              ffn_w_down, moe_w_router, moe_w_gate, moe_w_up, moe_w_down, final_norm_g):
    c_act = jax.nn.silu(c)
    kv_w = N_KV_HEADS * HEAD_DIM
    for l in range(DEPTH):
        mod = c_act @ w_ada[l] + b_ada[l]
        sh_m, sc_m, g_m, sh_f, sc_f, g_f = jnp.split(mod, 6, axis=-1)

        h = modulate(rms_norm(x, norm_mix_g[l]), sh_m, sc_m)
        proj = h @ w_in[l]
        u_ssm = proj[..., :D_SSM]
        q = proj[..., D_SSM:D_SSM + D_ATTN]
        k = proj[..., D_SSM + D_ATTN:D_SSM + D_ATTN + kv_w]
        v = proj[..., D_SSM + D_ATTN + kv_w:]
        y_ssm = s5_mixer(u_ssm, ssm_lam_re[l], ssm_lam_im[l], ssm_b_re[l], ssm_b_im[l],
                         ssm_c_re[l], ssm_c_im[l], ssm_d[l], ssm_log_step[l], ssm_w_glu[l])
        y_attn = swa_sink_attention(q, k, v, attn_sinks[l])
        y = jnp.concatenate([rms_norm(y_ssm, out_norm_ssm_g[l]),
                             rms_norm(y_attn, out_norm_attn_g[l])], axis=-1) @ w_out[l]
        x = x + g_m[:, None, :] * y

        h = modulate(rms_norm(x, norm_ffn_g[l]), sh_f, sc_f)
        if l % 2 == 0:
            i = l // 2
            f = dense_swiglu(h, ffn_w_gate[i], ffn_w_up[i], ffn_w_down[i])
        else:
            i = l // 2
            f = moe_swiglu(h, moe_w_router[i], moe_w_gate[i], moe_w_up[i], moe_w_down[i])
        x = x + g_f[:, None, :] * f
    return rms_norm(x, final_norm_g)


_drawn_inputs = setup_inputs


def setup_inputs(seed=0):
    import zlib

    import numpy as np

    out = dict(_drawn_inputs(seed))
    spreads = {}
    factors = {'norm_mix_g': 4.664,
     'norm_ffn_g': 3.512,
     'ssm_lam_re': 25.665,
     'ssm_b_re': 2.813,
     'ssm_c_re': 2.715,
     'attn_sinks': 64.0,
     'out_norm_ssm_g': 6.037,
     'out_norm_attn_g': 4.902,
     'final_norm_g': 9.881}
    for name, (base, spread) in spreads.items():
        noise = np.random.default_rng([zlib.crc32(name.encode()), seed]).standard_normal(out[name].shape)
        drawn = base * np.exp(spread * noise) if base else spread * noise
        out[name] = jnp.asarray(drawn.astype(out[name].dtype))
    for name, factor in factors.items():
        out[name] = (out[name] * factor).astype(out[name].dtype)
    return out
```

```python
import math
from contextlib import ExitStack

import concourse.bass as bass
from concourse import mybir

F32 = mybir.dt.float32
F32R = mybir.dt.float32r
I32 = mybir.dt.int32
ALU = mybir.AluOpType
ACT = mybir.ActivationFunctionType
AX = mybir.AxisListType.X

P = 128
D = 1024
KC = D // P
T = 256
TT = T // P
DEPTH = 2
D_SSM, GROUP, STATE = 512, 16, 64
UT = D_SSM // P
PAIRS = (D_SSM // GROUP) * STATE // P
GT = P // GROUP
HD, HEADS, KVH = 64, 8, 2
HPK = HEADS // KVH
CH = 64
NCH = T // CH
D_FF = 2816
FT = D_FF // P
E, F_E = 8, 3584
FE_T = F_E // P
FG = F_E // 512
CAP = P
JOBS = E * (T // CAP)
EPS = 1e-6
NEG = -1e30
TWO_PI_HI = 6.28125
TWO_PI_MID = math.floor((2 * math.pi - TWO_PI_HI) * 2 ** 21) / 2 ** 21
TWO_PI_LO = 2 * math.pi - TWO_PI_HI - TWO_PI_MID
ROUND = 1.5 * 2.0 ** 23

SLOTS = 7
UNIT = 1024
SPLITS = 4
PER_JOB = 4 * FG + FE_T // 2
UPJ = 2 * PER_JOB

PRM = {}
_at = 0
for _name, _n in (("b_ada", 48), ("g_mix", 8), ("g_ffn", 8), ("lam_re", PAIRS), ("lam_im", PAIRS),
                  ("log_step", PAIRS), ("d_skip", UT), ("g_ssm", UT), ("g_attn", UT), ("sinks", HEADS)):
    PRM[_name] = (_at, _at + _n)
    _at += _n
N_PRM = _at
CST = {}
_at = 0
for _name, _n in (("ident", P), ("before", P), ("ones", P), ("iota", P), ("mask_ch", GT), ("mask_st", 4 * GT)):
    CST[_name] = (_at, _at + _n)
    _at += _n
N_CST = _at
SH_M, SC_M, G_M, SH_F, SC_F, G_F = range(6)


def build(nc, x, small, prm, bc, cst, w_ada, b_ada, w_in, w_glu, w_out, w_gate, w_up, w_down,
          moe_gate, moe_up, moe_down, final_g, out):
    with ExitStack() as ctx:
        sem = lambda name: ctx.enter_context(nc.semaphore(name))
        at = [(nc.sbuf_base + 63) // 64 * 64]

        def place(name, shape, dt=F32, offset=None):
            size = 4
            for n in shape[1:]:
                size *= n
            if offset is None:
                offset = at[0]
                at[0] += (size + 63) // 64 * 64
            return nc.alloc_sbuf_tensor_at(name, shape, dt, offset=offset)

        def region(nbytes):
            start = at[0]
            at[0] += nbytes
            return start

        ring = place("ring", [P, SLOTS, 2048])
        r_split = region(4 * 8192)
        r_tab = region(32768)
        r_blk = region(32768)
        xs = place("xs", [P, TT, D])
        xn = place("xn", [P, TT, D])
        r_hT = region(8192)
        hT = place("hT", [P, KC, T], offset=r_hT)
        gate_m = place("gate_m", [P, D])
        gate_f = place("gate_f", [P, D])
        k_st = place("k_st", [P, N_CST])
        prms = place("prms", [P, DEPTH, N_PRM])
        smalls = place("smalls", [P, KC + KC * E])
        c_act = place("c_act", [P, KC])
        r_wide = region(4096)
        c_wide = place("c_wide", [P, KC, P], offset=r_wide)
        gate_f1 = place("gate_f1", [P, D], offset=r_wide)
        mod_raw = place("mod_raw", [P, 6 * KC])
        mod_a = place("mod_a", [P, 2, KC])
        mod_s = place("mod_s", [P, 2, KC])
        sq_sum = place("sq_sum", [P, TT])
        rstd = place("rstd", [P, TT])
        head_ss = place("head_ss", [P, 4])
        head_rs = place("head_rs", [P, 4])
        sv = {n: place("sv_" + n, [P, DEPTH, PAIRS]) for n in
              ("step", "dec", "cr", "ci", "t1", "t2", "t3")}
        pw_c = place("pw_c", [P, 8, DEPTH, PAIRS])
        pw_s = place("pw_s", [P, 8, DEPTH, PAIRS])
        sinks_e = place("sinks_e", [P, TT, HEADS])
        s_max = place("s_max", [P, TT, HEADS])
        s_den = place("s_den", [P, TT, HEADS])
        yT = place("yT", [P, 2 * UT, T], offset=r_split)
        uT = place("uT", [P, UT, T], offset=r_split + 8192)
        sig = place("sig", [P, UT, T], offset=r_split + 8192)
        qT = place("qT", [P, HPK, T], offset=r_split + 12288)
        kz = place("kz", [P, KVH, T], offset=r_split + 16384)
        vt = place("vt", [P, 3, P], offset=r_split + 18432)
        rot_a = place("rot_a", [P, 2, T], offset=r_split + 20480)
        rot_b = place("rot_b", [P, 2, T], offset=r_split + 22528)
        st_re = place("st_re", [P, 2, T], offset=r_split + 24576)
        st_im = place("st_im", [P, 2, T], offset=r_split + 26624)
        st_t = place("st_t", [P, 2, T], offset=r_split + 28672)
        bcs = place("bcs", [P, 4, 256], offset=r_split + 24576)
        resid = place("resid", [P, 2, 512], offset=r_split + 20480)
        tab_t = [place("tab_t0", [P, PAIRS, P], offset=r_split), xn[:].rearrange("p t (q n) -> p (t q) n", n=P)]
        cos_t = place("cos_t", [P, PAIRS, T], offset=r_tab)
        sin_t = place("sin_t", [P, PAIRS, T], offset=r_tab + 16384)
        b_re = place("b_re", [P, PAIRS, P], offset=r_blk)
        b_im = place("b_im", [P, PAIRS, P], offset=r_blk + 8192)
        c_re = place("c_re", [P, PAIRS, P], offset=r_blk + 16384)
        c_im = place("c_im", [P, PAIRS, P], offset=r_blk + 24576)
        z = xn[:, :, :].rearrange("p t (c n) -> p (t c) n", n=512)
        z_re = [z[:, 2 * b, :].rearrange("p (q n) -> p q n", q=2) for b in range(2)]
        z_im = [z[:, 2 * b + 1, :].rearrange("p (q n) -> p q n", q=2) for b in range(2)]
        sc = xn[:, :, :].rearrange("p t (h n) -> p t h n", h=HEADS)
        pT = place("pT", [P, TT, HEADS, P], offset=r_hT)
        a_T = place("a_T", [P, FT, T], offset=r_blk)
        hT_hi = place("hT_hi", [P, KC, T], F32R, offset=r_blk + FT * T * 4)
        hT_lo = place("hT_lo", [P, KC, T], F32R, offset=r_hT)
        sil = place("sil", [P, 2 * T], offset=r_blk + FT * T * 4 + 8192)
        w_hi = [place(f"w_hi{i}", [P, UNIT], F32R, offset=r_split + 8192 * i) for i in range(SPLITS)]
        w_lo = [place(f"w_lo{i}", [P, UNIT], F32R, offset=r_split + 8192 * i + 4096) for i in range(SPLITS)]
        e_act = place("e_act", [P, F_E], offset=r_tab)
        eT_hi = place("eT_hi", [P, FE_T, P], F32R, offset=r_tab + 14336)
        eT_lo = place("eT_lo", [P, FE_T, P], F32R, offset=r_tab + 28672)
        hg = place("hg", [P, KC, P], offset=r_tab + 43008)
        hg_hi = place("hg_hi", [P, KC, P], F32R, offset=r_tab + 47104)
        hg_lo = place("hg_lo", [P, KC, P], F32R, offset=r_tab + 51200)
        y_sb = place("y_sb", [P, D], offset=r_tab + 55296)
        e_sil = place("e_sil", [P, 512], offset=r_tab + 59392)
        sel = place("sel", [P, TT, CAP], offset=r_tab + 61440)
        selT = place("selT", [P, TT, P], offset=r_tab + 62464)
        r_acc = region(8192)
        acc = place("acc", [P, TT, D], offset=r_acc)
        mod_acc = place("mod_acc", [P, 2, 512], offset=r_acc)
        mod_diag = place("mod_diag", [P, 4, P], offset=r_acc + 4096)
        lg = place("lg", [P, TT, E])
        top = place("top", [P, TT, 8])
        idx = place("idx", [P, TT, 8], mybir.dt.uint32)
        idx_f = place("idx_f", [P, TT, 8])
        g1 = place("g1", [P, TT])
        g2 = place("g2", [P, TT])
        oh1 = place("oh1", [P, TT, E])
        oh2 = place("oh2", [P, TT, E])
        chosen = place("chosen", [P, TT, JOBS + 1])
        rank = place("rank", [P, TT, JOBS + 1])
        gate_of = place("gate_of", [P, TT, JOBS + 1])
        over_f = place("over_f", [P, 1])
        over = place("over", [P, 1], I32)
        assert at[0] <= nc.sbuf_usable_end, at[0]

        ps = ctx.enter_context(nc.psum_tensor("ps", [P, 8, 512], F32))

        def mod_bank(m):
            return m % 2 if m < 10 + GG - 1 else 2 + m % 2

        def const(name):
            a, b = CST[name]
            return k_st[:, a:b]

        def par(l, name):
            a, b = PRM[name]
            return prms[:, l, a:b]

        ident, ones = const("ident"), const("ones")
        mask_ch = const("mask_ch")
        mask_st = const("mask_st").rearrange("p (a g) -> p a g", g=GT)
        c_col = smalls[:, 0:KC]
        w_router = smalls[:, KC:KC + KC * E].rearrange("p (k e) -> p k e", e=E)

        loaded = [sem(f"slot{i}_loaded") for i in range(SLOTS)]
        small_in, x_in, bc_in, gbias_in, fg_in, stored = (
            sem(n) for n in ("small_in", "x_in", "bc_in", "gbias_in", "fg_in", "stored"))
        c_silu, c_spread = sem("c_silu"), sem("c_spread")
        mod_psum, mod_taken, mod_summed, mod_mix, mod_ffn = (
            sem(n) for n in ("mod_psum", "mod_taken", "mod_summed", "mod_mix", "mod_ffn"))
        x_updated, squares, variance, deviation, normed = (
            sem(n) for n in ("x_updated", "squares", "variance", "deviation", "normed"))
        turned, hT_dve, hT_act = sem("turned"), sem("hT_dve"), sem("hT_act")
        projected, proj_out = sem("projected"), sem("proj_out")
        sv_step, sv_angle, sv_trig, sv_ready = (sem(n) for n in ("sv_step", "sv_angle", "sv_trig", "sv_ready"))
        table0, table1 = sem("table0"), sem("table1")
        matrices, bu_psum, bu_used, scanned, rotated = (
            sem(n) for n in ("matrices", "bu_psum", "bu_used", "scanned", "rotated"))
        y_psum, y_skip, y_gelu = sem("y_psum"), sem("y_skip"), sem("y_gelu")
        glu_psum, glu_sig, ssm_sq, attn_sq, ss_psum = (
            sem(n) for n in ("glu_psum", "glu_sig", "ssm_sq", "attn_sq", "ss_psum"))
        kz_zero = sem("kz_zero")
        scores, shifted, exps, probs, probs_T, pT_act, pT_dve, pv_psum = (
            sem(n) for n in ("scores", "shifted", "exps", "probs", "probs_T", "pT_act", "pT_dve", "pv_psum"))
        head_var, head_dev, head_ready = sem("head_var"), sem("head_dev"), sem("head_ready")
        out_psum, hT_high, hT_split, gu_silu, gu_out, down_psum = (
            sem(n) for n in ("out_psum", "hT_high", "hT_split", "gu_silu", "gu_out", "down_psum"))
        logits, diff, diff_e, picked, rank_psum, routed = (
            sem(n) for n in ("logits", "diff", "diff_e", "picked", "rank_psum", "routed"))
        e_high, e_low, e_free = sem("e_high"), sem("e_low"), sem("e_free")
        e_silu, e_prod, e_turned, eT_high, eT_ready = (
            sem(n) for n in ("e_silu", "e_prod", "e_turned", "eT_high", "eT_ready"))
        sel_made, sel_turned, selT_ready, gathered, hg_mod, hg_high, hg_ready = (
            sem(n) for n in ("sel_made", "sel_turned", "selT_ready", "gathered", "hg_mod", "hg_high", "hg_ready"))
        y_out, scattered, added = sem("y_out"), sem("scattered"), sem("added")
        dve_step, dve_job, act_step, pool_step = (
            sem(n) for n in ("dve_step", "dve_job", "act_step", "pool_step"))

        def chain(eng, s):
            done = [0]

            def link(ins):
                done[0] += 1
                ins.then_inc(s, 1)
                eng.wait_ge(s, done[0])
            return link

        stream = []

        def cols(w, k0, kn, c0, cn):
            return w.rearrange("(k p) n -> p k n", p=P)[:, k0:k0 + kn, c0:c0 + cn]

        ON_DVE = [(0, 5), (0, 7), (0, 9), (0, 10), (0, 11)] + [(1, cg) for cg in range(12)]
        MODS = [(0, cg) for cg in range(12)] + [(1, cg) for cg in range(12)]

        def stream_mod(l, cg):
            if (l, cg) in ON_DVE:
                used = (mod_summed, ON_DVE.index((l, cg)) + 1)
            else:
                used = (mod_psum, MODS.index((l, cg)) + 1)
            for half in range(2):
                stream.append((cols(w_ada[l], 4 * half, 4, 512 * cg, 512), (4, 512), used))
            at_mod[l, cg] = len(stream) - 2

        FFN_MODS = MODS[10:]
        GG = FT // 2
        at_mod, at_in, at_glu, at_out, at_gu, at_down = {}, {}, {}, {}, {}, {}
        for l in range(DEPTH):
            if l == 0:
                for cg in range(4):
                    stream_mod(0, cg)
            for u in range(2):
                at_in[l, u] = len(stream)
                stream.append((cols(w_in[l], 0, KC, 256 * u, 256), (KC, 256), (projected, 12 * l + 2 * u + 2)))
            for j in range(8):
                if j in (0, 2, 4):
                    at_in[l, 2 + j // 2] = len(stream)
                    stream.append((cols(w_in[l], 0, KC, 512 + 128 * j, 256), (KC, 256),
                                   (projected, 12 * l + (6, 0, 8, 0, 12)[j])))
                if l == 0 and j < 6:
                    stream_mod(0, 4 + j)
            at_glu[l] = len(stream)
            stream.append((cols(w_glu[l], 0, UT, 0, D_SSM), (UT, D_SSM), (glu_psum, 4 * l + 4)))
            for n in range(4):
                at_out[l, n] = len(stream)
                stream.append((cols(w_out[l], 4 * (n % 2), 4, 512 * (n // 2), 512), (4, 512), (out_psum, 4 * l + n + 1)))
            if l == 0:
                for g in range(GG):
                    at_gu[g] = len(stream)
                    for i, w in enumerate((w_gate, w_up)):
                        stream.append((cols(w[0], 0, KC, 256 * g, 256), (KC, 256), (e_low, 4 * g + 2 * i + 2)))
                    stream_mod(*FFN_MODS[g])
                for n in range(GG):
                    at_down[n] = len(stream)
                    stream.append((cols(w_down[0], 2 * n, 2, 0, D), (2, D), (down_psum, n + 1)))
                    if n in (1, 4, 7):
                        stream_mod(*FFN_MODS[GG + n // 3])
        U0 = 4 * GG
        base = len(stream)

        def slot(n, shape):
            return ring[:, n % SLOTS, :].rearrange("p (a b) -> p a b", a=shape[0])

        def chunk(eng, n):
            eng.wait_ge(loaded[n % SLOTS], 16 * (n // SLOTS + 1))
            return slot(n, stream[n][1])

        assert PER_JOB % SLOTS == 0 and UPJ % SPLITS == 0 and U0 % SPLITS == 0 and len(FFN_MODS) == GG + 3
        turns = PER_JOB // SLOTS

        def loaded_by(job, k):
            return 16 * ((base + k) // SLOTS + 1) + 16 * turns * job

        block = ctx.enter_context(nc.Block())

        @block.sync
        def _(sp):
            sp.dma_start(smalls[:], small).then_inc(small_in, 16)
            sp.dma_start(prms[:], prm).then_inc(small_in, 16)
            sp.dma_start(k_st[:], cst).then_inc(small_in, 16)
            sp.dma_start(xs[:], x[0].rearrange("(t p) d -> p t d", p=P)).then_inc(x_in, 16)

            def load(n):
                src, shape, _ = stream[n]
                if n >= SLOTS:
                    s, v = stream[n - SLOTS][2]
                    sp.wait_ge(s, v)
                sp.dma_start(slot(n, shape), src).then_inc(loaded[n % SLOTS], 16)

            for n in range(base):
                load(n)

            def load_job(job, expert, first=False):
                def expert_cols(w, k0, kn, c0, cn):
                    return w[bass.ds(expert, 1)].rearrange("a (k p) n -> p (a k) n", p=P)[:, k0:k0 + kn, c0:c0 + cn]
                for k in range(PER_JOB):
                    if k < 4 * FG:
                        w = (moe_gate, moe_up)[k // 2 % 2][0]
                        src, shape = expert_cols(w, 4 * (k % 2), 4, 512 * (k // 4), 512), (4, 512)
                    else:
                        src, shape = expert_cols(moe_down[0], 2 * (k - 4 * FG), 2, 0, D), (2, D)
                    if first and k < SLOTS:
                        sp.wait_ge(*stream[base + k - SLOTS][2])
                    else:
                        sp.wait_ge(e_low, U0 + UPJ * job + 2 * (k - SLOTS + 1))
                    sp.dma_start(slot(base + k, shape), src).then_inc(loaded[(base + k) % SLOTS], 16)

            load_job(0, 0, first=True)
            with sp.Fori(1, E) as job:
                load_job(job, job)
            sp.wait_ge(routed, 1)
            more = sp.value_load(over[0:1, 0:1], min_val=0, max_val=1)
            with sp.If(more > 0):
                with sp.Fori(E, JOBS) as job:
                    load_job(job, job - E)
            with sp.Else():
                sp.nop()
            sp.wait_ge(normed, 5)
            sp.dma_start(out[0].rearrange("(t p) d -> p t d", p=P), xn[:]).then_inc(stored, 16)
            sp.wait_ge(stored, 16)

        def make_table(eng, ops, l, link, ready):
            ops.memset(cos_t[:, :, 0:1], 1.0)
            link(ops.memset(sin_t[:, :, 0:1], 0.0))
            for m in range(8):
                n = 1 << m
                wide = lambda v: v[:, m, l, :].unsqueeze(2).to_broadcast([P, PAIRS, n])
                cl, sl = wide(pw_c), wide(pw_s)
                c0, s0 = cos_t[:, :, 0:n], sin_t[:, :, 0:n]
                c1, s1 = cos_t[:, :, n:2 * n], sin_t[:, :, n:2 * n]
                tt = tab_t[l][:, :, 0:n]
                ops.tensor_tensor(c1, c0, cl, ALU.mult)
                link(ops.tensor_tensor(tt, s0, sl, ALU.mult))
                link(ops.tensor_tensor(c1, c1, tt, ALU.subtract))
                ops.tensor_tensor(s1, s0, cl, ALU.mult)
                link(ops.tensor_tensor(tt, c0, sl, ALU.mult))
                ins = ops.tensor_tensor(s1, s1, tt, ALU.add)
                if m < 7:
                    link(ins)
            ins.then_inc(ready, 1)
            eng.wait_ge(ready, 1)

        @block.gpsimd
        def _(pool):
            link = chain(pool, pool_step)

            def load_params(l):
                if l:
                    pool.wait_ge(gu_out, GG)
                pool.dma_start(bcs[:], bc[l]).then_inc(bc_in, 16)

            def load_gate(dst, src, s):
                pool.dma_start(dst[:], src.partition_broadcast(P)).then_inc(s, 16)

            def make_matrices(l):
                pool.wait_ge(bc_in, 16 * (l + 1))
                pool.wait_ge(small_in, 48)
                pool.wait_ge(sv_ready, 1)
                if l:
                    pool.wait_ge(down_psum, FT // 2)
                for m, dst in ((0, b_re), (1, b_im)):
                    o = dst[:].rearrange("p (u q) (b s) -> p u (q b) s", u=UT, b=2)
                    v = bcs[:, m, :].rearrange("p (u s) -> p u s", u=UT)
                    nc.gpsimd.tensor_tensor(o, v.unsqueeze(2).to_broadcast([P, UT, GT, STATE]),
                                            mask_ch.unsqueeze(1).unsqueeze(3).to_broadcast([P, UT, GT, STATE]),
                                            ALU.mult)
                cre, cim = (bcs[:, m, :].rearrange("p (q h) -> p q h", h=GROUP) for m in (2, 3))
                t0, t1 = (st_t[:, m, :].rearrange("p (q h) -> p q h", h=GROUP) for m in (0, 1))
                kr, ki, nkr, nki = (sv[n][:, l, :].unsqueeze(2).to_broadcast([P, PAIRS, GROUP])
                                    for n in ("cr", "ci", "t1", "t2"))
                nc.gpsimd.tensor_tensor(t0, cre, kr, ALU.mult)
                link(nc.gpsimd.tensor_tensor(t1, cim, ki, ALU.mult))
                nc.gpsimd.tensor_tensor(t0, t0, t1, ALU.subtract)
                nc.gpsimd.tensor_tensor(cre, cre, nki, ALU.mult)
                link(nc.gpsimd.tensor_tensor(cim, cim, nkr, ALU.mult))
                link(nc.gpsimd.tensor_tensor(cre, cre, cim, ALU.add))
                for v, dst in ((t0, c_re), (cre, c_im)):
                    for u in range(UT):
                        o = dst[:, 4 * u:4 * u + 4, :].rearrange("p q (g h) -> p q g h", h=GROUP)
                        ins = nc.gpsimd.tensor_tensor(
                            o, v[:, 4 * u:4 * u + 4, :].unsqueeze(2).to_broadcast([P, 4, GT, GROUP]),
                            mask_st.unsqueeze(3).to_broadcast([P, 4, GT, GROUP]), ALU.mult)
                ins.then_inc(matrices, 1)

            def turn_back(l, j):
                pool.wait_ge(scanned, 8 * l + j + 1)
                if 8 * l + j:
                    pool.wait_ge(y_psum, 8 * l + j)
                if j == 0:
                    pool.wait_ge(matrices, l + 1)
                q0 = 2 * j
                zr, zi = z_re[j % 2], z_im[j % 2]
                cs, sn = cos_t[:, q0:q0 + 2, :], sin_t[:, q0:q0 + 2, :]
                nc.gpsimd.tensor_tensor(st_re[:], zr, cs, ALU.mult)
                link(nc.gpsimd.tensor_tensor(st_im[:], zi, sn, ALU.mult))
                link(nc.gpsimd.tensor_tensor(st_re[:], st_re[:], st_im[:], ALU.subtract))
                nc.gpsimd.tensor_tensor(st_im[:], zr, sn, ALU.mult)
                link(nc.gpsimd.tensor_tensor(st_t[:], zi, cs, ALU.mult))
                nc.gpsimd.tensor_tensor(st_im[:], st_im[:], st_t[:], ALU.add).then_inc(rotated, 1)

            load_params(0)
            load_gate(gate_m, b_ada[0, G_M * D:(G_M + 1) * D], gbias_in)
            load_gate(gate_f, b_ada[0, G_F * D:(G_F + 1) * D], gbias_in)
            nc.gpsimd.memset(kz[:], 0.0).then_inc(kz_zero, 1)
            make_matrices(0)
            for j in range(8):
                turn_back(0, j)
            pool.wait_ge(x_updated, 1)
            pool.wait_ge(gbias_in, 32)
            load_gate(gate_m, b_ada[1, G_M * D:(G_M + 1) * D], gbias_in)
            pool.wait_ge(bu_used, 8)
            pool.wait_ge(out_psum, 4)
            pool.wait_ge(mod_psum, 9)
            pool.wait_ge(gbias_in, 48)
            load_gate(gate_f1, b_ada[1, G_F * D:(G_F + 1) * D], gbias_in)
            pool.wait_ge(turned, 8)
            make_table(pool, nc.gpsimd, 1, link, table1)
            load_params(1)
            nc.gpsimd.memset(kz[:], 0.0).then_inc(kz_zero, 1)
            make_matrices(1)
            for j in range(8):
                turn_back(1, j)
            pool.wait_ge(x_updated, 3)
            load_gate(gate_m, final_g, fg_in)

        @block.scalar
        def _(act):
            link = chain(act, act_step)
            A = nc.scalar.activation

            def norm(n):
                act.wait_ge(x_updated, n) if n else act.wait_ge(x_in, 16)
                if n == 2:
                    act.wait_ge(table1, 1)
                for t in range(TT):
                    A(xn[:, t, :], xs[:, t, :], ACT.Square, accum_out=sq_sum[:, t:t + 1]).then_inc(squares, 1)
                act.wait_ge(variance, n + 1)
                A(rstd[:], rstd[:], ACT.Sqrt).then_inc(deviation, 1)

            def modulate(n):
                which = n % 2
                act.wait_ge((mod_mix, mod_ffn)[which], n // 2 + 1)
                act.wait_ge(turned, 4 * (n + 1))
                for kc in range(4, KC):
                    A(hT[:, kc, :], ps[:, 2 + kc // 2, 256 * (kc % 2):256 * (kc % 2) + 256], ACT.Identity,
                      bias=mod_s[:, which, kc:kc + 1], scale=mod_a[:, which, kc:kc + 1]).then_inc(hT_act, 1)

            act.wait_ge(small_in, 48)
            A(c_act[:], c_col, ACT.Silu).then_inc(c_silu, 1)
            a, b = PRM["log_step"]
            A(sv["step"][:], prms[:, :, a:b], ACT.Exp).then_inc(sv_step, 1)
            norm(0)
            act.wait_ge(sv_angle, 1)
            A(sv["dec"][:], sv["dec"][:], ACT.Exp)
            A(pw_s[:], pw_c[:], ACT.Sin)
            A(pw_c[:], pw_c[:], ACT.Sin, scale=0.5).then_inc(sv_trig, 1)

            for l in range(DEPTH):
                if l:
                    norm(2)
                modulate(2 * l)
                for u in range(UT):
                    act.wait_ge(projected, 12 * l + u + 1)
                    nc.scalar.copy(uT[:, u, :], ps[:, 2 + u, 0:T]).then_inc(proj_out, 1)

                def gelu(u):
                    act.wait_ge(y_skip, 4 * l + u + 1)
                    A(yT[:, u, :], yT[:, u, :], ACT.Gelu_apprx_tanh).then_inc(y_gelu, 1)

                for j in range(8):
                    act.wait_ge(projected, 12 * l + 5 + j)
                    bank = ps[:, 7, 0:T]
                    if j < 4:
                        nc.scalar.mul(qT[:, j, :], bank, HD ** -0.5).then_inc(proj_out, 1)
                    elif j == 4:
                        act.wait_ge(kz_zero, l + 1)
                        link(nc.scalar.copy(kz[0:HD, 0, :], ps[0:HD, 7, 0:T]))
                        nc.scalar.copy(kz[HD:P, 1, :], ps[HD:P, 7, 0:T]).then_inc(proj_out, 1)
                    else:
                        nc.scalar.copy(vt[:, j - 5, :], ps[:, 7, 0:P]).then_inc(proj_out, 1)
                    if j in (4, 6):
                        gelu(j // 2 - 2)
                gelu(2)
                gelu(3)
                act.wait_ge(shifted, l + 1)
                A(sc, sc, ACT.Exp).then_inc(exps, 1)
                A(sinks_e[:], sinks_e[:], ACT.Exp).then_inc(exps, 1)
                for o in range(UT):
                    act.wait_ge(glu_psum, 4 * l + o // 2 * 2 + 2)
                    if o == 0:
                        act.wait_ge(y_skip, 4 * l + 4)
                    A(sig[:, o, :], ps[:, 6 + o // 2, 256 * (o % 2):256 * (o % 2) + 256],
                      ACT.Sigmoid).then_inc(glu_sig, 1)
                act.wait_ge(probs_T, 2 * l + 1)
                nc.scalar.copy(pT[:, 0, :, :].rearrange("p h n -> p (h n)"),
                               ps[:, 2:4, :].rearrange("p b n -> p (b n)")).then_inc(pT_act, 1)
                act.wait_ge(head_var, l + 1)
                A(head_rs[:], head_ss[:], ACT.Sqrt).then_inc(head_dev, 1)
                norm(2 * l + 1)
                modulate(2 * l + 1)
                if l == 0:
                    act.wait_ge(hT_dve, 8)
                    act.wait_ge(hT_act, 8)
                    link(nc.scalar.copy(hT_hi[:, 4:, :], hT[:, 4:, :]))
                    nc.scalar.copy(hT_hi[:, 0:4, :], hT[:, 0:4, :]).then_inc(hT_high, 1)

                    def silu(g):
                        act.wait_ge(e_free, SPLITS + 4 * (g + 1))
                        if g:
                            act.wait_ge(gu_out, g)
                        A(sil[:], ps[:, 2 + 2 * (g % 2), :], ACT.Silu).then_inc(gu_silu, 1)

                    act.wait_ge(e_free, SPLITS)
                    for g in range(GG):
                        for i in range(4):
                            u = 4 * g + i
                            src = chunk(act, at_gu[g] + i // 2)
                            if u >= SPLITS:
                                act.wait_ge(e_free, u + 1)
                            nc.scalar.copy(w_hi[i][:], src[:, 4 * (i % 2):4 * (i % 2) + 4, :]).then_inc(e_high, 1)
                        if g:
                            silu(g - 1)
                    silu(GG - 1)

            act.wait_ge(diff, 1)
            A(g2[:], g2[:], ACT.Exp).then_inc(diff_e, 1)
            act.wait_ge(routed, 1)
            more = act.value_load(over[0:1, 0:1], min_val=0, max_val=1)

            def gathered_high(job):
                act.wait_ge(hg_mod, job + 1)
                nc.scalar.copy(hg_hi[:], hg[:]).then_inc(hg_high, 1)

            def products_out(job):
                act.wait_ge(e_free, U0 + UPJ * job + SPLITS)
                act.wait_ge(scattered, job)
                for h in range(2):
                    nc.scalar.copy(y_sb[:, 512 * h:512 * h + 512], ps[:, 6 + h, :]).then_inc(y_out, 1)

            gathered_high(0)

            def act_job(job):
                for k in range(PER_JOB):
                    n = base + k
                    act.wait_ge(loaded[n % SLOTS], loaded_by(job, k))
                    for u in (2 * k, 2 * k + 1):
                        act.wait_ge(e_free, U0 + UPJ * job + u + 1)
                        nc.scalar.copy(w_hi[u % SPLITS][:],
                                       ring[:, n % SLOTS, UNIT * (u % 2):UNIT * (u % 2) + UNIT]).then_inc(e_high, 1)
                    if k == 1:
                        products_out(job)
                    if k == 6:
                        act.wait_ge(sel_turned, job + 1)
                        nc.scalar.copy(selT[:].rearrange("p t n -> p (t n)"), ps[:, 4, 0:T]).then_inc(selT_ready, 1)
                    g = (k - 5) // 4
                    if (k - 5) % 4 == 0 and 0 <= g < FG:
                        act.wait_ge(e_free, U0 + UPJ * job + SPLITS + 2 * (4 * g + 4))
                        act.wait_ge(e_prod, FG * job + g)
                        A(e_sil[:], ps[:, g % 2, :], ACT.Silu).then_inc(e_silu, 1)
                    g = (k - 10) // 4
                    if (k - 10) % 4 == 0 and 0 <= g < FG:
                        act.wait_ge(e_turned, FG * job + g + 1)
                        nc.scalar.copy(eT_hi[:, 4 * g:4 * g + 4, :].rearrange("p f n -> p (f n)"),
                                       ps[:, 4 + g % 2, :]).then_inc(eT_high, 1)
                    if k == 38:
                        gathered_high(job + 1)

            with act.Fori(0, E) as job:
                act_job(job)
            with act.If(more > 0):
                with act.Fori(E, JOBS) as job:
                    act_job(job)
                products_out(JOBS)
            with act.Else():
                products_out(E)
            norm(4)


        @block.vector
        def _(dve):
            link = chain(dve, dve_step)
            V = nc.vector
            TTo, TS, STT = V.tensor_tensor, V.tensor_scalar, V.scalar_tensor_tensor

            def norm(n):
                dve.wait_ge(squares, 2 * (n + 1))
                TS(rstd[:], sq_sum[:], 1.0 / D, EPS, ALU.mult, ALU.add).then_inc(variance, 1)
                dve.wait_ge(deviation, n + 1)
                link(V.reciprocal(rstd[:], rstd[:]))
                if n < 4:
                    link(TS(xn[:, 0, :], xs[:, 0, :], rstd[:, 0:1], None, ALU.mult))
                    TS(xn[:, 1, :], xs[:, 1, :], rstd[:, 1:2], None, ALU.mult).then_inc(normed, 1)
                else:
                    dve.wait_ge(fg_in, 16)
                    link(STT(xn[:, 0, :], xs[:, 0, :], rstd[:, 0:1], gate_m[:], ALU.mult, ALU.mult))
                    STT(xn[:, 1, :], xs[:, 1, :], rstd[:, 1:2], gate_m[:], ALU.mult, ALU.mult).then_inc(normed, 1)

            def take(l, cg):
                m = MODS.index((l, cg))
                dve.wait_ge(mod_psum, m + 1)
                bank = ps[:, mod_bank(m), :]
                if cg // 2 in (G_M, G_F):
                    dve.wait_ge(gbias_in, 32 if l == 0 else 64)
                    dst = (gate_m if cg // 2 == G_M else (gate_f, gate_f1)[l])[:, 512 * (cg % 2):512 * (cg % 2) + 512]
                    ins = TTo(dst, dst, bank, ALU.add)
                else:
                    if m:
                        dve.wait_ge(mod_taken, m)
                    for i in range(4):
                        ins = V.tensor_tensor_reduce(mod_diag[:, i, :], bank[:, P * i:P * i + P], ident, 1.0, 0.0,
                                                     ALU.mult, ALU.add, mod_raw[:, 4 * cg + i:4 * cg + i + 1])
                ins.then_inc(mod_taken, 1)

            def sum_mod(l, cg, ks):
                d = ON_DVE.index((l, cg))
                part = mod_acc[:, d % 2, :]
                for k in ks:
                    w = chunk(dve, at_mod[l, cg] + k // 4)[:, k % 4, :]
                    if k == 0:
                        if d >= 2:
                            dve.wait_ge(mod_psum, MODS.index(ON_DVE[d - 2]) + 1)
                        link(TS(part, w, c_act[:, 0:1], None, ALU.mult))
                    elif k < KC - 1:
                        link(STT(part, w, c_act[:, k:k + 1], part, ALU.mult, ALU.add))
                    else:
                        STT(part, w, c_act[:, k:k + 1], part, ALU.mult, ALU.add).then_inc(mod_summed, 1)

            def finish_mod(l, which):
                dve.wait_ge(mod_taken, 12 * l + (4 if which == 0 else 10))
                b = par(l, "b_ada").rearrange("p (m k) -> p m k", k=KC)
                raw = mod_raw[:].rearrange("p (m k) -> p m k", k=KC)
                shift, scale = (SH_M, SC_M) if which == 0 else (SH_F, SC_F)
                link(TTo(mod_s[:, which, :], raw[:, shift, :], b[:, shift, :], ALU.add))
                link(STT(mod_a[:, which, :], raw[:, scale, :], 1.0, b[:, scale, :], ALU.add, ALU.add))
                TTo(mod_a[:, which, :], mod_a[:, which, :], par(l, ("g_mix", "g_ffn")[which]),
                    ALU.mult).then_inc((mod_mix, mod_ffn)[which], 1)
                dve.wait_ge((mod_mix, mod_ffn)[which], l + 1)

            def modulate(n):
                which = n % 2
                dve.wait_ge(turned, 4 * n + 2)
                for kc in range(4):
                    TS(hT[:, kc, :], ps[:, 2 + kc // 2, 256 * (kc % 2):256 * (kc % 2) + 256],
                       mod_a[:, which, kc:kc + 1], mod_s[:, which, kc:kc + 1], ALU.mult, ALU.add).then_inc(hT_dve, 1)

            def state_scalars():
                a, b = PRM["lam_re"]
                lre = prms[:, :, a:b]
                a, b = PRM["lam_im"]
                lim = prms[:, :, a:b]
                t1, t2, t3 = sv["t1"][:], sv["t2"][:], sv["t3"][:]
                dve.wait_ge(sv_step, 1)
                TTo(sv["dec"][:], lre, sv["step"][:], ALU.mult)
                link(TTo(t1, lim, sv["step"][:], ALU.mult))
                for m in range(8):
                    ins = TS(pw_c[:, m], t1, float(1 << m), None, ALU.mult)
                link(ins)
                link(TS(pw_s[:], pw_c[:], 1.0 / (2 * math.pi), ROUND, ALU.mult, ALU.add))
                link(TS(pw_s[:], pw_s[:], -ROUND, None, ALU.add))
                for part in (TWO_PI_HI, TWO_PI_MID, TWO_PI_LO):
                    link(STT(pw_c[:], pw_s[:], -part, pw_c[:], ALU.mult, ALU.add))
                TS(pw_c[:], pw_c[:], 3.1415925, -3.1415925, ALU.min, ALU.max).then_inc(sv_angle, 1)
                dve.wait_ge(sv_trig, 1)
                link(TTo(pw_c[:], pw_c[:], pw_c[:], ALU.mult))
                link(TS(pw_c[:], pw_c[:], -2.0, 1.0, ALU.mult, ALU.add))
                dec, cr, ci = sv["dec"][:], sv["cr"][:], sv["ci"][:]
                TTo(t1, dec, pw_c[:, 0], ALU.mult)
                link(TTo(t2, dec, pw_s[:, 0], ALU.mult))
                link(TS(t1, t1, -1.0, None, ALU.add))
                TTo(cr, t1, lre, ALU.mult)
                link(TTo(t3, t2, lim, ALU.mult))
                link(TTo(cr, cr, t3, ALU.add))
                TTo(ci, t2, lre, ALU.mult)
                link(TTo(t3, t1, lim, ALU.mult))
                link(TTo(ci, ci, t3, ALU.subtract))
                TTo(t1, lre, lre, ALU.mult)
                link(TTo(t2, lim, lim, ALU.mult))
                link(TTo(t1, t1, t2, ALU.add))
                link(V.reciprocal(t1, t1))
                TTo(cr, cr, t1, ALU.mult)
                link(TTo(ci, ci, t1, ALU.mult))
                link(TS(t1, cr, -1.0, None, ALU.mult))
                TS(t2, ci, -1.0, None, ALU.mult).then_inc(sv_ready, 1)

            dve.wait_ge(small_in, 48)
            dve.wait_ge(c_silu, 1)
            V.tensor_copy(c_wide[:], c_act[:].unsqueeze(2).to_broadcast([P, KC, P])).then_inc(c_spread, 1)
            norm(0)
            state_scalars()
            make_table(dve, V, 0, link, table0)

            for l in range(DEPTH):
                if l:
                    norm(2)
                else:
                    for cg in range(4):
                        take(0, cg)
                    finish_mod(0, 0)
                modulate(2 * l)
                if l:
                    dve.wait_ge(table1, 1)

                def skip(u):
                    dve.wait_ge(y_psum, 8 * l + 2 * u + 2)
                    d0 = PRM["d_skip"][0] + u
                    STT(yT[:, u, :], uT[:, u, :], prms[:, l, d0:d0 + 1], ps[:, 6, 0:T],
                        ALU.mult, ALU.add).then_inc(y_skip, 1)

                for j in range(8):
                    b = 2 + 2 * (j % 2)
                    re, im = (ps[:, b + m, :].rearrange("p (q n) -> p q n", q=2) for m in (0, 1))
                    cs, sn = cos_t[:, 2 * j:2 * j + 2, :], sin_t[:, 2 * j:2 * j + 2, :]
                    zr, zi = z_re[j % 2], z_im[j % 2]
                    dve.wait_ge(bu_psum, 8 * l + j + 1)
                    if 8 * l + j >= 2:
                        dve.wait_ge(rotated, 8 * l + j - 1)
                    TTo(zr, re, cs, ALU.mult)
                    link(TTo(rot_a[:], im, sn, ALU.mult))
                    link(TTo(zr, zr, rot_a[:], ALU.add))
                    TTo(zi, im, cs, ALU.mult)
                    TTo(rot_b[:], re, sn, ALU.mult).then_inc(bu_used, 1)
                    dve.wait_ge(bu_used, 8 * l + j + 1)
                    link(TTo(zi, zi, rot_b[:], ALU.subtract))
                    for q in range(2):
                        decay = sv["dec"][:, l, 2 * j + q:2 * j + q + 1].to_broadcast([P, T])
                        for v in (zr, zi):
                            ins = V.tensor_tensor_scan(v[:, q, :], decay, v[:, q, :], 0.0, ALU.mult, ALU.add)
                    ins.then_inc(scanned, 1)
                    if l == 0 and j in (1, 3, 5):
                        sum_mod(0, 4 + j, range(KC))
                    if l == 0:
                        for cg in {1: (4,), 3: (5, 6), 5: (7, 8), 7: (9,)}.get(j, ()):
                            take(0, cg)
                    if j in (3, 5, 7):
                        skip((j - 3) // 2)
                skip(3)
                if l == 0:
                    finish_mod(0, 1)

                dve.wait_ge(scores, 2 * (l + 1))
                dve.wait_ge(rotated, 8 * (l + 1))
                banks = lambda p0, p1, b: ps[p0:p1, b:b + 2, :].rearrange("p b (h n) -> p (b h) n", n=P)
                V.tensor_copy(sc[HD:P, 0], banks(HD, P, 2))
                V.tensor_copy(sc[0:HD, 0, :, 0:CH], banks(0, HD, 2)[:, :, 0:CH])
                V.memset(sc[0:HD, 0, :, CH:P], NEG)
                link(V.tensor_copy(sc[:, 1], banks(0, P, 4)))
                link(V.tensor_reduce(s_max[:], sc, AX, ALU.max))
                sinks = par(l, "sinks").unsqueeze(1).to_broadcast([P, TT, HEADS])
                link(TTo(s_max[:], s_max[:], sinks, ALU.max))
                link(TTo(sinks_e[:], sinks, s_max[:], ALU.subtract))
                TTo(sc, sc, s_max[:].unsqueeze(3).to_broadcast([P, TT, HEADS, P]), ALU.subtract).then_inc(shifted, 1)
                dve.wait_ge(exps, 2 * (l + 1))
                link(V.tensor_reduce(s_den[:], sc, AX, ALU.add))
                link(TTo(s_den[:], s_den[:], sinks_e[:], ALU.add))
                link(V.reciprocal(s_den[:], s_den[:]))
                TTo(sc, sc, s_den[:].unsqueeze(3).to_broadcast([P, TT, HEADS, P]), ALU.mult).then_inc(probs, 1)

                dve.wait_ge(glu_sig, 4 * (l + 1))
                link(TTo(yT[:, 0:UT, :], yT[:, 0:UT, :], sig[:], ALU.mult))
                TTo(sig[:], yT[:, 0:UT, :], yT[:, 0:UT, :], ALU.mult).then_inc(ssm_sq, 1)
                dve.wait_ge(ssm_sq, 2 * l + 1)
                for u in range(UT):
                    g0 = PRM["g_ssm"][0] + u
                    ins = TS(yT[:, u, :], yT[:, u, :], prms[:, l, g0:g0 + 1], None, ALU.mult)
                ins.then_inc(ssm_sq, 1)

                dve.wait_ge(probs_T, 2 * (l + 1))
                V.tensor_copy(pT[:, 1, :, :].rearrange("p h n -> p (h n)"),
                              ps[:, 4:6, :].rearrange("p b n -> p (b n)")).then_inc(pT_dve, 1)
                dve.wait_ge(pv_psum, l + 1)
                for b in range(2):
                    src = ps[:, 6 + b, :].rearrange("p (c j n) -> p j c n", c=2, j=HPK)
                    dst = yT[:, UT:2 * UT, P * b:P * b + P].rearrange("p j (c n) -> p j c n", c=2)
                    ins = V.tensor_copy(dst, src)
                link(ins)
                dve.wait_ge(ss_psum, 2 * l + 1)
                TTo(sig[:], yT[:, UT:2 * UT, :], yT[:, UT:2 * UT, :], ALU.mult).then_inc(attn_sq, 1)
                dve.wait_ge(attn_sq, 2 * l + 1)
                for u in range(UT):
                    g0 = PRM["g_attn"][0] + u
                    ins = TS(yT[:, UT + u, :], yT[:, UT + u, :], prms[:, l, g0:g0 + 1], None, ALU.mult)
                ins.then_inc(attn_sq, 1)
                dve.wait_ge(ss_psum, 2 * (l + 1))
                TS(head_ss[:, 0:2], ps[:, 2, 0:2], 1.0 / D_SSM, EPS, ALU.mult, ALU.add)
                TS(head_ss[:, 2:4], ps[:, 3, 0:2], 1.0 / D_SSM, EPS, ALU.mult, ALU.add).then_inc(head_var, 1)
                dve.wait_ge(head_dev, l + 1)
                V.reciprocal(head_rs[:], head_rs[:]).then_inc(head_ready, 1)
                dve.wait_ge(head_ready, l + 1)
                for n in range(2):
                    dve.wait_ge(out_psum, 4 * l + 2 * n + 2)
                    for t in range(TT):
                        s_bank, a_bank = (2 + t, 4 + t) if n == 0 else (6 + t, t)
                        part = slice(512 * n, 512 * n + 512)
                        link(TS(resid[:, t, :], ps[:, s_bank, :], head_rs[:, t:t + 1], None, ALU.mult))
                        link(STT(resid[:, t, :], ps[:, a_bank, :], head_rs[:, 2 + t:3 + t], resid[:, t, :],
                                 ALU.mult, ALU.add))
                        link(TTo(resid[:, t, :], resid[:, t, :], gate_m[:, part], ALU.mult))
                        ins = TTo(xs[:, t, part], xs[:, t, part], resid[:, t, :], ALU.add)
                        if n == 0 or t == 0:
                            link(ins)
                ins.then_inc(x_updated, 1)

                norm(2 * l + 1)
                modulate(2 * l + 1)
                if l == 0:
                    dve.wait_ge(hT_high, 1)
                    TTo(hT_lo[:], hT[:], hT_hi[:].bitcast(F32), ALU.subtract).then_inc(hT_split, 1)

                    def product(g):
                        dve.wait_ge(gu_silu, g + 1)
                        TTo(a_T[:, 2 * g:2 * g + 2, :].rearrange("p f n -> p (f n)"), sil[:],
                            ps[:, 3 + 2 * (g % 2), :], ALU.mult).then_inc(gu_out, 1)

                    for g in range(GG):
                        for i in range(4):
                            dve.wait_ge(e_high, 4 * g + i + 1)
                            part = ring[:, (at_gu[g] + i // 2) % SLOTS, UNIT * (i % 2):UNIT * (i % 2) + UNIT]
                            TTo(w_lo[i][:], part, w_hi[i][:].bitcast(F32), ALU.subtract).then_inc(e_low, 1)
                            if g:
                                sum_mod(*FFN_MODS[g - 1], (2 * i, 2 * i + 1))
                            if i == 2 and g >= 2:
                                take(*FFN_MODS[g - 2])
                        if g:
                            product(g - 1)
                    sum_mod(*FFN_MODS[GG - 1], range(KC))
                    product(GG - 1)
                    take(*FFN_MODS[GG - 2])
                    for i in range(3):
                        sum_mod(*FFN_MODS[GG + i], range(KC))
                        take(*FFN_MODS[GG + i - 1])
                    take(*FFN_MODS[GG + 2])
                    finish_mod(1, 0)
                    finish_mod(1, 1)
                    dve.wait_ge(down_psum, GG)
                    for t in range(TT):
                        for n in range(2):
                            bank = (6, 7, 0, 1)[2 * t + n]
                            part = slice(512 * n, 512 * n + 512)
                            link(TTo(resid[:, n, :], ps[:, bank, :], gate_f[:, part], ALU.mult))
                            ins = TTo(xs[:, t, part], xs[:, t, part], resid[:, n, :], ALU.add)
                            if t == 0 or n == 0:
                                link(ins)
                    ins.then_inc(x_updated, 1)

            dve.wait_ge(logits, 1)
            link(V.tensor_copy(lg[:].rearrange("p t e -> p (t e)"), ps[:, 6, 0:TT * E]))
            for t in range(TT):
                link(V.max(top[:, t, :], lg[:, t, :]))
                link(V.max_index(idx[:, t, :], top[:, t, :], lg[:, t, :]))
            link(V.tensor_copy(idx_f[:], idx[:]))
            TTo(g2[:], top[:, :, 1], top[:, :, 0], ALU.subtract).then_inc(diff, 1)
            iota = const("iota")
            for t in range(TT):
                TS(oh1[:, t, :], iota[:, 0:E], idx_f[:, t, 0:1], None, ALU.is_equal)
                link(TS(oh2[:, t, :], iota[:, 0:E], idx_f[:, t, 1:2], None, ALU.is_equal))
            link(V.memset(gate_of[:, :, 0:1], 0.0))
            TTo(chosen[:, :, 0:E], oh1[:], oh2[:], ALU.add)
            TTo(chosen[:, :, E:2 * E], oh1[:], oh2[:], ALU.add)
            TTo(chosen[:, :, 2 * E:], oh1[:, :, 0:1], oh2[:, :, 0:1], ALU.add).then_inc(picked, 1)
            dve.wait_ge(diff_e, 1)
            link(TS(g1[:], g2[:], 1.0, None, ALU.add))
            link(V.reciprocal(g1[:], g1[:]))
            link(TTo(g2[:], g2[:], g1[:], ALU.mult))
            for t in range(TT):
                link(TS(oh1[:, t, :], oh1[:, t, :], g1[:, t:t + 1], None, ALU.mult))
                link(STT(gate_of[:, t, 1:E + 1], oh2[:, t, :], g2[:, t:t + 1], oh1[:, t, :], ALU.mult, ALU.add))
            link(V.tensor_copy(gate_of[:, :, E + 1:], gate_of[:, :, 1:E + 1]))
            dve.wait_ge(rank_psum, 1)
            r = ps[:, 7, 0:TT * E].rearrange("p (t e) -> p t e", t=TT)
            V.tensor_copy(rank[:, :, 0:E], r)
            TS(rank[:, :, E:2 * E], r, -float(CAP), None, ALU.add)
            V.tensor_copy(rank[:, :, 2 * E:], r[:, :, 0:1])
            link(V.tensor_reduce(over_f[:], ps[:, 7, 16:16 + E], AX, ALU.max))
            link(V.memset(acc[:], 0.0))
            link(V.memset(selT[:], 0.0))
            link(V.memset(ps[:, 6:8, :], 0.0))
            TS(over[:], over_f[:], float(CAP), None, ALU.is_gt).then_inc(routed, 1)
            dve.wait_ge(routed, 1)
            more = dve.value_load(over[0:1, 0:1], min_val=0, max_val=1)

            def choose(job):
                for t in range(TT):
                    TS(sel[:, t, :], iota, rank[:, t, bass.ds(job, 1)], chosen[:, t, bass.ds(job, 1)],
                       ALU.is_equal, ALU.mult).then_inc(sel_made, 1)

            def gathered_mod(job):
                dve.wait_ge(gathered, job + 1)
                for kc in range(KC):
                    TS(hg[:, kc, :], ps[:, 2 * (kc // 4), P * (kc % 4):P * (kc % 4) + P],
                       mod_a[:, 1, kc:kc + 1], mod_s[:, 1, kc:kc + 1], ALU.mult, ALU.add).then_inc(
                           hg_mod if kc == KC - 1 else dve_job, 1)

            def gathered_low(job):
                dve.wait_ge(hg_high, job + 1)
                TTo(hg_lo[:], hg[:], hg_hi[:].bitcast(F32), ALU.subtract).then_inc(hg_ready, 1)

            def add_products(job):
                dve.wait_ge(scattered, job + 1)
                dve.wait_ge(added, 4 * job)
                for t in range(TT):
                    for h in range(2):
                        part = slice(512 * h, 512 * h + 512)
                        STT(acc[:, t, part], ps[:, (4, 5, 1, 3)[2 * t + h], :], gate_of[:, t, bass.ds(job, 1)],
                            acc[:, t, part], ALU.mult, ALU.add).then_inc(added, 1)

            choose(0)
            gathered_mod(0)
            gathered_low(0)

            def dve_one(job):
                for k in range(PER_JOB):
                    n = base + k
                    for u in (2 * k, 2 * k + 1):
                        dve.wait_ge(e_high, U0 + UPJ * job + u + 1)
                        TTo(w_lo[u % SPLITS][:], ring[:, n % SLOTS, UNIT * (u % 2):UNIT * (u % 2) + UNIT],
                            w_hi[u % SPLITS][:].bitcast(F32), ALU.subtract).then_inc(e_low, 1)
                    if k == 3:
                        add_products(job)
                    g = (k - 5) // 4
                    if (k - 5) % 4 == 0 and 0 <= g < FG:
                        dve.wait_ge(e_silu, FG * job + g + 1)
                        TTo(e_act[:, 512 * g:512 * g + 512], e_sil[:], ps[:, 2 + g % 2, :], ALU.mult).then_inc(e_prod, 1)
                    g = (k - 10) // 4
                    if (k - 10) % 4 == 0 and 0 <= g < FG:
                        dve.wait_ge(eT_high, FG * job + g + 1)
                        hi = eT_hi[:, 4 * g:4 * g + 4, :].rearrange("p f n -> p (f n)").bitcast(F32)
                        TTo(eT_lo[:, 4 * g:4 * g + 4, :].rearrange("p f n -> p (f n)"), ps[:, 4 + g % 2, :], hi,
                            ALU.subtract).then_inc(eT_ready, 1)
                    if k == 31:
                        dve.wait_ge(sel_turned, job + 1)
                        choose(job + 1)
                    if k == 37:
                        gathered_mod(job + 1)
                    if k == 39:
                        gathered_low(job + 1)

            with dve.Fori(0, E) as job:
                dve_one(job)
            with dve.If(more > 0):
                with dve.Fori(E, JOBS) as job:
                    dve_one(job)
                add_products(JOBS)
                dve.wait_ge(added, 4 * (JOBS + 1))
            with dve.Else():
                add_products(E)
                dve.wait_ge(added, 4 * (E + 1))
            for t in range(TT):
                link(TTo(acc[:, t, :], acc[:, t, :], gate_f1[:], ALU.mult))
                ins = TTo(xs[:, t, :], xs[:, t, :], acc[:, t, :], ALU.add)
                if t == 0:
                    link(ins)
            ins.then_inc(x_updated, 1)
            norm(4)

        @block.tensor
        def _(pe):
            M = nc.tensor.matmul

            def mod_wide(l, cg):
                m = MODS.index((l, cg))
                if m >= 2:
                    pe.wait_ge(mod_taken, m - 1)
                for half in range(2):
                    w = chunk(pe, at_mod[l, cg] + half)
                    for k in range(4):
                        ins = M(ps[:, mod_bank(m), :], c_wide[:, 4 * half + k, :], w[:, k, :],
                                start=(half == 0 and k == 0), stop=(half == 1 and k == 3))
                ins.then_inc(mod_psum, 1)

            def mod_ones(l, cg):
                m, d = MODS.index((l, cg)), ON_DVE.index((l, cg))
                pe.wait_ge(mod_taken, m - 1)
                pe.wait_ge(mod_summed, d + 1)
                M(ps[:, mod_bank(m), :], ones, mod_acc[:, d % 2, :], start=True, stop=True).then_inc(mod_psum, 1)

            def turn(n):
                pe.wait_ge(normed, n + 1)
                for kc in range(KC):
                    for t in range(TT):
                        c0 = 256 * (kc % 2) + P * t
                        ins = nc.tensor.transpose(ps[:, 2 + kc // 2, c0:c0 + P], xn[:, t, P * kc:P * kc + P], ident)
                    if kc % 2:
                        ins.then_inc(turned, 1)

            pe.wait_ge(small_in, 48)
            pe.wait_ge(c_spread, 1)
            for cg in range(4):
                mod_wide(0, cg)

            for l in range(DEPTH):
                if l:
                    pe.wait_ge(x_updated, 2)
                turn(2 * l)
                pe.wait_ge(hT_dve, 8 * l + 4)
                pe.wait_ge(hT_act, 8 * l + 4)

                def project(m, w, c0, bank):
                    for kc in range(KC):
                        ins = M(ps[:, bank, 0:T], w[:, kc, c0:c0 + P], hT[:, kc, :], start=(kc == 0), stop=(kc == KC - 1))
                    ins.then_inc(projected, 1)

                for u in range(UT):
                    project(u, chunk(pe, at_in[l, u // 2]), P * (u % 2), 2 + u)

                def drive(j):
                    pe.wait_ge(proj_out, 12 * l + 4)
                    pe.wait_ge(matrices, l + 1)
                    if j >= 2:
                        pe.wait_ge(bu_used, 8 * l + j - 1)
                    for m, mat in ((0, b_re), (1, b_im)):
                        for q in range(2):
                            ins = M(ps[:, 2 + 2 * (j % 2) + m, T * q:T * q + T], mat[:, 2 * j + q, :], uT[:, j // 2, :],
                                    start=True, stop=True)
                    ins.then_inc(bu_psum, 1)

                def read_out(j):
                    pe.wait_ge(rotated, 8 * l + j + 1)
                    if j % 2 == 0 and j:
                        pe.wait_ge(y_skip, 4 * l + j // 2)
                    for q in range(2):
                        for mat, st in ((c_re, st_re), (c_im, st_im)):
                            first = j % 2 == 0 and q == 0 and mat is c_re
                            ins = M(ps[:, 6, 0:T], mat[:, 2 * j + q, :], st[:, q, :], start=first,
                                    stop=(j % 2 == 1 and q == 1 and mat is c_im))
                    ins.then_inc(y_psum, 1)

                drive(0)
                drive(1)
                for j in range(8):
                    if j:
                        pe.wait_ge(proj_out, 12 * l + 4 + j)
                    if j < 5:
                        project(j, chunk(pe, at_in[l, 2 + j // 2]), P * (j % 2), 7)
                    else:
                        w = chunk(pe, at_in[l, 4])
                        for kc in range(KC):
                            ins = M(ps[:, 7, 0:P], hT[:, kc, CH * (j - 5):CH * (j - 5) + P], w[:, kc, P:2 * P],
                                    start=(kc == 0), stop=(kc == KC - 1))
                        ins.then_inc(projected, 1)
                    if l == 0 and j in (2, 4, 6):
                        mod_ones(0, 3 + j)
                    if l == 0 and j in (0, 2, 4):
                        mod_wide(0, 4 + j)
                    read_out(j)
                    if j + 2 < 8:
                        drive(j + 2)

                pe.wait_ge(proj_out, 12 * (l + 1))
                pe.wait_ge(bu_used, 8 * (l + 1))
                for t in range(TT):
                    for h in range(KVH):
                        for j in range(HPK):
                            for c in (2 * t, 2 * t + 1):
                                k0 = CH * max(c - 1, 0)
                                kn = CH if c == 0 else P
                                p0 = CH * (c % 2)
                                ins = M(ps[p0:p0 + CH, 2 + 2 * t + h, P * j:P * j + kn], qT[:, j, CH * c:CH * c + CH],
                                        kz[:, h, k0:k0 + kn], start=True, stop=True)
                    ins.then_inc(scores, 1)

                pe.wait_ge(y_gelu, 4 * (l + 1))
                pe.wait_ge(y_skip, 4 * (l + 1))
                w = chunk(pe, at_glu[l])
                for o in range(UT):
                    for k in range(UT):
                        ins = M(ps[:, 6 + o // 2, T * (o % 2):T * (o % 2) + T], w[:, k, P * o:P * o + P], yT[:, k, :],
                                start=(k == 0), stop=(k == UT - 1))
                    ins.then_inc(glu_psum, 1)

                pe.wait_ge(probs, l + 1)
                for t in range(TT):
                    for h in range(HEADS):
                        ins = nc.tensor.transpose(ps[:, 2 + 2 * t + h // 4, P * (h % 4):P * (h % 4) + P],
                                                  sc[:, t, h, :], ident)
                    ins.then_inc(probs_T, 1)
                pe.wait_ge(glu_sig, 4 * (l + 1))
                pe.wait_ge(pT_act, l + 1)
                pe.wait_ge(pT_dve, l + 1)
                for c in range(NCH):
                    window = (0, 0, 1, 2)[c]
                    for h in range(KVH):
                        o = ps[HD * h:HD * h + HD, 6 + c // 2, T * (c % 2):T * (c % 2) + T]
                        ins = M(o.rearrange("p (j n) -> p j n", j=HPK), vt[:, window, HD * h:HD * h + HD],
                                pT[:, c // 2, HPK * h:HPK * h + HPK, CH * (c % 2):CH * (c % 2) + CH],
                                start=True, stop=True)
                ins.then_inc(pv_psum, 1)

                for which, done in ((0, ssm_sq), (1, attn_sq)):
                    pe.wait_ge(done, 2 * l + 1)
                    for t in range(TT):
                        for k in range(UT):
                            ins = M(ps[:, 2 + which, t:t + 1], sig[:, k, P * t:P * t + P], ones[:, 0:1],
                                    start=(k == 0), stop=(k == UT - 1))
                    ins.then_inc(ss_psum, 1)
                pe.wait_ge(head_ready, l + 1)
                pe.wait_ge(ssm_sq, 2 * (l + 1))
                pe.wait_ge(attn_sq, 2 * (l + 1))
                pe.wait_ge(mod_ffn, l + 1)
                for n in range(4):
                    w = chunk(pe, at_out[l, n])
                    for t in range(TT):
                        bank = ((2, 4), (6, 0))[n // 2][n % 2] + t
                        for k in range(4):
                            ins = M(ps[:, bank, :], yT[:, 4 * (n % 2) + k, P * t:P * t + P], w[:, k, :],
                                    start=(k == 0), stop=(k == 3))
                    ins.then_inc(out_psum, 1)

                turn(2 * l + 1)
                pe.wait_ge(hT_dve, 8 * l + 8)
                pe.wait_ge(hT_act, 8 * l + 8)
                if l == 0:
                    pe.wait_ge(hT_split, 1)
                    pe.sem_inc(e_free, SPLITS)
                    for g in range(GG):
                        if g >= 2:
                            pe.wait_ge(gu_out, g - 1)
                        for i in range(4):
                            pe.wait_ge(e_low, 4 * g + i + 1)
                            hi, lo = (v[i][:].rearrange("p (k n) -> p k n", k=4) for v in (w_hi, w_lo))
                            for kk in range(4):
                                kc = 4 * (i % 2) + kk
                                for f in range(2):
                                    o = ps[:, 2 + 2 * (g % 2) + i // 2, T * f:T * f + T]
                                    part = slice(P * f, P * f + P)
                                    M(o, hi[:, kk, part], hT_hi[:, kc, :], start=(kc == 0 and f == 0), stop=False,
                                      skip_group_check=True)
                                    M(o, hi[:, kk, part], hT_lo[:, kc, :], start=False, stop=False,
                                      skip_group_check=True)
                                    ins = M(o, lo[:, kk, part], hT_hi[:, kc, :], start=False, stop=(kc == KC - 1),
                                            skip_group_check=True)
                            ins.then_inc(e_free, 1)
                        if g:
                            mod_ones(*FFN_MODS[g - 1])
                    pe.wait_ge(gu_out, GG)
                    pe.wait_ge(mod_taken, 10 + GG - 1)
                    for n in range(FT // 2):
                        w = chunk(pe, at_down[n])
                        for t in range(TT):
                            for h in range(2):
                                for k in range(2):
                                    f = 2 * n + k
                                    ins = M(ps[:, (6, 7, 0, 1)[2 * t + h], :], a_T[:, f, P * t:P * t + P],
                                            w[:, k, 512 * h:512 * h + 512], start=(f == 0), stop=(f == FT - 1))
                        ins.then_inc(down_psum, 1)
                        if n in (1, 4, 7, 10):
                            mod_ones(*FFN_MODS[GG - 1 + n // 3])

            for t in range(TT):
                for kc in range(KC):
                    ins = M(ps[:, 6, E * t:E * t + E], hT[:, kc, P * t:P * t + P], w_router[:, kc, :],
                            start=(kc == 0), stop=(kc == KC - 1))
            ins.then_inc(logits, 1)
            pe.wait_ge(picked, 1)
            M(ps[:, 7, 0:E], const("before"), chosen[:, 0, 0:E], start=True, stop=True)
            M(ps[:, 7, E:2 * E], const("before"), chosen[:, 1, 0:E], start=True, stop=False)
            M(ps[:, 7, E:2 * E], ones, chosen[:, 0, 0:E], start=False, stop=True)
            M(ps[:, 7, 2 * E:3 * E], ones, chosen[:, 0, 0:E], start=True, stop=False)
            M(ps[:, 7, 2 * E:3 * E], ones, chosen[:, 1, 0:E], start=False, stop=True).then_inc(rank_psum, 1)
            pe.wait_ge(routed, 1)
            more = pe.value_load(over[0:1, 0:1], min_val=0, max_val=1)

            def gather(job):
                pe.wait_ge(sel_made, TT * (job + 1))
                for kc in range(KC):
                    for t in range(TT):
                        ins = M(ps[:, 2 * (kc // 4), P * (kc % 4):P * (kc % 4) + P], xn[:, t, P * kc:P * kc + P],
                                sel[:, t, :], start=(t == 0), stop=(t == TT - 1))
                ins.then_inc(gathered, 1)

            def scatter(job):
                pe.wait_ge(y_out, 2 * (job + 1))
                for t in range(TT):
                    for h in range(2):
                        ins = M(ps[:, (4, 5, 1, 3)[2 * t + h], :], selT[:, t, :], y_sb[:, 512 * h:512 * h + 512],
                                start=True, stop=True)
                ins.then_inc(scattered, 1)

            gather(0)

            def pe_one(job):
                pe.wait_ge(hg_ready, job + 1)
                for k in range(PER_JOB):
                    if k < 4 * FG:
                        g, which, half = k // 4, k // 2 % 2, k % 2
                        bank = ps[:, 2 * which + g % 2, :]
                        if half == 0 and which == 0 and g == 1:
                            pe.wait_ge(added, 4 * (job + 1))
                        if half == 0 and which == 0 and g >= 2:
                            pe.wait_ge(e_prod, FG * job + g - 1)
                        for i in range(2):
                            u = 2 * k + i
                            hi, lo = w_hi[u % SPLITS], w_lo[u % SPLITS]
                            pe.wait_ge(e_low, U0 + UPJ * job + u + 1)
                            for kc in range(2):
                                kk = 4 * half + 2 * i + kc
                                part = slice(512 * kc, 512 * kc + 512)
                                M(bank, hg_hi[:, kk, :], hi[:, part], start=(kk == 0), stop=False)
                                M(bank, hg_lo[:, kk, :], hi[:, part], start=False, stop=False)
                                ins = M(bank, hg_hi[:, kk, :], lo[:, part], start=False, stop=(kk == KC - 1))
                            ins.then_inc(e_free, 1)
                    else:
                        for i in range(2):
                            u = 2 * k + i
                            hi, lo = w_hi[u % SPLITS], w_lo[u % SPLITS]
                            pe.wait_ge(e_low, U0 + UPJ * job + u + 1)
                            f = 2 * (k - 4 * FG) + i
                            if f % 4 == 0:
                                pe.wait_ge(eT_ready, FG * job + f // 4 + 1)
                            for h in range(2):
                                part = slice(512 * h, 512 * h + 512)
                                bank = ps[:, 6 + h, :]
                                M(bank, eT_hi[:, f, :], hi[:, part], start=(f == 0), stop=False)
                                M(bank, eT_lo[:, f, :], hi[:, part], start=False, stop=False)
                                ins = M(bank, eT_hi[:, f, :], lo[:, part], start=False, stop=(f == FE_T - 1))
                            ins.then_inc(e_free, 1)
                    if k == 1:
                        scatter(job)
                    if k == 3:
                        pe.wait_ge(sel_made, TT * (job + 1))
                        pe.wait_ge(added, 4 * job + 1)
                        for t in range(TT):
                            ins = nc.tensor.transpose(ps[:, 4, P * t:P * t + P], sel[:, t, :], ident)
                        ins.then_inc(sel_turned, 1)
                    for g in range(FG):
                        if k == (4 * g + 7 if g < FG - 1 else 30):
                            pe.wait_ge(e_prod, FG * job + g + 1)
                            if g >= 2:
                                pe.wait_ge(eT_ready, FG * job + g - 1)
                            if g == 0:
                                pe.wait_ge(selT_ready, job + 1)
                            for i in range(4):
                                f = 4 * g + i
                                ins = nc.tensor.transpose(ps[:, 4 + g % 2, P * i:P * i + P],
                                                          e_act[:, P * f:P * f + P], ident)
                            ins.then_inc(e_turned, 1)
                    if k == 34:
                        gather(job + 1)

            with pe.Fori(0, E) as job:
                pe_one(job)
            with pe.If(more > 0):
                with pe.Fori(E, JOBS) as job:
                    pe_one(job)
                scatter(JOBS)
            with pe.Else():
                scatter(E)


def kernel(x, c, norm_mix_g, norm_ffn_g, w_ada, b_ada, w_in, ssm_lam_re, ssm_lam_im,
           ssm_b_re, ssm_b_im, ssm_c_re, ssm_c_im, ssm_d, ssm_log_step, ssm_w_glu,
           attn_sinks, out_norm_ssm_g, out_norm_attn_g, w_out, ffn_w_gate, ffn_w_up,
           ffn_w_down, moe_w_router, moe_w_gate, moe_w_up, moe_w_down, final_norm_g):
    import numpy as np
    import concourse.bacc as bacc
    from concourse.bass_utils import run_bass_kernel_spmd

    f = lambda a: np.ascontiguousarray(np.asarray(a))
    cols = lambda v: np.asarray(v).reshape(-1, P).T
    order = np.arange(HEADS).reshape(KVH, HPK).T.reshape(-1)
    by_head = (order[:, None] * HD + np.arange(HD)[None, :]).reshape(-1)
    w_in, w_out = np.array(w_in), np.array(w_out)
    w_in[:, :, D_SSM:D_SSM + 512] = w_in[:, :, D_SSM + by_head]
    w_out[:, D_SSM:] = w_out[:, D_SSM + by_head]
    states = lambda v: np.asarray(v).reshape(PAIRS, P).T

    layer = lambda make: np.stack([make(l) for l in range(DEPTH)])
    prm = np.concatenate([
        layer(lambda l: cols(b_ada[l])), layer(lambda l: cols(norm_mix_g[l])), layer(lambda l: cols(norm_ffn_g[l])),
        layer(lambda l: states(ssm_lam_re[l])), layer(lambda l: states(ssm_lam_im[l])),
        layer(lambda l: states(np.repeat(np.asarray(ssm_log_step[l]), STATE))),
        layer(lambda l: cols(ssm_d[l])), layer(lambda l: cols(out_norm_ssm_g[l])),
        layer(lambda l: cols(np.asarray(out_norm_attn_g[l])[by_head])),
        layer(lambda l: np.broadcast_to(np.asarray(attn_sinks[l]), (P, HEADS))),
    ], axis=2).transpose(1, 0, 2)
    b_lay = lambda v: np.asarray(v).transpose(0, 2, 1).reshape(UT, P, STATE).transpose(1, 0, 2).reshape(P, -1)
    c_lay = lambda v: np.asarray(v).transpose(0, 2, 1).reshape(PAIRS, P, GROUP).transpose(1, 0, 2).reshape(P, -1)
    bc = np.stack([np.stack([b_lay(ssm_b_re[l]), b_lay(ssm_b_im[l]), c_lay(ssm_c_re[l]), c_lay(ssm_c_im[l])], 1)
                   for l in range(DEPTH)])
    small = np.concatenate([cols(c[0]), np.asarray(moe_w_router[0]).reshape(KC, P, E).transpose(1, 0, 2).reshape(P, -1)], 1)

    i = np.arange(P)
    cst = np.concatenate([
        np.eye(P), i[:, None] < i[None, :], np.ones((P, P)), np.broadcast_to(i, (P, P)),
        i[:, None] // GROUP == np.arange(GT)[None, :],
        (2 * np.arange(4)[None, :, None] + i[:, None, None] // STATE == np.arange(GT)).reshape(P, -1),
    ], axis=1).astype(np.float32)

    nc = bacc.Bacc("TRN2", target_bir_lowering=False, num_devices=1)
    arrays, args = {}, []
    for name, a in (("x", x), ("small", small), ("prm", prm), ("bc", bc), ("cst", cst), ("w_ada", w_ada),
                    ("b_ada", b_ada), ("w_in", w_in), ("w_glu", ssm_w_glu), ("w_out", w_out),
                    ("w_gate", ffn_w_gate), ("w_up", ffn_w_up), ("w_down", ffn_w_down), ("moe_gate", moe_w_gate),
                    ("moe_up", moe_w_up), ("moe_down", moe_w_down), ("final_g", final_norm_g)):
        arrays[name + "_dram"] = f(a)
        args.append(nc.dram_tensor(name + "_dram", arrays[name + "_dram"].shape, F32, kind="ExternalInput").ap())
    args.append(nc.dram_tensor("out_dram", (1, T, D), F32, kind="ExternalOutput").ap())
    build(nc, *args)
    r = run_bass_kernel_spmd(nc, [arrays], core_ids=[0])
    return r.results[0]["out_dram"]
```

```python
import math
from contextlib import ExitStack

import concourse.bass as bass
from concourse import mybir

F32 = mybir.dt.float32
F32R = mybir.dt.float32r
I32 = mybir.dt.int32
ALU = mybir.AluOpType
ACT = mybir.ActivationFunctionType
AX = mybir.AxisListType.X

P = 128
D = 1024
KC = D // P
T = 256
TT = T // P
DEPTH = 2
D_SSM, GROUP, STATE = 512, 16, 64
UT = D_SSM // P
PAIRS = (D_SSM // GROUP) * STATE // P
GT = P // GROUP
HD, HEADS, KVH = 64, 8, 2
HPK = HEADS // KVH
CH = 64
NCH = T // CH
D_FF = 2816
FT = D_FF // P
E, F_E = 8, 3584
FE_T = F_E // P
FG = F_E // 512
CAP = P
JOBS = E * (T // CAP)
EPS = 1e-6
NEG = -1e30
TWO_PI_HI = 6.28125
TWO_PI_MID = math.floor((2 * math.pi - TWO_PI_HI) * 2 ** 21) / 2 ** 21
TWO_PI_LO = 2 * math.pi - TWO_PI_HI - TWO_PI_MID
ROUND = 1.5 * 2.0 ** 23

SLOTS = 7
UNIT = 1024
SPLITS = 4
PER_JOB = 4 * FG + FE_T // 2
UPJ = 2 * PER_JOB

PRM = {}
_at = 0
for _name, _n in (("b_ada", 48), ("g_mix", 8), ("g_ffn", 8), ("lam_re", PAIRS), ("lam_im", PAIRS),
                  ("log_step", PAIRS), ("d_skip", UT), ("g_ssm", UT), ("g_attn", UT), ("sinks", HEADS)):
    PRM[_name] = (_at, _at + _n)
    _at += _n
N_PRM = _at
CST = {}
_at = 0
for _name, _n in (("ident", P), ("before", P), ("ones", P), ("iota", P), ("mask_ch", GT), ("mask_st", 4 * GT)):
    CST[_name] = (_at, _at + _n)
    _at += _n
N_CST = _at
SH_M, SC_M, G_M, SH_F, SC_F, G_F = range(6)


def build(nc, x, small, prm, bc, cst, w_ada, b_ada, w_in, w_glu, w_out, w_gate, w_up, w_down,
          moe_gate, moe_up, moe_down, final_g, out):
    with ExitStack() as ctx:
        sem = lambda name: ctx.enter_context(nc.semaphore(name))
        at = [(nc.sbuf_base + 63) // 64 * 64]

        def place(name, shape, dt=F32, offset=None):
            size = 4
            for n in shape[1:]:
                size *= n
            if offset is None:
                offset = at[0]
                at[0] += (size + 63) // 64 * 64
            return nc.alloc_sbuf_tensor_at(name, shape, dt, offset=offset)

        def region(nbytes):
            start = at[0]
            at[0] += nbytes
            return start

        ring = place("ring", [P, SLOTS, 2048])
        r_split = region(4 * 8192)
        r_tab = region(32768)
        r_blk = region(32768)
        xs = place("xs", [P, TT, D])
        xn = place("xn", [P, TT, D])
        r_hT = region(8192)
        hT = place("hT", [P, KC, T], offset=r_hT)
        gate_m = place("gate_m", [P, D])
        gate_f = place("gate_f", [P, D])
        k_st = place("k_st", [P, N_CST])
        prms = place("prms", [P, DEPTH, N_PRM])
        smalls = place("smalls", [P, KC + KC * E])
        c_act = place("c_act", [P, KC])
        r_wide = region(4096)
        c_wide = place("c_wide", [P, KC, P], offset=r_wide)
        gate_f1 = place("gate_f1", [P, D], offset=r_wide)
        mod_raw = place("mod_raw", [P, 6 * KC])
        mod_a = place("mod_a", [P, 2, KC])
        mod_s = place("mod_s", [P, 2, KC])
        sq_sum = place("sq_sum", [P, TT])
        rstd = place("rstd", [P, TT])
        head_ss = place("head_ss", [P, 4])
        head_rs = place("head_rs", [P, 4])
        sv = {n: place("sv_" + n, [P, DEPTH, PAIRS]) for n in
              ("step", "dec", "cr", "ci", "t1", "t2", "t3")}
        pw_c = place("pw_c", [P, 8, DEPTH, PAIRS])
        pw_s = place("pw_s", [P, 8, DEPTH, PAIRS])
        sinks_e = place("sinks_e", [P, TT, HEADS])
        s_max = place("s_max", [P, TT, HEADS])
        s_den = place("s_den", [P, TT, HEADS])
        yT = place("yT", [P, 2 * UT, T], offset=r_split)
        uT = place("uT", [P, UT, T], offset=r_split + 8192)
        sig = place("sig", [P, UT, T], offset=r_split + 8192)
        qT = place("qT", [P, HPK, T], offset=r_split + 12288)
        kz = place("kz", [P, KVH, T], offset=r_split + 16384)
        vt = place("vt", [P, 3, P], offset=r_split + 18432)
        rot_a = place("rot_a", [P, 2, T], offset=r_split + 20480)
        rot_b = place("rot_b", [P, 2, T], offset=r_split + 22528)
        st_t = place("st_t", [P, 2, T], offset=r_split + 28672)
        bcs = place("bcs", [P, 4, 256], offset=r_split + 24576)
        resid = place("resid", [P, 2, 512], offset=r_split + 20480)
        tab_t = [place("tab_t0", [P, PAIRS, P], offset=r_split), xn[:].rearrange("p t (q n) -> p (t q) n", n=P)]
        cos_t = place("cos_t", [P, PAIRS, T], offset=r_tab)
        sin_t = place("sin_t", [P, PAIRS, T], offset=r_tab + 16384)
        b_re = place("b_re", [P, PAIRS, P], offset=r_blk)
        b_im = place("b_im", [P, PAIRS, P], offset=r_blk + 8192)
        c_re = place("c_re", [P, PAIRS, P], offset=r_blk + 16384)
        c_im = place("c_im", [P, PAIRS, P], offset=r_blk + 24576)
        z = xn[:, :, :].rearrange("p t (c n) -> p (t c) n", n=512)
        z_re = [z[:, 2 * b, :].rearrange("p (q n) -> p q n", q=2) for b in range(2)]
        z_im = [z[:, 2 * b + 1, :].rearrange("p (q n) -> p q n", q=2) for b in range(2)]
        sc = xn[:, :, :].rearrange("p t (h n) -> p t h n", h=HEADS)
        pT = place("pT", [P, TT, HEADS, P], offset=r_hT)
        a_T = place("a_T", [P, FT, T], offset=r_blk)
        hT_hi = place("hT_hi", [P, KC, T], F32R, offset=r_blk + FT * T * 4)
        hT_lo = place("hT_lo", [P, KC, T], F32R, offset=r_hT)
        sil = place("sil", [P, 2 * T], offset=r_blk + FT * T * 4 + 8192)
        w_hi = [place(f"w_hi{i}", [P, UNIT], F32R, offset=r_split + 8192 * i) for i in range(SPLITS)]
        w_lo = [place(f"w_lo{i}", [P, UNIT], F32R, offset=r_split + 8192 * i + 4096) for i in range(SPLITS)]
        e_act = place("e_act", [P, F_E], offset=r_tab)
        eT_hi = place("eT_hi", [P, FE_T, P], F32R, offset=r_tab + 14336)
        eT_lo = place("eT_lo", [P, FE_T, P], F32R, offset=r_tab + 28672)
        hg = place("hg", [P, KC, P], offset=r_tab + 43008)
        hg_hi = place("hg_hi", [P, KC, P], F32R, offset=r_tab + 47104)
        hg_lo = place("hg_lo", [P, KC, P], F32R, offset=r_tab + 51200)
        y_sb = place("y_sb", [P, D], offset=r_tab + 55296)
        e_sil = place("e_sil", [P, 512], offset=r_tab + 59392)
        sel = place("sel", [P, TT, CAP], offset=r_tab + 61440)
        selT = place("selT", [P, TT, P], offset=r_tab + 62464)
        r_acc = region(8192)
        st_re = [place(f"st_re{i}", [P, 2, T], offset=(r_split + 24576, r_split + 30720)[i]) for i in range(2)]
        st_im = [place(f"st_im{i}", [P, 2, T], offset=(r_split + 26624, r_acc + 6144)[i]) for i in range(2)]
        acc = place("acc", [P, TT, D], offset=r_acc)
        mod_acc = place("mod_acc", [P, 2, 512], offset=r_acc)
        mod_diag = place("mod_diag", [P, 4, P], offset=r_acc + 4096)
        lg = place("lg", [P, TT, E])
        top = place("top", [P, TT, 8])
        idx = place("idx", [P, TT, 8], mybir.dt.uint32)
        idx_f = place("idx_f", [P, TT, 8])
        g1 = place("g1", [P, TT])
        g2 = place("g2", [P, TT])
        oh1 = place("oh1", [P, TT, E])
        oh2 = place("oh2", [P, TT, E])
        chosen = place("chosen", [P, TT, JOBS + 1])
        rank = place("rank", [P, TT, JOBS + 1])
        gate_of = place("gate_of", [P, TT, JOBS + 1])
        over_f = place("over_f", [P, 1])
        over = place("over", [P, 1], I32)
        assert at[0] <= nc.sbuf_usable_end, at[0]

        ps = ctx.enter_context(nc.psum_tensor("ps", [P, 8, 512], F32))

        def mod_bank(m):
            if m < 4:
                return (0, 1, 6, 7)[m]
            return m % 2 if m < 10 + GU_MODS else 2 + m % 2

        def const(name):
            a, b = CST[name]
            return k_st[:, a:b]

        def par(l, name):
            a, b = PRM[name]
            return prms[:, l, a:b]

        ident, ones = const("ident"), const("ones")
        mask_ch = const("mask_ch")
        mask_st = const("mask_st").rearrange("p (a g) -> p a g", g=GT)
        c_col = smalls[:, 0:KC]
        w_router = smalls[:, KC:KC + KC * E].rearrange("p (k e) -> p k e", e=E)

        loaded = [sem(f"slot{i}_loaded") for i in range(SLOTS)]
        c_in, small_in, x_in, bc_in, gbias_in, fg_in, stored = (
            sem(n) for n in ("c_in", "small_in", "x_in", "bc_in", "gbias_in", "fg_in", "stored"))
        c_silu, c_spread = sem("c_silu"), sem("c_spread")
        mod_psum, mod_taken, mod_summed, mod_mix, mod_ffn = (
            sem(n) for n in ("mod_psum", "mod_taken", "mod_summed", "mod_mix", "mod_ffn"))
        x_updated, squares, variance, deviation, normed = (
            sem(n) for n in ("x_updated", "squares", "variance", "deviation", "normed"))
        turned, hT_dve, hT_act = sem("turned"), sem("hT_dve"), sem("hT_act")
        projected, proj_out = sem("projected"), sem("proj_out")
        sv_step, sv_angle, sv_trig, sv_ready = (sem(n) for n in ("sv_step", "sv_angle", "sv_trig", "sv_ready"))
        table0, table1 = sem("table0"), sem("table1")
        matrices, bu_psum, bu_used, scanned, rotated = (
            sem(n) for n in ("matrices", "bu_psum", "bu_used", "scanned", "rotated"))
        y_psum, y_skip, y_gelu = sem("y_psum"), sem("y_skip"), sem("y_gelu")
        glu_psum, glu_sig, ssm_sq, attn_sq, ss_psum = (
            sem(n) for n in ("glu_psum", "glu_sig", "ssm_sq", "attn_sq", "ss_psum"))
        kz_zero = sem("kz_zero")
        scores, shifted, exps, probs, probs_T, pT_act, pT_dve, pv_psum = (
            sem(n) for n in ("scores", "shifted", "exps", "probs", "probs_T", "pT_act", "pT_dve", "pv_psum"))
        head_var, head_dev, head_ready = sem("head_var"), sem("head_dev"), sem("head_ready")
        out_psum, hT_high, hT_split, gu_silu, gu_out, down_psum = (
            sem(n) for n in ("out_psum", "hT_high", "hT_split", "gu_silu", "gu_out", "down_psum"))
        logits, diff, diff_e, picked, rank_psum, routed = (
            sem(n) for n in ("logits", "diff", "diff_e", "picked", "rank_psum", "routed"))
        e_high, e_low, e_free = sem("e_high"), sem("e_low"), sem("e_free")
        e_silu, e_prod, e_turned, eT_high, eT_ready = (
            sem(n) for n in ("e_silu", "e_prod", "e_turned", "eT_high", "eT_ready"))
        sel_made, sel_turned, selT_ready, gathered, hg_mod, hg_high, hg_ready = (
            sem(n) for n in ("sel_made", "sel_turned", "selT_ready", "gathered", "hg_mod", "hg_high", "hg_ready"))
        zeroed, y_out, scattered, added = sem("zeroed"), sem("y_out"), sem("scattered"), sem("added")
        dve_step, dve_job, act_step, pool_step = (
            sem(n) for n in ("dve_step", "dve_job", "act_step", "pool_step"))

        def chain(eng, s):
            done = [0]

            def link(ins):
                done[0] += 1
                ins.then_inc(s, 1)
                eng.wait_ge(s, done[0])
            return link

        stream = []

        def cols(w, k0, kn, c0, cn):
            return w.rearrange("(k p) n -> p k n", p=P)[:, k0:k0 + kn, c0:c0 + cn]

        ON_DVE = [(0, cg) for cg in range(5, 12)] + [(1, cg) for cg in range(12)]
        MODS = [(0, cg) for cg in range(12)] + [(1, cg) for cg in range(12)]

        def stream_mod(l, cg):
            if (l, cg) in ON_DVE:
                used = (mod_summed, ON_DVE.index((l, cg)) + 1)
            else:
                used = (mod_psum, MODS.index((l, cg)) + 1)
            for half in range(2):
                stream.append((cols(w_ada[l], 4 * half, 4, 512 * cg, 512), (4, 512), used))
            at_mod[l, cg] = len(stream) - 2

        UNITS = [("u", 0), ("u", 1), ("u", 2), ("u", 3), ("q", 0), ("q", 1), ("q", 2), ("q", 3),
                 ("v", 0), ("k", 0), ("v", 1), ("v", 2)]

        def in_chunk(kind, which):
            c = {"u": 0, "q": 4, "k": 8, "v": 9}[kind] + (0 if kind == "v" else which)
            return c // 2, P * (c % 2)

        FFN_MODS = MODS[10:]
        GG = FT // 2
        GU_MODS = 8
        DOWN_MODS = (0, 1, 3, 4, 6, 7)
        at_mod, at_in, at_glu, at_out, at_gu, at_down = {}, {}, {}, {}, {}, {}
        for l in range(DEPTH):
            if l == 0:
                for cg in range(4):
                    stream_mod(0, cg)
            for i in range(5):
                at_in[l, i] = len(stream)
                last = max(n for n, (kind, which) in enumerate(UNITS) if in_chunk(kind, which)[0] == i)
                stream.append((cols(w_in[l], 0, KC, 256 * i, 256), (KC, 256), (projected, 12 * l + last + 1)))
                if l == 0:
                    for cg in ((), (4, 5), (6,), (7,), (8, 9))[i]:
                        stream_mod(0, cg)
            at_glu[l] = len(stream)
            stream.append((cols(w_glu[l], 0, UT, 0, D_SSM), (UT, D_SSM), (glu_psum, 4 * l + 4)))
            for n in range(4):
                at_out[l, n] = len(stream)
                stream.append((cols(w_out[l], 4 * (n // 2), 4, 512 * (n % 2), 512), (4, 512),
                               (out_psum, 5 * l + (1, 3, 5, 5)[n])))
            if l == 0:
                for g in range(GG):
                    at_gu[g] = len(stream)
                    for i, w in enumerate((w_gate, w_up)):
                        stream.append((cols(w[0], 0, KC, 256 * g, 256), (KC, 256), (e_low, 4 * g + 2 * i + 2)))
                    if g < GU_MODS:
                        stream_mod(*FFN_MODS[g])
                for n in range(GG):
                    at_down[n] = len(stream)
                    stream.append((cols(w_down[0], 2 * n, 2, 0, D), (2, D), (down_psum, n + 1 + n // (GG - 1))))
                    if n in DOWN_MODS:
                        stream_mod(*FFN_MODS[GU_MODS + DOWN_MODS.index(n)])
        U0 = 4 * GG
        base = len(stream)

        def slot(n, shape):
            return ring[:, n % SLOTS, :].rearrange("p (a b) -> p a b", a=shape[0])

        def chunk(eng, n):
            eng.wait_ge(loaded[n % SLOTS], 16 * (n // SLOTS + 1))
            return slot(n, stream[n][1])

        assert PER_JOB % SLOTS == 0 and UPJ % SPLITS == 0 and U0 % SPLITS == 0 and len(FFN_MODS) == GU_MODS + len(DOWN_MODS)
        turns = PER_JOB // SLOTS

        def loaded_by(job, k):
            return 16 * ((base + k) // SLOTS + 1) + 16 * turns * job

        block = ctx.enter_context(nc.Block())

        @block.sync
        def _(sp):
            sp.dma_start(smalls[:], small).then_inc(c_in, 16)
            sp.dma_start(prms[:], prm).then_inc(small_in, 16)
            sp.dma_start(k_st[:], cst).then_inc(small_in, 16)

            def load(n):
                src, shape, _ = stream[n]
                if n >= SLOTS:
                    s, v = stream[n - SLOTS][2]
                    sp.wait_ge(s, v)
                sp.dma_start(slot(n, shape), src).then_inc(loaded[n % SLOTS], 16)

            for n in range(base):
                load(n)
                if n == 3:
                    sp.dma_start(xs[:], x[0].rearrange("(t p) d -> p t d", p=P)).then_inc(x_in, 16)

            def load_job(job, expert, first=False):
                def expert_cols(w, k0, kn, c0, cn):
                    return w[bass.ds(expert, 1)].rearrange("a (k p) n -> p (a k) n", p=P)[:, k0:k0 + kn, c0:c0 + cn]
                for k in range(PER_JOB):
                    if k < 4 * FG:
                        w = (moe_gate, moe_up)[k // 2 % 2][0]
                        src, shape = expert_cols(w, 4 * (k % 2), 4, 512 * (k // 4), 512), (4, 512)
                    else:
                        src, shape = expert_cols(moe_down[0], 2 * (k - 4 * FG), 2, 0, D), (2, D)
                    if first and k < SLOTS:
                        sp.wait_ge(*stream[base + k - SLOTS][2])
                    else:
                        sp.wait_ge(e_low, U0 + UPJ * job + 2 * (k - SLOTS + 1))
                    sp.dma_start(slot(base + k, shape), src).then_inc(loaded[(base + k) % SLOTS], 16)

            load_job(0, 0, first=True)
            with sp.Fori(1, E) as job:
                load_job(job, job)
            sp.wait_ge(routed, 1)
            more = sp.value_load(over[0:1, 0:1], min_val=0, max_val=1)
            with sp.If(more > 0):
                with sp.Fori(E, JOBS) as job:
                    load_job(job, job - E)
            with sp.Else():
                sp.nop()
            for t in range(TT):
                sp.wait_ge(normed, 2 * 4 + t + 1)
                sp.dma_start(out[0, P * t:P * t + P, :], xn[:, t, :]).then_inc(stored, 16)
            sp.wait_ge(stored, 16 * TT)

        def make_table(eng, ops, l, link, ready, levels=range(8)):
            if 0 in levels:
                ops.memset(cos_t[:, :, 0:1], 1.0)
                link(ops.memset(sin_t[:, :, 0:1], 0.0))
            for m in levels:
                n = 1 << m
                wide = lambda v: v[:, m, l, :].unsqueeze(2).to_broadcast([P, PAIRS, n])
                cl, sl = wide(pw_c), wide(pw_s)
                c0, s0 = cos_t[:, :, 0:n], sin_t[:, :, 0:n]
                c1, s1 = cos_t[:, :, n:2 * n], sin_t[:, :, n:2 * n]
                tt = tab_t[l][:, :, 0:n]
                ops.tensor_tensor(c1, c0, cl, ALU.mult)
                link(ops.tensor_tensor(tt, s0, sl, ALU.mult))
                link(ops.tensor_tensor(c1, c1, tt, ALU.subtract))
                ops.tensor_tensor(s1, s0, cl, ALU.mult)
                link(ops.tensor_tensor(tt, c0, sl, ALU.mult))
                ins = ops.tensor_tensor(s1, s1, tt, ALU.add)
                if m < 7:
                    link(ins)
                else:
                    ins.then_inc(ready, 1)
                    eng.wait_ge(ready, 1)

        @block.gpsimd
        def _(pool):
            link = chain(pool, pool_step)

            def load_params(l):
                if l:
                    pool.wait_ge(gu_out, GG)
                pool.dma_start(bcs[:], bc[l]).then_inc(bc_in, 16)

            def load_gate(dst, src, s):
                pool.dma_start(dst[:], src.partition_broadcast(P)).then_inc(s, 16)

            def make_matrices(l):
                pool.wait_ge(bc_in, 16 * (l + 1))
                pool.wait_ge(small_in, 32)
                pool.wait_ge(sv_ready, 1)
                if l:
                    pool.wait_ge(down_psum, GG + 1)
                for m, dst in ((0, b_re), (1, b_im)):
                    o = dst[:].rearrange("p (u q) (b s) -> p u (q b) s", u=UT, b=2)
                    v = bcs[:, m, :].rearrange("p (u s) -> p u s", u=UT)
                    nc.gpsimd.tensor_tensor(o, v.unsqueeze(2).to_broadcast([P, UT, GT, STATE]),
                                            mask_ch.unsqueeze(1).unsqueeze(3).to_broadcast([P, UT, GT, STATE]),
                                            ALU.mult)
                cre, cim = (bcs[:, m, :].rearrange("p (q h) -> p q h", h=GROUP) for m in (2, 3))
                t0, t1 = (st_t[:, m, :].rearrange("p (q h) -> p q h", h=GROUP) for m in (0, 1))
                kr, ki, nkr, nki = (sv[n][:, l, :].unsqueeze(2).to_broadcast([P, PAIRS, GROUP])
                                    for n in ("cr", "ci", "t1", "t2"))
                nc.gpsimd.tensor_tensor(t0, cre, kr, ALU.mult)
                link(nc.gpsimd.tensor_tensor(t1, cim, ki, ALU.mult))
                nc.gpsimd.tensor_tensor(t0, t0, t1, ALU.subtract)
                nc.gpsimd.tensor_tensor(cre, cre, nki, ALU.mult)
                link(nc.gpsimd.tensor_tensor(cim, cim, nkr, ALU.mult))
                link(nc.gpsimd.tensor_tensor(cre, cre, cim, ALU.add))
                for v, dst in ((t0, c_re), (cre, c_im)):
                    for u in range(UT):
                        o = dst[:, 4 * u:4 * u + 4, :].rearrange("p q (g h) -> p q g h", h=GROUP)
                        ins = nc.gpsimd.tensor_tensor(
                            o, v[:, 4 * u:4 * u + 4, :].unsqueeze(2).to_broadcast([P, 4, GT, GROUP]),
                            mask_st.unsqueeze(3).to_broadcast([P, 4, GT, GROUP]), ALU.mult)
                ins.then_inc(matrices, 1)

            def turn_back(l, j):
                pool.wait_ge(scanned, 8 * l + j + 1)
                if 8 * l + j >= 2:
                    pool.wait_ge(y_psum, 8 * l + j - 1)
                if j == 0:
                    pool.wait_ge(matrices, l + 1)
                q0 = 2 * j
                zr, zi = z_re[j % 2], z_im[j % 2]
                cs, sn = cos_t[:, q0:q0 + 2, :], sin_t[:, q0:q0 + 2, :]
                re, im = st_re[j % 2][:], st_im[j % 2][:]
                nc.gpsimd.tensor_tensor(re, zr, cs, ALU.mult)
                link(nc.gpsimd.tensor_tensor(im, zi, sn, ALU.mult))
                link(nc.gpsimd.tensor_tensor(re, re, im, ALU.subtract))
                nc.gpsimd.tensor_tensor(im, zr, sn, ALU.mult)
                link(nc.gpsimd.tensor_tensor(st_t[:], zi, cs, ALU.mult))
                nc.gpsimd.tensor_tensor(im, im, st_t[:], ALU.add).then_inc(rotated, 1)

            load_params(0)
            nc.gpsimd.memset(kz[:], 0.0).then_inc(kz_zero, 1)
            make_matrices(0)
            load_gate(gate_m, b_ada[0, G_M * D:(G_M + 1) * D], gbias_in)
            load_gate(gate_f, b_ada[0, G_F * D:(G_F + 1) * D], gbias_in)
            for j in range(8):
                turn_back(0, j)
            pool.wait_ge(x_updated, 2)
            pool.wait_ge(gbias_in, 32)
            load_gate(gate_m, b_ada[1, G_M * D:(G_M + 1) * D], gbias_in)
            pool.wait_ge(bu_used, 8)
            pool.wait_ge(out_psum, 5)
            pool.wait_ge(mod_psum, 9)
            pool.wait_ge(gbias_in, 48)
            load_gate(gate_f1, b_ada[1, G_F * D:(G_F + 1) * D], gbias_in)
            pool.wait_ge(turned, 8)
            make_table(pool, nc.gpsimd, 1, link, table1)
            load_params(1)
            nc.gpsimd.memset(kz[:], 0.0).then_inc(kz_zero, 1)
            make_matrices(1)
            for j in range(8):
                turn_back(1, j)
            pool.wait_ge(x_updated, 6)
            load_gate(gate_m, final_g, fg_in)

        @block.scalar
        def _(act):
            link = chain(act, act_step)
            A = nc.scalar.activation

            def norm(n):
                for t in range(TT):
                    act.wait_ge(x_updated, 2 * (n - 1) + t + 1) if n else act.wait_ge(x_in, 16)
                    if n == 2:
                        act.wait_ge(table1, 1)
                    A(xn[:, t, :], xs[:, t, :], ACT.Square, accum_out=sq_sum[:, t:t + 1]).then_inc(squares, 1)
                    act.wait_ge(variance, 2 * n + t + 1)
                    A(rstd[:, t:t + 1], rstd[:, t:t + 1], ACT.Sqrt).then_inc(deviation, 1)

            def modulate(n):
                which = n % 2
                act.wait_ge((mod_mix, mod_ffn)[which], n // 2 + 1)
                act.wait_ge(turned, 4 * (n + 1))
                for kc in range(4, KC):
                    A(hT[:, kc, :], ps[:, 2 + kc // 2, 256 * (kc % 2):256 * (kc % 2) + 256], ACT.Identity,
                      bias=mod_s[:, which, kc:kc + 1], scale=mod_a[:, which, kc:kc + 1]).then_inc(hT_act, 1)

            act.wait_ge(c_in, 16)
            A(c_act[:], c_col, ACT.Silu).then_inc(c_silu, 1)
            act.wait_ge(small_in, 32)
            a, b = PRM["log_step"]
            A(sv["step"][:], prms[:, :, a:b], ACT.Exp).then_inc(sv_step, 1)
            act.wait_ge(sv_angle, 1)
            A(sv["dec"][:], sv["dec"][:], ACT.Exp)
            A(pw_s[:], pw_c[:], ACT.Sin)
            A(pw_c[:], pw_c[:], ACT.Sin, scale=0.5).then_inc(sv_trig, 1)
            norm(0)

            for l in range(DEPTH):
                if l:
                    norm(2)
                modulate(2 * l)
                def gelu(u):
                    act.wait_ge(y_skip, 4 * l + u + 1)
                    A(yT[:, u, :], yT[:, u, :], ACT.Gelu_apprx_tanh).then_inc(y_gelu, 1)

                for n, (kind, which) in enumerate(UNITS):
                    act.wait_ge(projected, 12 * l + n + 1)
                    if kind == "u":
                        nc.scalar.copy(uT[:, which, :], ps[:, 7, 0:T]).then_inc(proj_out, 1)
                    elif kind == "q":
                        nc.scalar.mul(qT[:, which, :], ps[:, 7, 0:T], HD ** -0.5).then_inc(proj_out, 1)
                    elif kind == "k":
                        act.wait_ge(kz_zero, l + 1)
                        link(nc.scalar.copy(kz[0:HD, 0, :], ps[0:HD, 7, 0:T]))
                        nc.scalar.copy(kz[HD:P, 1, :], ps[HD:P, 7, 0:T]).then_inc(proj_out, 1)
                    else:
                        nc.scalar.copy(vt[:, which, :], ps[:, 7, 0:P]).then_inc(proj_out, 1)
                    if n in (8, 10):
                        gelu(n // 2 - 4)
                gelu(2)
                gelu(3)
                for o in range(UT):
                    act.wait_ge(glu_psum, 4 * l + o // 2 * 2 + 2)
                    if o == 0:
                        act.wait_ge(y_skip, 4 * l + 4)
                    A(sig[:, o, :], ps[:, 6 + o // 2, 256 * (o % 2):256 * (o % 2) + 256],
                      ACT.Sigmoid).then_inc(glu_sig, 1)
                act.wait_ge(shifted, l + 1)
                A(sc, sc, ACT.Exp).then_inc(exps, 1)
                A(sinks_e[:], sinks_e[:], ACT.Exp).then_inc(exps, 1)
                act.wait_ge(probs_T, 2 * l + 1)
                nc.scalar.copy(pT[:, 0, :, :].rearrange("p h n -> p (h n)"),
                               ps[:, 2:4, :].rearrange("p b n -> p (b n)")).then_inc(pT_act, 1)
                act.wait_ge(head_var, l + 1)
                A(head_rs[:], head_ss[:], ACT.Sqrt).then_inc(head_dev, 1)
                norm(2 * l + 1)
                modulate(2 * l + 1)
                if l == 0:
                    act.wait_ge(hT_dve, 8)
                    act.wait_ge(hT_act, 8)
                    link(nc.scalar.copy(hT_hi[:, 4:, :], hT[:, 4:, :]))
                    nc.scalar.copy(hT_hi[:, 0:4, :], hT[:, 0:4, :]).then_inc(hT_high, 1)

                    def silu(g):
                        act.wait_ge(e_free, SPLITS + 4 * (g + 1))
                        if g:
                            act.wait_ge(gu_out, g)
                        A(sil[:], ps[:, 2 + 2 * (g % 2), :], ACT.Silu).then_inc(gu_silu, 1)

                    act.wait_ge(e_free, SPLITS)
                    for g in range(GG):
                        for i in range(4):
                            u = 4 * g + i
                            src = chunk(act, at_gu[g] + i // 2)
                            if u >= SPLITS:
                                act.wait_ge(e_free, u + 1)
                            nc.scalar.copy(w_hi[i][:], src[:, 4 * (i % 2):4 * (i % 2) + 4, :]).then_inc(e_high, 1)
                        if g:
                            silu(g - 1)
                    silu(GG - 1)

            act.wait_ge(diff, 1)
            A(g2[:], g2[:], ACT.Exp).then_inc(diff_e, 1)
            act.wait_ge(routed, 1)
            more = act.value_load(over[0:1, 0:1], min_val=0, max_val=1)

            def gathered_high(job):
                for h in range(2):
                    act.wait_ge(hg_mod, 2 * job + h + 1)
                    nc.scalar.copy(hg_hi[:, 4 * h:4 * h + 4, :], hg[:, 4 * h:4 * h + 4, :]).then_inc(hg_high, 1)

            def products_out(job):
                act.wait_ge(e_free, U0 + UPJ * job + SPLITS)
                act.wait_ge(scattered, job)
                for h in range(2):
                    nc.scalar.copy(y_sb[:, 512 * h:512 * h + 512], ps[:, 6 + h, :]).then_inc(y_out, 1)

            gathered_high(0)
            act.wait_ge(zeroed, 1)

            def act_job(job):
                for k in range(PER_JOB):
                    n = base + k
                    act.wait_ge(loaded[n % SLOTS], loaded_by(job, k))
                    for u in (2 * k, 2 * k + 1):
                        act.wait_ge(e_free, U0 + UPJ * job + u + 1)
                        nc.scalar.copy(w_hi[u % SPLITS][:],
                                       ring[:, n % SLOTS, UNIT * (u % 2):UNIT * (u % 2) + UNIT]).then_inc(e_high, 1)
                    if k == 1:
                        products_out(job)
                    if k == 6:
                        act.wait_ge(sel_turned, job + 1)
                        nc.scalar.copy(selT[:].rearrange("p t n -> p (t n)"), ps[:, 4, 0:T]).then_inc(selT_ready, 1)
                    g = (k - 5) // 4
                    if (k - 5) % 4 == 0 and 0 <= g < FG:
                        act.wait_ge(e_free, U0 + UPJ * job + SPLITS + 2 * (4 * g + 4))
                        act.wait_ge(e_prod, FG * job + g)
                        A(e_sil[:], ps[:, g % 2, :], ACT.Silu).then_inc(e_silu, 1)
                    g = (k - 10) // 4
                    if (k - 10) % 4 == 0 and 0 <= g < FG:
                        act.wait_ge(e_turned, FG * job + g + 1)
                        nc.scalar.copy(eT_hi[:, 4 * g:4 * g + 4, :].rearrange("p f n -> p (f n)"),
                                       ps[:, 4 + g % 2, :]).then_inc(eT_high, 1)
                    if k == 38:
                        gathered_high(job + 1)

            with act.Fori(0, E) as job:
                act_job(job)
            with act.If(more > 0):
                with act.Fori(E, JOBS) as job:
                    act_job(job)
                products_out(JOBS)
            with act.Else():
                products_out(E)
            norm(4)


        @block.vector
        def _(dve):
            link = chain(dve, dve_step)
            V = nc.vector
            TTo, TS, STT = V.tensor_tensor, V.tensor_scalar, V.scalar_tensor_tensor

            def norm_tile(n, t):
                one = slice(t, t + 1)
                dve.wait_ge(squares, 2 * n + t + 1)
                TS(rstd[:, one], sq_sum[:, one], 1.0 / D, EPS, ALU.mult, ALU.add).then_inc(variance, 1)
                dve.wait_ge(deviation, 2 * n + t + 1)
                link(V.reciprocal(rstd[:, one], rstd[:, one]))
                if n < 4:
                    TS(xn[:, t, :], xs[:, t, :], rstd[:, one], None, ALU.mult).then_inc(normed, 1)
                else:
                    dve.wait_ge(fg_in, 16)
                    STT(xn[:, t, :], xs[:, t, :], rstd[:, one], gate_m[:], ALU.mult, ALU.mult).then_inc(normed, 1)

            def norm(n):
                for t in range(TT):
                    norm_tile(n, t)

            def take(l, cg):
                m = MODS.index((l, cg))
                dve.wait_ge(mod_psum, m + 1)
                bank = ps[:, mod_bank(m), :]
                if cg // 2 in (G_M, G_F):
                    dve.wait_ge(gbias_in, 32 if l == 0 else 64)
                    dst = (gate_m if cg // 2 == G_M else (gate_f, gate_f1)[l])[:, 512 * (cg % 2):512 * (cg % 2) + 512]
                    ins = TTo(dst, dst, bank, ALU.add)
                else:
                    if m:
                        dve.wait_ge(mod_taken, m)
                    for i in range(4):
                        ins = V.tensor_tensor_reduce(mod_diag[:, i, :], bank[:, P * i:P * i + P], ident, 1.0, 0.0,
                                                     ALU.mult, ALU.add, mod_raw[:, 4 * cg + i:4 * cg + i + 1])
                ins.then_inc(mod_taken, 1)

            def sum_mod(l, cg, ks):
                d = ON_DVE.index((l, cg))
                part = mod_acc[:, d % 2, :]
                for k in ks:
                    w = chunk(dve, at_mod[l, cg] + k // 4)[:, k % 4, :]
                    if k == 0:
                        if d >= 2:
                            dve.wait_ge(mod_psum, MODS.index(ON_DVE[d - 2]) + 1)
                        link(TS(part, w, c_act[:, 0:1], None, ALU.mult))
                    elif k < KC - 1:
                        link(STT(part, w, c_act[:, k:k + 1], part, ALU.mult, ALU.add))
                    else:
                        STT(part, w, c_act[:, k:k + 1], part, ALU.mult, ALU.add).then_inc(mod_summed, 1)

            def finish_mod(l, which):
                dve.wait_ge(mod_taken, 12 * l + (4 if which == 0 else 10))
                b = par(l, "b_ada").rearrange("p (m k) -> p m k", k=KC)
                raw = mod_raw[:].rearrange("p (m k) -> p m k", k=KC)
                shift, scale = (SH_M, SC_M) if which == 0 else (SH_F, SC_F)
                link(TTo(mod_s[:, which, :], raw[:, shift, :], b[:, shift, :], ALU.add))
                link(STT(mod_a[:, which, :], raw[:, scale, :], 1.0, b[:, scale, :], ALU.add, ALU.add))
                TTo(mod_a[:, which, :], mod_a[:, which, :], par(l, ("g_mix", "g_ffn")[which]),
                    ALU.mult).then_inc((mod_mix, mod_ffn)[which], 1)
                dve.wait_ge((mod_mix, mod_ffn)[which], l + 1)

            def modulate(n):
                which = n % 2
                dve.wait_ge(turned, 4 * n + 2)
                for kc in range(4):
                    TS(hT[:, kc, :], ps[:, 2 + kc // 2, 256 * (kc % 2):256 * (kc % 2) + 256],
                       mod_a[:, which, kc:kc + 1], mod_s[:, which, kc:kc + 1], ALU.mult, ALU.add).then_inc(hT_dve, 1)

            def state_scalars():
                a, b = PRM["lam_re"]
                lre = prms[:, :, a:b]
                a, b = PRM["lam_im"]
                lim = prms[:, :, a:b]
                t1, t2, t3 = sv["t1"][:], sv["t2"][:], sv["t3"][:]
                dve.wait_ge(sv_step, 1)
                TTo(sv["dec"][:], lre, sv["step"][:], ALU.mult)
                link(TTo(t1, lim, sv["step"][:], ALU.mult))
                for m in range(8):
                    ins = TS(pw_c[:, m], t1, float(1 << m), None, ALU.mult)
                link(ins)
                link(TS(pw_s[:], pw_c[:], 1.0 / (2 * math.pi), ROUND, ALU.mult, ALU.add))
                link(TS(pw_s[:], pw_s[:], -ROUND, None, ALU.add))
                for part in (TWO_PI_HI, TWO_PI_MID, TWO_PI_LO):
                    link(STT(pw_c[:], pw_s[:], -part, pw_c[:], ALU.mult, ALU.add))
                TS(pw_c[:], pw_c[:], 3.1415925, -3.1415925, ALU.min, ALU.max).then_inc(sv_angle, 1)
                dve.wait_ge(sv_trig, 1)
                link(TTo(pw_c[:], pw_c[:], pw_c[:], ALU.mult))
                link(TS(pw_c[:], pw_c[:], -2.0, 1.0, ALU.mult, ALU.add))
                dec, cr, ci = sv["dec"][:], sv["cr"][:], sv["ci"][:]
                TTo(t1, dec, pw_c[:, 0], ALU.mult)
                link(TTo(t2, dec, pw_s[:, 0], ALU.mult))
                link(TS(t1, t1, -1.0, None, ALU.add))
                TTo(cr, t1, lre, ALU.mult)
                link(TTo(t3, t2, lim, ALU.mult))
                link(TTo(cr, cr, t3, ALU.add))
                TTo(ci, t2, lre, ALU.mult)
                link(TTo(t3, t1, lim, ALU.mult))
                link(TTo(ci, ci, t3, ALU.subtract))
                TTo(t1, lre, lre, ALU.mult)
                link(TTo(t2, lim, lim, ALU.mult))
                link(TTo(t1, t1, t2, ALU.add))
                link(V.reciprocal(t1, t1))
                TTo(cr, cr, t1, ALU.mult)
                link(TTo(ci, ci, t1, ALU.mult))
                link(TS(t1, cr, -1.0, None, ALU.mult))
                TS(t2, ci, -1.0, None, ALU.mult).then_inc(sv_ready, 1)

            dve.wait_ge(c_silu, 1)
            V.tensor_copy(c_wide[:], c_act[:].unsqueeze(2).to_broadcast([P, KC, P])).then_inc(c_spread, 1)
            dve.wait_ge(small_in, 32)
            state_scalars()
            make_table(dve, V, 0, link, table0, range(5))
            norm(0)
            make_table(dve, V, 0, link, table0, range(5, 6))

            for l in range(DEPTH):
                if l == 0:
                    take(0, 0)
                    make_table(dve, V, 0, link, table0, range(6, 7))
                    for cg in range(1, 4):
                        take(0, cg)
                    finish_mod(0, 0)
                modulate(2 * l)
                if l == 0:
                    make_table(dve, V, 0, link, table0, range(7, 8))
                if l:
                    dve.wait_ge(table1, 1)

                def skip(u):
                    dve.wait_ge(y_psum, 8 * l + 2 * u + 2)
                    d0 = PRM["d_skip"][0] + u
                    STT(yT[:, u, :], uT[:, u, :], prms[:, l, d0:d0 + 1], ps[:, 6, 0:T],
                        ALU.mult, ALU.add).then_inc(y_skip, 1)

                for j in range(8):
                    b = 2 + 2 * (j % 2)
                    re, im = (ps[:, b + m, :].rearrange("p (q n) -> p q n", q=2) for m in (0, 1))
                    cs, sn = cos_t[:, 2 * j:2 * j + 2, :], sin_t[:, 2 * j:2 * j + 2, :]
                    zr, zi = z_re[j % 2], z_im[j % 2]
                    dve.wait_ge(bu_psum, 8 * l + j + 1)
                    if 8 * l + j >= 2:
                        dve.wait_ge(rotated, 8 * l + j - 1)
                    TTo(zr, re, cs, ALU.mult)
                    link(TTo(rot_a[:], im, sn, ALU.mult))
                    link(TTo(zr, zr, rot_a[:], ALU.add))
                    TTo(zi, im, cs, ALU.mult)
                    TTo(rot_b[:], re, sn, ALU.mult).then_inc(bu_used, 1)
                    dve.wait_ge(bu_used, 8 * l + j + 1)
                    link(TTo(zi, zi, rot_b[:], ALU.subtract))
                    for q in range(2):
                        decay = sv["dec"][:, l, 2 * j + q:2 * j + q + 1].to_broadcast([P, T])
                        for v in (zr, zi):
                            ins = V.tensor_tensor_scan(v[:, q, :], decay, v[:, q, :], 0.0, ALU.mult, ALU.add)
                    ins.then_inc(scanned, 1)
                    if j in (3, 5, 7):
                        skip((j - 3) // 2)
                    if l == 0:
                        if j % 2:
                            take(0, 4 + j // 2)
                        if j in (0, 2, 4, 5, 6):
                            sum_mod(0, (5, 0, 6, 0, 7, 8, 9)[j], range(KC))
                skip(3)
                if l == 0:
                    take(0, 8)
                    take(0, 9)
                    finish_mod(0, 1)

                dve.wait_ge(scores, 2 * (l + 1))
                dve.wait_ge(rotated, 8 * (l + 1))
                banks = lambda p0, p1, b: ps[p0:p1, b:b + 2, :].rearrange("p b (h n) -> p (b h) n", n=P)
                V.tensor_copy(sc[HD:P, 0], banks(HD, P, 2))
                V.tensor_copy(sc[0:HD, 0, :, 0:CH], banks(0, HD, 2)[:, :, 0:CH])
                V.memset(sc[0:HD, 0, :, CH:P], NEG)
                link(V.tensor_copy(sc[:, 1], banks(0, P, 4)))
                link(V.tensor_reduce(s_max[:], sc, AX, ALU.max))
                sinks = par(l, "sinks").unsqueeze(1).to_broadcast([P, TT, HEADS])
                link(TTo(s_max[:], s_max[:], sinks, ALU.max))
                link(TTo(sinks_e[:], sinks, s_max[:], ALU.subtract))
                TTo(sc, sc, s_max[:].unsqueeze(3).to_broadcast([P, TT, HEADS, P]), ALU.subtract).then_inc(shifted, 1)

                dve.wait_ge(glu_sig, 4 * (l + 1))
                link(TTo(yT[:, 0:UT, :], yT[:, 0:UT, :], sig[:], ALU.mult))
                TTo(sig[:], yT[:, 0:UT, :], yT[:, 0:UT, :], ALU.mult).then_inc(ssm_sq, 1)
                dve.wait_ge(ssm_sq, 2 * l + 1)
                for u in range(UT):
                    g0 = PRM["g_ssm"][0] + u
                    ins = TS(yT[:, u, :], yT[:, u, :], prms[:, l, g0:g0 + 1], None, ALU.mult)
                ins.then_inc(ssm_sq, 1)

                dve.wait_ge(exps, 2 * (l + 1))
                link(V.tensor_reduce(s_den[:], sc, AX, ALU.add))
                link(TTo(s_den[:], s_den[:], sinks_e[:], ALU.add))
                link(V.reciprocal(s_den[:], s_den[:]))
                TTo(sc, sc, s_den[:].unsqueeze(3).to_broadcast([P, TT, HEADS, P]), ALU.mult).then_inc(probs, 1)

                dve.wait_ge(probs_T, 2 * (l + 1))
                V.tensor_copy(pT[:, 1, :, :].rearrange("p h n -> p (h n)"),
                              ps[:, 4:6, :].rearrange("p b n -> p (b n)")).then_inc(pT_dve, 1)
                dve.wait_ge(pv_psum, l + 1)
                for b in range(2):
                    src = ps[:, 6 + b, :].rearrange("p (c j n) -> p j c n", c=2, j=HPK)
                    dst = yT[:, UT:2 * UT, P * b:P * b + P].rearrange("p j (c n) -> p j c n", c=2)
                    ins = V.tensor_copy(dst, src)
                link(ins)
                dve.wait_ge(ss_psum, 2 * l + 1)
                TTo(sig[:], yT[:, UT:2 * UT, :], yT[:, UT:2 * UT, :], ALU.mult).then_inc(attn_sq, 1)
                dve.wait_ge(attn_sq, 2 * l + 1)
                for u in range(UT):
                    g0 = PRM["g_attn"][0] + u
                    ins = TS(yT[:, UT + u, :], yT[:, UT + u, :], prms[:, l, g0:g0 + 1], None, ALU.mult)
                ins.then_inc(attn_sq, 1)
                dve.wait_ge(ss_psum, 2 * (l + 1))
                TS(head_ss[:, 0:2], ps[:, 4, 0:2], 1.0 / D_SSM, EPS, ALU.mult, ALU.add)
                TS(head_ss[:, 2:4], ps[:, 5, 0:2], 1.0 / D_SSM, EPS, ALU.mult, ALU.add).then_inc(head_var, 1)
                dve.wait_ge(head_dev, l + 1)
                V.reciprocal(head_rs[:], head_rs[:]).then_inc(head_ready, 1)
                dve.wait_ge(head_ready, l + 1)
                def join(t, n, bank, rs):
                    part = slice(512 * n, 512 * n + 512)
                    link(STT(resid[:, n, :], ps[:, bank, :], head_rs[:, rs:rs + 1], gate_m[:, part],
                             ALU.mult, ALU.mult))
                    return TTo(xs[:, t, part], xs[:, t, part], resid[:, n, :], ALU.add)

                for n in range(2):
                    for t in range(TT):
                        dve.wait_ge(out_psum, 5 * l + (1, 1, 2, 3)[2 * n + t])
                        link(join(t, n, 2 * n + t, t))
                for t in range(TT):
                    dve.wait_ge(out_psum, 5 * l + 4 + t)
                    link(join(t, 0, 4 + 2 * t, 2 + t))
                    join(t, 1, 5 + 2 * t, 2 + t).then_inc(x_updated, 1)
                    norm_tile(2 * l + 1, t)
                modulate(2 * l + 1)
                if l == 0:
                    dve.wait_ge(hT_high, 1)
                    TTo(hT_lo[:], hT[:], hT_hi[:].bitcast(F32), ALU.subtract).then_inc(hT_split, 1)

                    def product(g):
                        dve.wait_ge(gu_silu, g + 1)
                        TTo(a_T[:, 2 * g:2 * g + 2, :].rearrange("p f n -> p (f n)"), sil[:],
                            ps[:, 3 + 2 * (g % 2), :], ALU.mult).then_inc(gu_out, 1)

                    for g in range(GG):
                        for i in range(4):
                            dve.wait_ge(e_high, 4 * g + i + 1)
                            part = ring[:, (at_gu[g] + i // 2) % SLOTS, UNIT * (i % 2):UNIT * (i % 2) + UNIT]
                            TTo(w_lo[i][:], part, w_hi[i][:].bitcast(F32), ALU.subtract).then_inc(e_low, 1)
                            if 1 <= g <= GU_MODS:
                                sum_mod(*FFN_MODS[g - 1], (2 * i, 2 * i + 1))
                            if i == 2 and 2 <= g <= GU_MODS + 1:
                                take(*FFN_MODS[g - 2])
                        if g:
                            product(g - 1)
                    product(GG - 1)
                    for i in range(GU_MODS, len(FFN_MODS)):
                        sum_mod(*FFN_MODS[i], range(KC))
                        if i > GU_MODS:
                            take(*FFN_MODS[i - 1])
                    take(*FFN_MODS[-1])
                    finish_mod(1, 0)
                    finish_mod(1, 1)
                    for t in range(TT):
                        dve.wait_ge(down_psum, GG + t)
                        for n in range(2):
                            bank = (6, 7, 0, 1)[2 * t + n]
                            part = slice(512 * n, 512 * n + 512)
                            link(TTo(resid[:, n, :], ps[:, bank, :], gate_f[:, part], ALU.mult))
                            ins = TTo(xs[:, t, part], xs[:, t, part], resid[:, n, :], ALU.add)
                            if n == 0:
                                link(ins)
                        ins.then_inc(x_updated, 1)
                        if t == 0:
                            dve.wait_ge(table1, 1)
                        norm_tile(2, t)

            dve.wait_ge(logits, 1)
            link(V.tensor_copy(lg[:].rearrange("p t e -> p (t e)"), ps[:, 6, 0:TT * E]))
            for t in range(TT):
                link(V.max(top[:, t, :], lg[:, t, :]))
                link(V.max_index(idx[:, t, :], top[:, t, :], lg[:, t, :]))
            link(V.tensor_copy(idx_f[:], idx[:]))
            TTo(g2[:], top[:, :, 1], top[:, :, 0], ALU.subtract).then_inc(diff, 1)
            iota = const("iota")
            for t in range(TT):
                TS(oh1[:, t, :], iota[:, 0:E], idx_f[:, t, 0:1], None, ALU.is_equal)
                link(TS(oh2[:, t, :], iota[:, 0:E], idx_f[:, t, 1:2], None, ALU.is_equal))
            link(V.memset(gate_of[:, :, 0:1], 0.0))
            TTo(chosen[:, :, 0:E], oh1[:], oh2[:], ALU.add)
            TTo(chosen[:, :, E:2 * E], oh1[:], oh2[:], ALU.add)
            TTo(chosen[:, :, 2 * E:], oh1[:, :, 0:1], oh2[:, :, 0:1], ALU.add).then_inc(picked, 1)
            dve.wait_ge(diff_e, 1)
            link(TS(g1[:], g2[:], 1.0, None, ALU.add))
            link(V.reciprocal(g1[:], g1[:]))
            link(TTo(g2[:], g2[:], g1[:], ALU.mult))
            for t in range(TT):
                link(TS(oh1[:, t, :], oh1[:, t, :], g1[:, t:t + 1], None, ALU.mult))
                link(STT(gate_of[:, t, 1:E + 1], oh2[:, t, :], g2[:, t:t + 1], oh1[:, t, :], ALU.mult, ALU.add))
            link(V.tensor_copy(gate_of[:, :, E + 1:], gate_of[:, :, 1:E + 1]))
            dve.wait_ge(rank_psum, 1)
            r = ps[:, 7, 0:TT * E].rearrange("p (t e) -> p t e", t=TT)
            V.tensor_copy(rank[:, :, 0:E], r)
            TS(rank[:, :, E:2 * E], r, -float(CAP), None, ALU.add)
            V.tensor_copy(rank[:, :, 2 * E:], r[:, :, 0:1])
            link(V.tensor_reduce(over_f[:], ps[:, 7, 16:16 + E], AX, ALU.max))
            TS(over[:], over_f[:], float(CAP), None, ALU.is_gt).then_inc(routed, 1)
            dve.wait_ge(routed, 1)
            more = dve.value_load(over[0:1, 0:1], min_val=0, max_val=1)

            def choose(job):
                for t in range(TT):
                    TS(sel[:, t, :], iota, rank[:, t, bass.ds(job, 1)], chosen[:, t, bass.ds(job, 1)],
                       ALU.is_equal, ALU.mult).then_inc(sel_made, 1)

            def gathered_mod(job):
                for kc in range(KC):
                    if kc % 4 == 0:
                        dve.wait_ge(gathered, 2 * job + kc // 4 + 1)
                    TS(hg[:, kc, :], ps[:, 2 * (kc // 4), P * (kc % 4):P * (kc % 4) + P],
                       mod_a[:, 1, kc:kc + 1], mod_s[:, 1, kc:kc + 1], ALU.mult, ALU.add).then_inc(
                           hg_mod if kc % 4 == 3 else dve_job, 1)

            def gathered_low(job):
                for h in range(2):
                    dve.wait_ge(hg_high, 2 * job + h + 1)
                    TTo(hg_lo[:, 4 * h:4 * h + 4, :], hg[:, 4 * h:4 * h + 4, :],
                        hg_hi[:, 4 * h:4 * h + 4, :].bitcast(F32), ALU.subtract).then_inc(hg_ready, 1)

            def add_products(job):
                dve.wait_ge(scattered, job + 1)
                dve.wait_ge(added, 4 * job)
                for t in range(TT):
                    for h in range(2):
                        part = slice(512 * h, 512 * h + 512)
                        STT(acc[:, t, part], ps[:, (4, 5, 1, 3)[2 * t + h], :], gate_of[:, t, bass.ds(job, 1)],
                            acc[:, t, part], ALU.mult, ALU.add).then_inc(added, 1)

            choose(0)
            link(V.memset(selT[:], 0.0))
            link(V.memset(ps[:, 6:8, :], 0.0))
            V.memset(acc[:], 0.0).then_inc(zeroed, 1)
            gathered_mod(0)
            gathered_low(0)

            def dve_one(job):
                for k in range(PER_JOB):
                    n = base + k
                    for u in (2 * k, 2 * k + 1):
                        dve.wait_ge(e_high, U0 + UPJ * job + u + 1)
                        TTo(w_lo[u % SPLITS][:], ring[:, n % SLOTS, UNIT * (u % 2):UNIT * (u % 2) + UNIT],
                            w_hi[u % SPLITS][:].bitcast(F32), ALU.subtract).then_inc(e_low, 1)
                    if k == 3:
                        add_products(job)
                    g = (k - 5) // 4
                    if (k - 5) % 4 == 0 and 0 <= g < FG:
                        dve.wait_ge(e_silu, FG * job + g + 1)
                        TTo(e_act[:, 512 * g:512 * g + 512], e_sil[:], ps[:, 2 + g % 2, :], ALU.mult).then_inc(e_prod, 1)
                    g = (k - 10) // 4
                    if (k - 10) % 4 == 0 and 0 <= g < FG:
                        dve.wait_ge(eT_high, FG * job + g + 1)
                        hi = eT_hi[:, 4 * g:4 * g + 4, :].rearrange("p f n -> p (f n)").bitcast(F32)
                        TTo(eT_lo[:, 4 * g:4 * g + 4, :].rearrange("p f n -> p (f n)"), ps[:, 4 + g % 2, :], hi,
                            ALU.subtract).then_inc(eT_ready, 1)
                    if k == 31:
                        dve.wait_ge(sel_turned, job + 1)
                        choose(job + 1)
                    if k == 37:
                        gathered_mod(job + 1)
                    if k == 39:
                        gathered_low(job + 1)

            with dve.Fori(0, E) as job:
                dve_one(job)
            with dve.If(more > 0):
                with dve.Fori(E, JOBS) as job:
                    dve_one(job)
                add_products(JOBS)
                dve.wait_ge(added, 4 * (JOBS + 1))
            with dve.Else():
                add_products(E)
                dve.wait_ge(added, 4 * (E + 1))
            for t in range(TT):
                link(TTo(acc[:, t, :], acc[:, t, :], gate_f1[:], ALU.mult))
                TTo(xs[:, t, :], xs[:, t, :], acc[:, t, :], ALU.add).then_inc(x_updated, 1)
            norm(4)

        @block.tensor
        def _(pe):
            M = nc.tensor.matmul

            def mod_wide(l, cg):
                m = MODS.index((l, cg))
                if m >= 4:
                    pe.wait_ge(mod_taken, m - 1)
                for half in range(2):
                    w = chunk(pe, at_mod[l, cg] + half)
                    for k in range(4):
                        ins = M(ps[:, mod_bank(m), :], c_wide[:, 4 * half + k, :], w[:, k, :],
                                start=(half == 0 and k == 0), stop=(half == 1 and k == 3))
                ins.then_inc(mod_psum, 1)

            def mod_ones(l, cg):
                m, d = MODS.index((l, cg)), ON_DVE.index((l, cg))
                pe.wait_ge(mod_taken, m - 1)
                pe.wait_ge(mod_summed, d + 1)
                M(ps[:, mod_bank(m), :], ones, mod_acc[:, d % 2, :], start=True, stop=True).then_inc(mod_psum, 1)

            def turn(n):
                for t in range(TT):
                    pe.wait_ge(normed, 2 * n + t + 1)
                    for kc in range(KC):
                        c0 = 256 * (kc % 2) + P * t
                        ins = nc.tensor.transpose(ps[:, 2 + kc // 2, c0:c0 + P], xn[:, t, P * kc:P * kc + P], ident)
                        if kc % 2 and t == TT - 1:
                            ins.then_inc(turned, 1)

            pe.wait_ge(c_spread, 1)
            for cg in range(4):
                mod_wide(0, cg)

            pe.wait_ge(small_in, 32)
            for l in range(DEPTH):
                turn(2 * l)
                pe.wait_ge(hT_dve, 8 * l + 4)
                pe.wait_ge(hT_act, 8 * l + 4)

                def project(n):
                    kind, which = UNITS[n]
                    chunk_at, c0 = in_chunk(kind, which)
                    w = chunk(pe, at_in[l, chunk_at])
                    if 12 * l + n:
                        pe.wait_ge(proj_out, 12 * l + n)
                    for kc in range(KC):
                        if kind == "v":
                            ins = M(ps[:, 7, 0:P], hT[:, kc, CH * which:CH * which + P], w[:, kc, c0:c0 + P],
                                    start=(kc == 0), stop=(kc == KC - 1))
                        else:
                            ins = M(ps[:, 7, 0:T], w[:, kc, c0:c0 + P], hT[:, kc, :], start=(kc == 0), stop=(kc == KC - 1))
                    ins.then_inc(projected, 1)

                def drive(j):
                    pe.wait_ge(proj_out, 12 * l + UNITS.index(("u", j // 2)) + 1)
                    pe.wait_ge(matrices, l + 1)
                    if j >= 2:
                        pe.wait_ge(bu_used, 8 * l + j - 1)
                    for m, mat in ((0, b_re), (1, b_im)):
                        for q in range(2):
                            ins = M(ps[:, 2 + 2 * (j % 2) + m, T * q:T * q + T], mat[:, 2 * j + q, :], uT[:, j // 2, :],
                                    start=True, stop=True)
                    ins.then_inc(bu_psum, 1)

                def read_out(j):
                    pe.wait_ge(rotated, 8 * l + j + 1)
                    if j % 2 == 0 and j:
                        pe.wait_ge(y_skip, 4 * l + j // 2)
                    for q in range(2):
                        for mat, st in ((c_re, st_re[j % 2]), (c_im, st_im[j % 2])):
                            first = j % 2 == 0 and q == 0 and mat is c_re
                            ins = M(ps[:, 6, 0:T], mat[:, 2 * j + q, :], st[:, q, :], start=first,
                                    stop=(j % 2 == 1 and q == 1 and mat is c_im))
                    ins.then_inc(y_psum, 1)

                project(0)
                drive(0)
                project(1)
                drive(1)
                project(2)
                project(3)
                for j in range(8):
                    project(4 + j)
                    if l == 0 and j == 0:
                        mod_wide(0, 4)
                    if l == 0 and j in (2, 4, 6, 7):
                        mod_ones(0, (5, 0, 6, 0, 7, 8)[j - 2])
                    read_out(j)
                    if j + 2 < 8:
                        drive(j + 2)

                if l == 0:
                    mod_ones(0, 9)
                pe.wait_ge(proj_out, 12 * (l + 1))
                pe.wait_ge(bu_used, 8 * (l + 1))
                for t in range(TT):
                    for h in range(KVH):
                        for j in range(HPK):
                            for c in (2 * t, 2 * t + 1):
                                k0 = CH * max(c - 1, 0)
                                kn = CH if c == 0 else P
                                p0 = CH * (c % 2)
                                ins = M(ps[p0:p0 + CH, 2 + 2 * t + h, P * j:P * j + kn], qT[:, j, CH * c:CH * c + CH],
                                        kz[:, h, k0:k0 + kn], start=True, stop=True)
                    ins.then_inc(scores, 1)

                pe.wait_ge(y_gelu, 4 * (l + 1))
                pe.wait_ge(y_skip, 4 * (l + 1))
                w = chunk(pe, at_glu[l])
                for o in range(UT):
                    for k in range(UT):
                        ins = M(ps[:, 6 + o // 2, T * (o % 2):T * (o % 2) + T], w[:, k, P * o:P * o + P], yT[:, k, :],
                                start=(k == 0), stop=(k == UT - 1))
                    ins.then_inc(glu_psum, 1)

                def project_out(n, t, bank):
                    w = chunk(pe, at_out[l, n])
                    for k in range(4):
                        ins = M(ps[:, bank, :], yT[:, 4 * (n // 2) + k, P * t:P * t + P], w[:, k, :],
                                start=(k == 0), stop=(k == 3))
                    return ins

                def sum_squares(bank):
                    for t in range(TT):
                        for k in range(UT):
                            ins = M(ps[:, bank, t:t + 1], sig[:, k, P * t:P * t + P], ones[:, 0:1],
                                    start=(k == 0), stop=(k == UT - 1))
                    ins.then_inc(ss_psum, 1)

                pe.wait_ge(ssm_sq, 2 * (l + 1))
                pe.wait_ge(mod_ffn, l + 1)
                project_out(0, 0, 0)
                project_out(0, 1, 1).then_inc(out_psum, 1)

                pe.wait_ge(probs, l + 1)
                for t in range(TT):
                    for h in range(HEADS):
                        ins = nc.tensor.transpose(ps[:, 2 + 2 * t + h // 4, P * (h % 4):P * (h % 4) + P],
                                                  sc[:, t, h, :], ident)
                    ins.then_inc(probs_T, 1)
                pe.wait_ge(glu_sig, 4 * (l + 1))
                pe.wait_ge(pT_act, l + 1)
                pe.wait_ge(pT_dve, l + 1)
                for c in range(NCH):
                    window = (0, 0, 1, 2)[c]
                    for h in range(KVH):
                        o = ps[HD * h:HD * h + HD, 6 + c // 2, T * (c % 2):T * (c % 2) + T]
                        ins = M(o.rearrange("p (j n) -> p j n", j=HPK), vt[:, window, HD * h:HD * h + HD],
                                pT[:, c // 2, HPK * h:HPK * h + HPK, CH * (c % 2):CH * (c % 2) + CH],
                                start=True, stop=True)
                ins.then_inc(pv_psum, 1)

                sum_squares(4)
                project_out(1, 0, 2).then_inc(out_psum, 1)
                pe.wait_ge(attn_sq, 2 * l + 1)
                sum_squares(5)
                project_out(1, 1, 3).then_inc(out_psum, 1)
                pe.wait_ge(attn_sq, 2 * (l + 1))
                for t in range(TT):
                    if t == 0:
                        pe.wait_ge(head_var, l + 1)
                    project_out(2, t, 4 + 2 * t)
                    project_out(3, t, 5 + 2 * t).then_inc(out_psum, 1)

                turn(2 * l + 1)
                pe.wait_ge(hT_dve, 8 * l + 8)
                pe.wait_ge(hT_act, 8 * l + 8)
                if l == 0:
                    pe.wait_ge(hT_split, 1)
                    pe.sem_inc(e_free, SPLITS)
                    for g in range(GG):
                        if g >= 2:
                            pe.wait_ge(gu_out, g - 1)
                        for i in range(4):
                            pe.wait_ge(e_low, 4 * g + i + 1)
                            hi, lo = (v[i][:].rearrange("p (k n) -> p k n", k=4) for v in (w_hi, w_lo))
                            for kk in range(4):
                                kc = 4 * (i % 2) + kk
                                for f in range(2):
                                    o = ps[:, 2 + 2 * (g % 2) + i // 2, T * f:T * f + T]
                                    part = slice(P * f, P * f + P)
                                    M(o, hi[:, kk, part], hT_hi[:, kc, :], start=(kc == 0 and f == 0), stop=False,
                                      skip_group_check=True)
                                    M(o, hi[:, kk, part], hT_lo[:, kc, :], start=False, stop=False,
                                      skip_group_check=True)
                                    ins = M(o, lo[:, kk, part], hT_hi[:, kc, :], start=False, stop=(kc == KC - 1),
                                            skip_group_check=True)
                            ins.then_inc(e_free, 1)
                        if 1 <= g <= GU_MODS:
                            mod_ones(*FFN_MODS[g - 1])
                    pe.wait_ge(gu_out, GG)
                    pe.wait_ge(mod_taken, 10 + GU_MODS)
                    for n in range(FT // 2):
                        w = chunk(pe, at_down[n])
                        for t in range(TT):
                            for h in range(2):
                                for k in range(2):
                                    f = 2 * n + k
                                    ins = M(ps[:, (6, 7, 0, 1)[2 * t + h], :], a_T[:, f, P * t:P * t + P],
                                            w[:, k, 512 * h:512 * h + 512], start=(f == 0), stop=(f == FT - 1))
                            if t == TT - 1 or n == GG - 1:
                                ins.then_inc(down_psum, 1)
                        if n - 2 in DOWN_MODS:
                            mod_ones(*FFN_MODS[GU_MODS + DOWN_MODS.index(n - 2)])

            for t in range(TT):
                for kc in range(KC):
                    ins = M(ps[:, 6, E * t:E * t + E], hT[:, kc, P * t:P * t + P], w_router[:, kc, :],
                            start=(kc == 0), stop=(kc == KC - 1))
            ins.then_inc(logits, 1)
            pe.wait_ge(picked, 1)
            M(ps[:, 7, 0:E], const("before"), chosen[:, 0, 0:E], start=True, stop=True)
            M(ps[:, 7, E:2 * E], const("before"), chosen[:, 1, 0:E], start=True, stop=False)
            M(ps[:, 7, E:2 * E], ones, chosen[:, 0, 0:E], start=False, stop=True)
            M(ps[:, 7, 2 * E:3 * E], ones, chosen[:, 0, 0:E], start=True, stop=False)
            M(ps[:, 7, 2 * E:3 * E], ones, chosen[:, 1, 0:E], start=False, stop=True).then_inc(rank_psum, 1)
            pe.wait_ge(routed, 1)
            more = pe.value_load(over[0:1, 0:1], min_val=0, max_val=1)

            def gather(job):
                pe.wait_ge(sel_made, TT * (job + 1))
                for kc in range(KC):
                    for t in range(TT):
                        ins = M(ps[:, 2 * (kc // 4), P * (kc % 4):P * (kc % 4) + P], xn[:, t, P * kc:P * kc + P],
                                sel[:, t, :], start=(t == 0), stop=(t == TT - 1))
                    if kc % 4 == 3:
                        ins.then_inc(gathered, 1)

            def scatter(job):
                pe.wait_ge(y_out, 2 * (job + 1))
                for t in range(TT):
                    for h in range(2):
                        ins = M(ps[:, (4, 5, 1, 3)[2 * t + h], :], selT[:, t, :], y_sb[:, 512 * h:512 * h + 512],
                                start=True, stop=True)
                ins.then_inc(scattered, 1)

            gather(0)

            def pe_one(job):
                pe.wait_ge(hg_ready, 2 * job + 2)
                for k in range(PER_JOB):
                    if k < 4 * FG:
                        g, which, half = k // 4, k // 2 % 2, k % 2
                        bank = ps[:, 2 * which + g % 2, :]
                        if half == 0 and which == 0 and g == 1:
                            pe.wait_ge(added, 4 * (job + 1))
                        if half == 0 and which == 0 and g >= 2:
                            pe.wait_ge(e_prod, FG * job + g - 1)
                        for i in range(2):
                            u = 2 * k + i
                            hi, lo = w_hi[u % SPLITS], w_lo[u % SPLITS]
                            pe.wait_ge(e_low, U0 + UPJ * job + u + 1)
                            for kc in range(2):
                                kk = 4 * half + 2 * i + kc
                                part = slice(512 * kc, 512 * kc + 512)
                                M(bank, hg_hi[:, kk, :], hi[:, part], start=(kk == 0), stop=False)
                                M(bank, hg_lo[:, kk, :], hi[:, part], start=False, stop=False)
                                ins = M(bank, hg_hi[:, kk, :], lo[:, part], start=False, stop=(kk == KC - 1))
                            ins.then_inc(e_free, 1)
                    else:
                        for i in range(2):
                            u = 2 * k + i
                            hi, lo = w_hi[u % SPLITS], w_lo[u % SPLITS]
                            pe.wait_ge(e_low, U0 + UPJ * job + u + 1)
                            f = 2 * (k - 4 * FG) + i
                            if f % 4 == 0:
                                pe.wait_ge(eT_ready, FG * job + f // 4 + 1)
                            for h in range(2):
                                part = slice(512 * h, 512 * h + 512)
                                bank = ps[:, 6 + h, :]
                                M(bank, eT_hi[:, f, :], hi[:, part], start=(f == 0), stop=False)
                                M(bank, eT_lo[:, f, :], hi[:, part], start=False, stop=False)
                                ins = M(bank, eT_hi[:, f, :], lo[:, part], start=False, stop=(f == FE_T - 1))
                            ins.then_inc(e_free, 1)
                    if k == 1:
                        scatter(job)
                    if k == 3:
                        pe.wait_ge(sel_made, TT * (job + 1))
                        pe.wait_ge(added, 4 * job + 1)
                        for t in range(TT):
                            ins = nc.tensor.transpose(ps[:, 4, P * t:P * t + P], sel[:, t, :], ident)
                        ins.then_inc(sel_turned, 1)
                    for g in range(FG):
                        if k == (4 * g + 7 if g < FG - 1 else 30):
                            pe.wait_ge(e_prod, FG * job + g + 1)
                            if g >= 2:
                                pe.wait_ge(eT_ready, FG * job + g - 1)
                            if g == 0:
                                pe.wait_ge(selT_ready, job + 1)
                            for i in range(4):
                                f = 4 * g + i
                                ins = nc.tensor.transpose(ps[:, 4 + g % 2, P * i:P * i + P],
                                                          e_act[:, P * f:P * f + P], ident)
                            ins.then_inc(e_turned, 1)
                    if k == 34:
                        gather(job + 1)

            with pe.Fori(0, E) as job:
                pe_one(job)
            with pe.If(more > 0):
                with pe.Fori(E, JOBS) as job:
                    pe_one(job)
                scatter(JOBS)
            with pe.Else():
                scatter(E)


def kernel(x, c, norm_mix_g, norm_ffn_g, w_ada, b_ada, w_in, ssm_lam_re, ssm_lam_im,
           ssm_b_re, ssm_b_im, ssm_c_re, ssm_c_im, ssm_d, ssm_log_step, ssm_w_glu,
           attn_sinks, out_norm_ssm_g, out_norm_attn_g, w_out, ffn_w_gate, ffn_w_up,
           ffn_w_down, moe_w_router, moe_w_gate, moe_w_up, moe_w_down, final_norm_g):
    import numpy as np
    import concourse.bacc as bacc
    from concourse.bass_utils import run_bass_kernel_spmd

    f = lambda a: np.ascontiguousarray(np.asarray(a))
    cols = lambda v: np.asarray(v).reshape(-1, P).T
    order = np.arange(HEADS).reshape(KVH, HPK).T.reshape(-1)
    by_head = (order[:, None] * HD + np.arange(HD)[None, :]).reshape(-1)
    w_in, w_out = np.array(w_in), np.array(w_out)
    w_in[:, :, D_SSM:D_SSM + 512] = w_in[:, :, D_SSM + by_head]
    w_out[:, D_SSM:] = w_out[:, D_SSM + by_head]
    states = lambda v: np.asarray(v).reshape(PAIRS, P).T

    layer = lambda make: np.stack([make(l) for l in range(DEPTH)])
    prm = np.concatenate([
        layer(lambda l: cols(b_ada[l])), layer(lambda l: cols(norm_mix_g[l])), layer(lambda l: cols(norm_ffn_g[l])),
        layer(lambda l: states(ssm_lam_re[l])), layer(lambda l: states(ssm_lam_im[l])),
        layer(lambda l: states(np.repeat(np.asarray(ssm_log_step[l]), STATE))),
        layer(lambda l: cols(ssm_d[l])), layer(lambda l: cols(out_norm_ssm_g[l])),
        layer(lambda l: cols(np.asarray(out_norm_attn_g[l])[by_head])),
        layer(lambda l: np.broadcast_to(np.asarray(attn_sinks[l]), (P, HEADS))),
    ], axis=2).transpose(1, 0, 2)
    b_lay = lambda v: np.asarray(v).transpose(0, 2, 1).reshape(UT, P, STATE).transpose(1, 0, 2).reshape(P, -1)
    c_lay = lambda v: np.asarray(v).transpose(0, 2, 1).reshape(PAIRS, P, GROUP).transpose(1, 0, 2).reshape(P, -1)
    bc = np.stack([np.stack([b_lay(ssm_b_re[l]), b_lay(ssm_b_im[l]), c_lay(ssm_c_re[l]), c_lay(ssm_c_im[l])], 1)
                   for l in range(DEPTH)])
    small = np.concatenate([cols(c[0]), np.asarray(moe_w_router[0]).reshape(KC, P, E).transpose(1, 0, 2).reshape(P, -1)], 1)

    i = np.arange(P)
    cst = np.concatenate([
        np.eye(P), i[:, None] < i[None, :], np.ones((P, P)), np.broadcast_to(i, (P, P)),
        i[:, None] // GROUP == np.arange(GT)[None, :],
        (2 * np.arange(4)[None, :, None] + i[:, None, None] // STATE == np.arange(GT)).reshape(P, -1),
    ], axis=1).astype(np.float32)

    nc = bacc.Bacc("TRN2", target_bir_lowering=False, num_devices=1)
    arrays, args = {}, []
    for name, a in (("x", x), ("small", small), ("prm", prm), ("bc", bc), ("cst", cst), ("w_ada", w_ada),
                    ("b_ada", b_ada), ("w_in", w_in), ("w_glu", ssm_w_glu), ("w_out", w_out),
                    ("w_gate", ffn_w_gate), ("w_up", ffn_w_up), ("w_down", ffn_w_down), ("moe_gate", moe_w_gate),
                    ("moe_up", moe_w_up), ("moe_down", moe_w_down), ("final_g", final_norm_g)):
        arrays[name + "_dram"] = f(a)
        args.append(nc.dram_tensor(name + "_dram", arrays[name + "_dram"].shape, F32, kind="ExternalInput").ap())
    args.append(nc.dram_tensor("out_dram", (1, T, D), F32, kind="ExternalOutput").ap())
    build(nc, *args)
    r = run_bass_kernel_spmd(nc, [arrays], core_ids=[0])
    return r.results[0]["out_dram"]
```

```python
import math
from contextlib import ExitStack

import concourse.bass as bass
from concourse import mybir

F32 = mybir.dt.float32
F32R = mybir.dt.float32r
I32 = mybir.dt.int32
ALU = mybir.AluOpType
ACT = mybir.ActivationFunctionType
AX = mybir.AxisListType.X

P = 128
D = 1024
KC = D // P
T = 256
TT = T // P
DEPTH = 2
D_SSM, GROUP, STATE = 512, 16, 64
UT = D_SSM // P
PAIRS = (D_SSM // GROUP) * STATE // P
GT = P // GROUP
HD, HEADS, KVH = 64, 8, 2
HPK = HEADS // KVH
CH = 64
NCH = T // CH
D_FF = 2816
FT = D_FF // P
E, F_E = 8, 3584
FE_T = F_E // P
FG = F_E // 512
CAP = P
JOBS = E * (T // CAP)
EPS = 1e-6
NEG = -1e30
TWO_PI_HI = 6.28125
TWO_PI_MID = math.floor((2 * math.pi - TWO_PI_HI) * 2 ** 21) / 2 ** 21
TWO_PI_LO = 2 * math.pi - TWO_PI_HI - TWO_PI_MID
ROUND = 1.5 * 2.0 ** 23

SLOTS = 7
UNIT = 1024
SPLITS = 4
PER_JOB = 4 * FG + FE_T // 2
UPJ = 2 * PER_JOB

PRM = {}
_at = 0
for _name, _n in (("b_ada", 48), ("g_mix", 8), ("g_ffn", 8), ("lam_re", PAIRS), ("lam_im", PAIRS),
                  ("log_step", PAIRS), ("d_skip", UT), ("g_ssm", UT), ("g_attn", UT), ("sinks", HEADS)):
    PRM[_name] = (_at, _at + _n)
    _at += _n
N_PRM = _at
CST = {}
_at = 0
for _name, _n in (("ident", P), ("before", P), ("ones", P), ("iota", P), ("mask_ch", GT), ("mask_st", 4 * GT)):
    CST[_name] = (_at, _at + _n)
    _at += _n
N_CST = _at
SH_M, SC_M, G_M, SH_F, SC_F, G_F = range(6)


def build(nc, x, small, prm, bc, cst, w_ada, b_ada, w_in, w_glu, w_out, w_gate, w_up, w_down,
          moe_gate, moe_up, moe_down, final_g, out):
    with ExitStack() as ctx:
        sem = lambda name: ctx.enter_context(nc.semaphore(name))
        at = [(nc.sbuf_base + 63) // 64 * 64]

        def place(name, shape, dt=F32, offset=None):
            size = 4
            for n in shape[1:]:
                size *= n
            if offset is None:
                offset = at[0]
                at[0] += (size + 63) // 64 * 64
            return nc.alloc_sbuf_tensor_at(name, shape, dt, offset=offset)

        def region(nbytes):
            start = at[0]
            at[0] += nbytes
            return start

        ring = place("ring", [P, SLOTS, 2048])
        r_split = region(4 * 8192)
        r_tab = region(32768)
        r_blk = region(32768)
        xs = place("xs", [P, TT, D])
        xn = place("xn", [P, TT, D])
        r_hT = region(8192)
        hT = place("hT", [P, KC, T], offset=r_hT)
        gate_m = place("gate_m", [P, D])
        gate_f = place("gate_f", [P, D])
        k_st = place("k_st", [P, N_CST])
        prms = place("prms", [P, DEPTH, N_PRM])
        smalls = place("smalls", [P, KC + KC * E])
        c_act = place("c_act", [P, KC])
        r_wide = region(4096)
        c_wide = place("c_wide", [P, KC, P], offset=r_wide)
        gate_f1 = place("gate_f1", [P, D], offset=r_wide)
        mod_raw = place("mod_raw", [P, 6 * KC])
        mod_a = place("mod_a", [P, 2, KC])
        mod_s = place("mod_s", [P, 2, KC])
        sq_sum = place("sq_sum", [P, TT])
        rstd = place("rstd", [P, TT])
        head_ss = place("head_ss", [P, 4])
        head_rs = place("head_rs", [P, 4])
        sv = {n: place("sv_" + n, [P, DEPTH, PAIRS]) for n in
              ("step", "dec", "cr", "ci", "t1", "t2", "t3")}
        pw_c = place("pw_c", [P, 8, DEPTH, PAIRS])
        pw_s = place("pw_s", [P, 8, DEPTH, PAIRS])
        sinks_e = place("sinks_e", [P, TT, HEADS])
        s_max = place("s_max", [P, TT, HEADS])
        s_den = place("s_den", [P, TT, HEADS])
        yT = place("yT", [P, 2 * UT, T], offset=r_split)
        uT = place("uT", [P, UT, T], offset=r_split + 8192)
        sig = place("sig", [P, UT, T], offset=r_split + 8192)
        qT = place("qT", [P, HPK, T], offset=r_split + 12288)
        kz = place("kz", [P, KVH, T], offset=r_split + 16384)
        vt = place("vt", [P, 3, P], offset=r_split + 18432)
        rot_a = place("rot_a", [P, 2, T], offset=r_split + 20480)
        rot_b = place("rot_b", [P, 2, T], offset=r_split + 22528)
        st_t = [place("st_t0", [P, 2, T], offset=r_split + 28672), place("st_t1", [P, 2, T])]
        bcs = place("bcs", [P, 4, 256], offset=r_hT)
        resid = place("resid", [P, 2, 512], offset=r_split + 20480)
        tab_s = place("tab_s", [P, PAIRS, P], offset=r_split + 24576)
        tab_t = [place("tab_t0", [P, PAIRS, P], offset=r_split), xn[:].rearrange("p t (q n) -> p (t q) n", n=P)]
        cos_t = place("cos_t", [P, PAIRS, T], offset=r_tab)
        sin_t = place("sin_t", [P, PAIRS, T], offset=r_tab + 16384)
        b_re = place("b_re", [P, PAIRS, P], offset=r_blk)
        b_im = place("b_im", [P, PAIRS, P], offset=r_blk + 8192)
        c_re = place("c_re", [P, PAIRS, P], offset=r_blk + 16384)
        c_im = place("c_im", [P, PAIRS, P], offset=r_blk + 24576)
        z = xn[:, :, :].rearrange("p t (c n) -> p (t c) n", n=512)
        z_re = [z[:, 2 * b, :].rearrange("p (q n) -> p q n", q=2) for b in range(2)]
        z_im = [z[:, 2 * b + 1, :].rearrange("p (q n) -> p q n", q=2) for b in range(2)]
        sc = xn[:, :, :].rearrange("p t (h n) -> p t h n", h=HEADS)
        pT = place("pT", [P, TT, HEADS, P], offset=r_hT)
        a_T = place("a_T", [P, FT, T], offset=r_blk)
        hT_hi = place("hT_hi", [P, KC, T], F32R, offset=r_blk + FT * T * 4)
        a_hi = place("a_hi", [P, 2, 2, T], F32R, offset=r_blk + FT * T * 4)
        a_lo = place("a_lo", [P, 2, 2, T], F32R, offset=r_blk + FT * T * 4 + 4096)
        hT_lo = place("hT_lo", [P, KC, T], F32R, offset=r_hT)
        sil = place("sil", [P, 2 * T], offset=r_blk + FT * T * 4 + 8192)
        w_hi = [place(f"w_hi{i}", [P, UNIT], F32R, offset=r_split + 8192 * i) for i in range(SPLITS)]
        w_lo = [place(f"w_lo{i}", [P, UNIT], F32R, offset=r_split + 8192 * i + 4096) for i in range(SPLITS)]
        e_act = place("e_act", [P, F_E], offset=r_tab)
        eT_hi = place("eT_hi", [P, FE_T, P], F32R, offset=r_tab + 14336)
        eT_lo = place("eT_lo", [P, FE_T, P], F32R, offset=r_tab + 28672)
        hg = place("hg", [P, KC, P], offset=r_tab + 43008)
        hg_hi = place("hg_hi", [P, KC, P], F32R, offset=r_tab + 47104)
        hg_lo = place("hg_lo", [P, KC, P], F32R, offset=r_tab + 51200)
        y_sb = place("y_sb", [P, D], offset=r_tab + 55296)
        e_sil = place("e_sil", [P, 512], offset=r_tab + 59392)
        sel = place("sel", [P, TT, CAP], offset=r_tab + 61440)
        selT = place("selT", [P, TT, P], offset=r_tab + 62464)
        r_acc = region(8192)
        st_re = [place(f"st_re{i}", [P, 2, T], offset=(r_split + 24576, r_split + 30720)[i]) for i in range(2)]
        st_im = [place(f"st_im{i}", [P, 2, T], offset=(r_split + 26624, r_acc + 6144)[i]) for i in range(2)]
        acc = place("acc", [P, TT, D], offset=r_acc)
        mod_acc = place("mod_acc", [P, 3, 512], offset=r_acc)
        mod_diag = place("mod_diag", [P, 4, P], offset=r_acc + 4096)
        lg = place("lg", [P, TT, E])
        top = place("top", [P, TT, 8])
        idx = place("idx", [P, TT, 8], mybir.dt.uint32)
        idx_f = place("idx_f", [P, TT, 8])
        g1 = place("g1", [P, TT])
        g2 = place("g2", [P, TT])
        oh1 = place("oh1", [P, TT, E])
        oh2 = place("oh2", [P, TT, E])
        chosen = place("chosen", [P, TT, JOBS + 1])
        rank = place("rank", [P, TT, JOBS + 1])
        gate_of = place("gate_of", [P, TT, JOBS + 1])
        over_f = place("over_f", [P, 1])
        over = place("over", [P, 1], I32)
        assert at[0] <= nc.sbuf_usable_end, at[0]

        ps = ctx.enter_context(nc.psum_tensor("ps", [P, 8, 512], F32))

        Y_BANK = (6, 1)

        def mod_bank(m):
            if m < 10:
                return (0, 1, 6, 7)[m] if m < 4 else 0
            return m % 2 if m < 10 + len(GU_MODS) else 2 + m % 2

        def const(name):
            a, b = CST[name]
            return k_st[:, a:b]

        def par(l, name):
            a, b = PRM[name]
            return prms[:, l, a:b]

        ident, ones = const("ident"), const("ones")
        mask_ch = const("mask_ch")
        mask_st = const("mask_st").rearrange("p (a g) -> p a g", g=GT)
        c_col = smalls[:, 0:KC]
        w_router = smalls[:, KC:KC + KC * E].rearrange("p (k e) -> p k e", e=E)

        loaded = [sem(f"slot{i}_loaded") for i in range(SLOTS)]
        c_in, params_in, const_in, x_in, bc_in, gbias_in, fg_in, stored = (
            sem(n) for n in ("c_in", "params_in", "const_in", "x_in", "bc_in", "gbias_in", "fg_in", "stored"))
        c_silu, c_spread = sem("c_silu"), sem("c_spread")
        mod_psum, mod_taken, mod_summed, mod_mix, mod_ffn = (
            sem(n) for n in ("mod_psum", "mod_taken", "mod_summed", "mod_mix", "mod_ffn"))
        x_updated, squares, variance, deviation, normed = (
            sem(n) for n in ("x_updated", "squares", "variance", "deviation", "normed"))
        turned, hT_dve, hT_act = sem("turned"), sem("hT_dve"), sem("hT_act")
        projected, proj_out = sem("projected"), sem("proj_out")
        sv_step, sv_angle, sv_trig, sv_ready = (sem(n) for n in ("sv_step", "sv_angle", "sv_trig", "sv_ready"))
        table0, table0_sin, table0_cos, table1 = (sem(n) for n in ("table0", "table0_sin", "table0_cos", "table1"))
        bcs_read, matrices, bu_psum, bu_used, scanned, rotated = (
            sem(n) for n in ("bcs_read", "matrices", "bu_psum", "bu_used", "scanned", "rotated"))
        y_psum, y_skip, y_gelu = sem("y_psum"), sem("y_skip"), sem("y_gelu")
        glu_psum, glu_sig, ssm_sq, attn_sq, ss_psum = (
            sem(n) for n in ("glu_psum", "glu_sig", "ssm_sq", "attn_sq", "ss_psum"))
        kz_zero = sem("kz_zero")
        scores, shifted, exps, probs, probs_T, pT_act, pv_psum = (
            sem(n) for n in ("scores", "shifted", "exps", "probs", "probs_T", "pT_act", "pv_psum"))
        head_var, head_dev, head_ready = sem("head_var"), sem("head_dev"), sem("head_ready")
        out_psum, hT_high, hT_split, gu_silu, gu_out, a_high, a_split, down_psum = (
            sem(n) for n in ("out_psum", "hT_high", "hT_split", "gu_silu", "gu_out", "a_high", "a_split", "down_psum"))
        logits, diff, diff_e, picked, rank_psum, routed = (
            sem(n) for n in ("logits", "diff", "diff_e", "picked", "rank_psum", "routed"))
        e_high, e_low, e_free = sem("e_high"), sem("e_low"), sem("e_free")
        e_silu, e_prod, e_turned, eT_high, eT_ready = (
            sem(n) for n in ("e_silu", "e_prod", "e_turned", "eT_high", "eT_ready"))
        sel_made, sel_turned, selT_ready, gathered, hg_mod, hg_high, hg_ready = (
            sem(n) for n in ("sel_made", "sel_turned", "selT_ready", "gathered", "hg_mod", "hg_high", "hg_ready"))
        zeroed, y_out, scattered, last_scattered, added = (
            sem(n) for n in ("zeroed", "y_out", "scattered", "last_scattered", "added"))
        dve_step, dve_job, act_step, pool_step = (
            sem(n) for n in ("dve_step", "dve_job", "act_step", "pool_step"))

        def chain(eng, s):
            done = [0]

            def link(ins):
                done[0] += 1
                ins.then_inc(s, 1)
                eng.wait_ge(s, done[0])
            return link

        stream = []

        def cols(w, k0, kn, c0, cn):
            return w.rearrange("(k p) n -> p k n", p=P)[:, k0:k0 + kn, c0:c0 + cn]

        ON_DVE = [(0, cg) for cg in range(5, 12)] + [(1, cg) for cg in range(12)]
        MODS = [(0, cg) for cg in range(12)] + [(1, cg) for cg in range(12)]

        def of_dve(l, cg):
            return KC - 2 if l == 0 and cg < 10 else KC

        def stream_mod(l, cg):
            for half in range(2):
                if (l, cg) in ON_DVE and (half == 0 or of_dve(l, cg) == KC):
                    used = (mod_summed, ON_DVE.index((l, cg)) + 1)
                else:
                    used = (mod_psum, MODS.index((l, cg)) + 1)
                stream.append((cols(w_ada[l], 4 * half, 4, 512 * cg, 512), (4, 512), used))
            at_mod[l, cg] = len(stream) - 2

        UNITS = [("u", 0), ("u", 1), ("u", 2), ("u", 3), ("q", 0), ("q", 1), ("q", 2), ("q", 3),
                 ("v", 0), ("k", 0), ("v", 1), ("v", 2)]

        def in_chunk(kind, which):
            c = {"u": 0, "q": 4, "k": 8, "v": 9}[kind] + (0 if kind == "v" else which)
            return c // 2, P * (c % 2)

        FFN_MODS = MODS[10:]
        GG = FT // 2
        GU_MODS = (0, 1, 2, 3, 5, 6, 7, 8)
        DOWN_MODS = (0, 1, 3, 4, 6, 7)
        at_mod, at_in, at_glu, at_out, at_gu, at_down = {}, {}, {}, {}, {}, {}
        for l in range(DEPTH):
            if l == 0:
                for cg in range(4):
                    stream_mod(0, cg)
            for i in range(5):
                at_in[l, i] = len(stream)
                last = max(n for n, (kind, which) in enumerate(UNITS) if in_chunk(kind, which)[0] == i)
                stream.append((cols(w_in[l], 0, KC, 256 * i, 256), (KC, 256), (projected, 12 * l + last + 1)))
                if l == 0:
                    for cg in ((), (4, 5), (6,), (7,), (8, 9))[i]:
                        stream_mod(0, cg)
            at_glu[l] = len(stream)
            stream.append((cols(w_glu[l], 0, UT, 0, D_SSM), (UT, D_SSM), (glu_psum, 4 * l + 4)))
            for n in range(4):
                at_out[l, n] = len(stream)
                stream.append((cols(w_out[l], 4 * (n // 2), 4, 512 * (n % 2), 512), (4, 512),
                               (out_psum, 5 * l + (1, 3, 5, 5)[n])))
            if l == 0:
                for g in range(GG):
                    at_gu[g] = len(stream)
                    for i, w in enumerate((w_gate, w_up)):
                        stream.append((cols(w[0], 0, KC, 256 * g, 256), (KC, 256), (e_low, 4 * g + 2 * i + 2)))
                    if g in GU_MODS:
                        stream_mod(*FFN_MODS[GU_MODS.index(g)])
                for n in range(GG):
                    at_down[n] = len(stream)
                    stream.append((cols(w_down[0], 2 * n, 2, 0, D), (2, D), (e_low, 4 * GG + 2 * n + 2)))
                    if n in DOWN_MODS:
                        stream_mod(*FFN_MODS[len(GU_MODS) + DOWN_MODS.index(n)])
        U0 = 6 * GG
        base = len(stream)

        def slot(n, shape):
            return ring[:, n % SLOTS, :].rearrange("p (a b) -> p a b", a=shape[0])

        def chunk(eng, n):
            eng.wait_ge(loaded[n % SLOTS], 16 * (n // SLOTS + 1))
            return slot(n, stream[n][1])

        assert PER_JOB % SLOTS == 0 and UPJ % SPLITS == 0 and 4 * GG % SPLITS == 0 and len(FFN_MODS) == len(GU_MODS) + len(DOWN_MODS)
        turns = PER_JOB // SLOTS

        def loaded_by(job, k):
            return 16 * ((base + k) // SLOTS + 1) + 16 * turns * job

        block = ctx.enter_context(nc.Block())

        @block.sync
        def _(sp):
            sp.dma_start(smalls[:], small).then_inc(c_in, 16)

            def load(n):
                src, shape, _ = stream[n]
                if n >= SLOTS:
                    s, v = stream[n - SLOTS][2]
                    sp.wait_ge(s, v)
                sp.dma_start(slot(n, shape), src).then_inc(loaded[n % SLOTS], 16)

            for n in range(base):
                load(n)
                if n == 3:
                    sp.dma_start(xs[:], x[0].rearrange("(t p) d -> p t d", p=P)).then_inc(x_in, 16)

            def load_job(job, expert, first=False):
                def expert_cols(w, k0, kn, c0, cn):
                    return w[bass.ds(expert, 1)].rearrange("a (k p) n -> p (a k) n", p=P)[:, k0:k0 + kn, c0:c0 + cn]
                for k in range(PER_JOB):
                    if k < 4 * FG:
                        w = (moe_gate, moe_up)[k // 2 % 2][0]
                        src, shape = expert_cols(w, 4 * (k % 2), 4, 512 * (k // 4), 512), (4, 512)
                    else:
                        src, shape = expert_cols(moe_down[0], 2 * (k - 4 * FG), 2, 0, D), (2, D)
                    if first and k < SLOTS:
                        sp.wait_ge(*stream[base + k - SLOTS][2])
                    else:
                        sp.wait_ge(e_low, U0 + UPJ * job + 2 * (k - SLOTS + 1))
                    sp.dma_start(slot(base + k, shape), src).then_inc(loaded[(base + k) % SLOTS], 16)

            load_job(0, 0, first=True)
            with sp.Fori(1, E) as job:
                load_job(job, job)
            sp.wait_ge(routed, 1)
            more = sp.value_load(over[0:1, 0:1], min_val=0, max_val=1)
            with sp.If(more > 0):
                with sp.Fori(E, JOBS) as job:
                    load_job(job, job - E)
            with sp.Else():
                sp.nop()
            for t in range(TT):
                sp.wait_ge(normed, 2 * 4 + t + 1)
                sp.dma_start(out[0, P * t:P * t + P, :], xn[:, t, :]).then_inc(stored, 16)
            sp.wait_ge(stored, 16 * TT)

        def double(ops, l, m, part, link, tmp):
            n = 1 << m
            wide = lambda v: v[:, m, l, :].unsqueeze(2).to_broadcast([P, PAIRS, n])
            cl, sl = wide(pw_c), wide(pw_s)
            c0, s0 = cos_t[:, :, 0:n], sin_t[:, :, 0:n]
            tt = tmp[:, :, 0:n]
            if part == "cos":
                new, a, b, join = cos_t[:, :, n:2 * n], c0, s0, ALU.subtract
            else:
                new, a, b, join = sin_t[:, :, n:2 * n], s0, c0, ALU.add
            ops.tensor_tensor(new, a, cl, ALU.mult)
            link(ops.tensor_tensor(tt, b, sl, ALU.mult))
            return ops.tensor_tensor(new, new, tt, join)

        def first_columns(ops, l, link, levels, tmp):
            if 0 in levels:
                ops.memset(cos_t[:, :, 0:1], 1.0)
                link(ops.memset(sin_t[:, :, 0:1], 0.0))
            for m in levels:
                link(double(ops, l, m, "cos", link, tmp))
                ins = double(ops, l, m, "sin", link, tmp)
                if m < levels[-1]:
                    link(ins)
            return ins

        @block.gpsimd
        def _(pool):
            link = chain(pool, pool_step)

            def load_params(l):
                if l:
                    pool.wait_ge(e_free, SPLITS + 4 * GG)
                pool.dma_start(bcs[:], bc[l]).then_inc(bc_in, 16)

            def load_gate(dst, src, s):
                pool.dma_start(dst[:], src.partition_broadcast(P)).then_inc(s, 16)

            def make_matrices(l):
                pool.wait_ge(bc_in, 16 * (l + 1))
                pool.wait_ge(const_in, 16)
                pool.wait_ge(sv_ready, 1)
                cre, cim = (bcs[:, m, :].rearrange("p (q h) -> p q h", h=GROUP) for m in (2, 3))
                t0, t1 = (st_t[1][:, m, :].rearrange("p (q h) -> p q h", h=GROUP) for m in (0, 1))
                kr, ki, nkr, nki = (sv[n][:, l, :].unsqueeze(2).to_broadcast([P, PAIRS, GROUP])
                                    for n in ("cr", "ci", "t1", "t2"))
                nc.gpsimd.tensor_tensor(t0, cre, kr, ALU.mult)
                link(nc.gpsimd.tensor_tensor(t1, cim, ki, ALU.mult))
                nc.gpsimd.tensor_tensor(t0, t0, t1, ALU.subtract)
                nc.gpsimd.tensor_tensor(cre, cre, nki, ALU.mult)
                link(nc.gpsimd.tensor_tensor(cim, cim, nkr, ALU.mult))
                link(nc.gpsimd.tensor_tensor(t1, cre, cim, ALU.add))
                for m, dst in ((0, b_re), (1, b_im)):
                    if l:
                        pool.wait_ge(a_split, 4 * m + 4)
                    o = dst[:].rearrange("p (u q) (b s) -> p u (q b) s", u=UT, b=2)
                    v = bcs[:, m, :].rearrange("p (u s) -> p u s", u=UT)
                    ins = nc.gpsimd.tensor_tensor(o, v.unsqueeze(2).to_broadcast([P, UT, GT, STATE]),
                                                  mask_ch.unsqueeze(1).unsqueeze(3).to_broadcast([P, UT, GT, STATE]),
                                                  ALU.mult)
                ins.then_inc(bcs_read, 1)
                if l:
                    pool.wait_ge(e_free, U0 + SPLITS)
                for v, dst in ((t0, c_re), (t1, c_im)):
                    for u in range(UT):
                        o = dst[:, 4 * u:4 * u + 4, :].rearrange("p q (g h) -> p q g h", h=GROUP)
                        ins = nc.gpsimd.tensor_tensor(
                            o, v[:, 4 * u:4 * u + 4, :].unsqueeze(2).to_broadcast([P, 4, GT, GROUP]),
                            mask_st.unsqueeze(3).to_broadcast([P, 4, GT, GROUP]), ALU.mult)
                ins.then_inc(matrices, 1)

            def turn_back(l, j):
                pool.wait_ge(scanned, 8 * l + j + 1)
                if 8 * l + j >= 2:
                    pool.wait_ge(y_psum, 8 * l + j - 1)
                if j == 0:
                    pool.wait_ge(matrices, l + 1)
                q0 = 2 * j
                zr, zi = z_re[j % 2], z_im[j % 2]
                cs, sn = cos_t[:, q0:q0 + 2, :], sin_t[:, q0:q0 + 2, :]
                re, im = st_re[j % 2][:], st_im[j % 2][:]
                nc.gpsimd.tensor_tensor(re, zr, cs, ALU.mult)
                link(nc.gpsimd.tensor_tensor(im, zi, sn, ALU.mult))
                link(nc.gpsimd.tensor_tensor(re, re, im, ALU.subtract))
                ins = nc.gpsimd.tensor_tensor(im, zr, sn, ALU.mult)
                if l == 0:
                    ins = nc.gpsimd.tensor_tensor(st_t[j % 2][:], zi, cs, ALU.mult)
                link(ins)
                nc.gpsimd.tensor_tensor(im, im, st_t[j % 2][:], ALU.add).then_inc(rotated, 1)

            pool.wait_ge(params_in, 16)
            load_params(0)
            nc.gpsimd.memset(kz[:], 0.0).then_inc(kz_zero, 1)
            make_matrices(0)
            load_gate(gate_m, b_ada[0, G_M * D:(G_M + 1) * D], gbias_in)
            load_gate(gate_f, b_ada[0, G_F * D:(G_F + 1) * D], gbias_in)
            pool.wait_ge(table0, 1)
            pool.wait_ge(matrices, 1)
            double(nc.gpsimd, 0, 7, "sin", link, tab_s).then_inc(table0_sin, 1)
            pool.wait_ge(table0_sin, 1)
            for j in range(8):
                turn_back(0, j)
            pool.wait_ge(x_updated, 2)
            pool.wait_ge(gbias_in, 32)
            load_gate(gate_m, b_ada[1, G_M * D:(G_M + 1) * D], gbias_in)
            pool.wait_ge(bu_used, 8)
            pool.wait_ge(out_psum, 5)
            pool.wait_ge(mod_psum, 9)
            pool.wait_ge(gbias_in, 48)
            load_gate(gate_f1, b_ada[1, G_F * D:(G_F + 1) * D], gbias_in)
            pool.wait_ge(turned, 8)
            first_columns(nc.gpsimd, 1, link, range(8), tab_t[1]).then_inc(table1, 1)
            load_params(1)
            make_matrices(1)
            nc.gpsimd.memset(kz[:], 0.0).then_inc(kz_zero, 1)
            for j in range(8):
                turn_back(1, j)
            pool.wait_ge(x_updated, 6)
            load_gate(gate_m, final_g, fg_in)

        @block.scalar
        def _(act):
            link = chain(act, act_step)
            A = nc.scalar.activation

            def norm(n):
                for t in range(TT):
                    act.wait_ge(x_updated, 2 * (n - 1) + t + 1) if n else act.wait_ge(x_in, 16)
                    if n == 2:
                        act.wait_ge(table1, 1)
                    A(xn[:, t, :], xs[:, t, :], ACT.Square, accum_out=sq_sum[:, t:t + 1]).then_inc(squares, 1)
                    act.wait_ge(variance, 2 * n + t + 1)
                    A(rstd[:, t:t + 1], rstd[:, t:t + 1], ACT.Sqrt).then_inc(deviation, 1)

            def modulate(n):
                which = n % 2
                act.wait_ge((mod_mix, mod_ffn)[which], n // 2 + 1)
                act.wait_ge(turned, 4 * (n + 1))
                if which == 0:
                    act.wait_ge(bcs_read, n // 2 + 1)
                for kc in range(4, KC):
                    A(hT[:, kc, :], ps[:, 2 + kc // 2, 256 * (kc % 2):256 * (kc % 2) + 256], ACT.Identity,
                      bias=mod_s[:, which, kc:kc + 1], scale=mod_a[:, which, kc:kc + 1]).then_inc(hT_act, 1)

            act.dma_start(prms[:], prm).then_inc(params_in, 16)
            act.dma_start(k_st[:], cst).then_inc(const_in, 16)
            act.wait_ge(c_in, 16)
            A(c_act[:], c_col, ACT.Silu).then_inc(c_silu, 1)
            act.wait_ge(params_in, 16)
            a, b = PRM["log_step"]
            A(sv["step"][:], prms[:, :, a:b], ACT.Exp).then_inc(sv_step, 1)
            act.wait_ge(sv_angle, 1)
            A(sv["dec"][:], sv["dec"][:], ACT.Exp)
            A(pw_s[:], pw_c[:], ACT.Sin)
            A(pw_c[:], pw_c[:], ACT.Sin, scale=0.5).then_inc(sv_trig, 1)
            norm(0)

            for l in range(DEPTH):
                if l:
                    norm(2)
                modulate(2 * l)
                def gelu(u):
                    act.wait_ge(y_skip, 4 * l + u + 1)
                    A(yT[:, u, :], yT[:, u, :], ACT.Gelu_apprx_tanh).then_inc(y_gelu, 1)

                for n, (kind, which) in enumerate(UNITS):
                    act.wait_ge(projected, 12 * l + n + 1)
                    if kind == "u":
                        nc.scalar.copy(uT[:, which, :], ps[:, 7, 0:T]).then_inc(proj_out, 1)
                    elif kind == "q":
                        nc.scalar.mul(qT[:, which, :], ps[:, 7, 0:T], HD ** -0.5).then_inc(proj_out, 1)
                    elif kind == "k":
                        act.wait_ge(kz_zero, l + 1)
                        link(nc.scalar.copy(kz[0:HD, 0, :], ps[0:HD, 7, 0:T]))
                        nc.scalar.copy(kz[HD:P, 1, :], ps[HD:P, 7, 0:T]).then_inc(proj_out, 1)
                    else:
                        nc.scalar.copy(vt[:, which, :], ps[:, 7, 0:P]).then_inc(proj_out, 1)
                    if n in (8, 10):
                        gelu(n // 2 - 4)
                gelu(2)
                gelu(3)
                for t in range(TT):
                    act.wait_ge(shifted, 2 * l + t + 1)
                    A(sc[:, t], sc[:, t], ACT.Exp).then_inc(exps, 1)
                A(sinks_e[:], sinks_e[:], ACT.Exp).then_inc(exps, 1)
                for o in range(UT):
                    act.wait_ge(glu_psum, 4 * l + o // 2 * 2 + 2)
                    if o == 0:
                        act.wait_ge(y_skip, 4 * l + 4)
                    A(sig[:, o, :], ps[:, 6 + o // 2, 256 * (o % 2):256 * (o % 2) + 256],
                      ACT.Sigmoid).then_inc(glu_sig, 1)
                for t in range(TT):
                    act.wait_ge(probs_T, 2 * l + t + 1)
                    nc.scalar.copy(pT[:, t, :, :].rearrange("p h n -> p (h n)"),
                                   ps[:, 2 + 2 * t:4 + 2 * t, :].rearrange("p b n -> p (b n)")).then_inc(pT_act, 1)
                act.wait_ge(head_var, l + 1)
                A(head_rs[:], head_ss[:], ACT.Sqrt).then_inc(head_dev, 1)
                norm(2 * l + 1)
                if l == 0:
                    def high(g, i):
                        src = chunk(act, at_gu[g] + i // 2)
                        act.wait_ge(e_free, 4 * g + i + 1)
                        nc.scalar.copy(w_hi[i][:], src[:, 4 * (i % 2):4 * (i % 2) + 4, :]).then_inc(e_high, 1)

                    high(0, 0)
                    high(0, 1)
                modulate(2 * l + 1)
                if l == 0:
                    for half, done in ((0, hT_dve), (1, hT_act)):
                        act.wait_ge(done, 8)
                        nc.scalar.copy(hT_hi[:, 4 * half:4 * half + 4, :],
                                       hT[:, 4 * half:4 * half + 4, :]).then_inc(hT_high, 1)

                    def silu(g):
                        act.wait_ge(e_free, SPLITS + 4 * (g + 1))
                        if g:
                            act.wait_ge(gu_out, g)
                        A(sil[:], ps[:, 2 + 2 * (g % 2), :], ACT.Silu).then_inc(gu_silu, 1)

                    for g in range(GG):
                        for i in range(4):
                            if g or i >= 2:
                                high(g, i)
                        if g:
                            silu(g - 1)

                    def high_down(n):
                        src = chunk(act, at_down[n])
                        for i in range(2):
                            u = 4 * GG + 2 * n + i
                            act.wait_ge(e_free, u + 1)
                            nc.scalar.copy(w_hi[u % SPLITS][:], src[:, i, :]).then_inc(e_high, 1)

                    high_down(0)
                    silu(GG - 1)
                    for n in range(GG):
                        if n:
                            high_down(n)
                        act.wait_ge(gu_out, GG if n == 0 else n + 1)
                        if n >= 2:
                            act.wait_ge(e_free, SPLITS + 4 * GG + 2 * n - 2)
                        nc.scalar.copy(a_hi[:, n % 2], a_T[:, 2 * n:2 * n + 2, :]).then_inc(a_high, 1)

            act.wait_ge(diff, 1)
            A(g2[:], g2[:], ACT.Exp).then_inc(diff_e, 1)
            act.wait_ge(routed, 1)
            more = act.value_load(over[0:1, 0:1], min_val=0, max_val=1)

            def gathered_high(job):
                for h in range(2):
                    act.wait_ge(hg_mod, 2 * job + h + 1)
                    nc.scalar.copy(hg_hi[:, 4 * h:4 * h + 4, :], hg[:, 4 * h:4 * h + 4, :]).then_inc(hg_high, 1)

            def products_out(job):
                act.wait_ge(e_free, U0 + UPJ * job + SPLITS)
                act.wait_ge(scattered, 2 * job)
                for h in range(2):
                    nc.scalar.copy(y_sb[:, 512 * h:512 * h + 512], ps[:, 6 + h, :]).then_inc(y_out, 1)

            def act_job(job, first=False):
                for k in range(PER_JOB):
                    n = base + k
                    act.wait_ge(loaded[n % SLOTS], loaded_by(job, k))
                    for u in (2 * k, 2 * k + 1):
                        act.wait_ge(e_free, U0 + UPJ * job + u + 1)
                        nc.scalar.copy(w_hi[(U0 + u) % SPLITS][:],
                                       ring[:, n % SLOTS, UNIT * (u % 2):UNIT * (u % 2) + UNIT]).then_inc(e_high, 1)
                    if k == 1:
                        if first:
                            gathered_high(0)
                            act.wait_ge(zeroed, 1)
                        products_out(job)
                    if k == 6:
                        act.wait_ge(sel_turned, job + 1)
                        nc.scalar.copy(selT[:].rearrange("p t n -> p (t n)"), ps[:, 4, 0:T]).then_inc(selT_ready, 1)
                    g = (k - 5) // 4
                    if (k - 5) % 4 == 0 and 0 <= g < FG:
                        act.wait_ge(e_free, U0 + UPJ * job + SPLITS + 2 * (4 * g + 4))
                        act.wait_ge(e_prod, FG * job + g)
                        A(e_sil[:], ps[:, g % 2, :], ACT.Silu).then_inc(e_silu, 1)
                    g = (k - 10) // 4
                    if (k - 10) % 4 == 0 and 0 <= g < FG:
                        act.wait_ge(e_turned, FG * job + g + 1)
                        nc.scalar.copy(eT_hi[:, 4 * g:4 * g + 4, :].rearrange("p f n -> p (f n)"),
                                       ps[:, 4 + g % 2, :]).then_inc(eT_high, 1)
                    if k == 38:
                        gathered_high(job + 1)

            act_job(0, first=True)
            with act.Fori(1, E) as job:
                act_job(job)
            with act.If(more > 0):
                with act.Fori(E, JOBS) as job:
                    act_job(job)
                products_out(JOBS)
            with act.Else():
                products_out(E)
            norm(4)


        @block.vector
        def _(dve):
            link = chain(dve, dve_step)
            V = nc.vector
            TTo, TS, STT = V.tensor_tensor, V.tensor_scalar, V.scalar_tensor_tensor

            def norm_tile(n, t):
                one = slice(t, t + 1)
                dve.wait_ge(squares, 2 * n + t + 1)
                TS(rstd[:, one], sq_sum[:, one], 1.0 / D, EPS, ALU.mult, ALU.add).then_inc(variance, 1)
                dve.wait_ge(deviation, 2 * n + t + 1)
                link(V.reciprocal(rstd[:, one], rstd[:, one]))
                if n < 4:
                    TS(xn[:, t, :], xs[:, t, :], rstd[:, one], None, ALU.mult).then_inc(normed, 1)
                else:
                    dve.wait_ge(fg_in, 16)
                    STT(xn[:, t, :], xs[:, t, :], rstd[:, one], gate_m[:], ALU.mult, ALU.mult).then_inc(normed, 1)

            def norm(n):
                for t in range(TT):
                    norm_tile(n, t)

            def take(l, cg):
                m = MODS.index((l, cg))
                dve.wait_ge(mod_psum, m + 1)
                bank = ps[:, mod_bank(m), :]
                if cg // 2 in (G_M, G_F):
                    dve.wait_ge(gbias_in, 32 if l == 0 else 64)
                    dst = (gate_m if cg // 2 == G_M else (gate_f, gate_f1)[l])[:, 512 * (cg % 2):512 * (cg % 2) + 512]
                    ins = TTo(dst, dst, bank, ALU.add)
                else:
                    if m:
                        dve.wait_ge(mod_taken, m)
                    if (l, cg) in ON_DVE:
                        ins = V.tensor_copy(mod_raw[:, 4 * cg:4 * cg + 4], bank[:, 0:4])
                    for i in () if (l, cg) in ON_DVE else range(4):
                        ins = V.tensor_tensor_reduce(mod_diag[:, i, :], bank[:, P * i:P * i + P], ident, 1.0, 0.0,
                                                     ALU.mult, ALU.add, mod_raw[:, 4 * cg + i:4 * cg + i + 1])
                ins.then_inc(mod_taken, 1)

            def sum_mod(l, cg, ks):
                d = ON_DVE.index((l, cg))
                part = mod_acc[:, d % 3, :]
                for k in ks:
                    w = chunk(dve, at_mod[l, cg] + k // 4)[:, k % 4, :]
                    if k == 0:
                        if d >= 3:
                            dve.wait_ge(mod_psum, MODS.index(ON_DVE[d - 3]) + 1)
                        link(TS(part, w, c_act[:, 0:1], None, ALU.mult))
                    elif k < of_dve(l, cg) - 1:
                        link(STT(part, w, c_act[:, k:k + 1], part, ALU.mult, ALU.add))
                    else:
                        STT(part, w, c_act[:, k:k + 1], part, ALU.mult, ALU.add).then_inc(mod_summed, 1)

            def finish_mod(l, which):
                dve.wait_ge(mod_taken, 12 * l + (4 if which == 0 else 10))
                b = par(l, "b_ada").rearrange("p (m k) -> p m k", k=KC)
                raw = mod_raw[:].rearrange("p (m k) -> p m k", k=KC)
                shift, scale = (SH_M, SC_M) if which == 0 else (SH_F, SC_F)
                link(TTo(mod_s[:, which, :], raw[:, shift, :], b[:, shift, :], ALU.add))
                link(STT(mod_a[:, which, :], raw[:, scale, :], 1.0, b[:, scale, :], ALU.add, ALU.add))
                TTo(mod_a[:, which, :], mod_a[:, which, :], par(l, ("g_mix", "g_ffn")[which]),
                    ALU.mult).then_inc((mod_mix, mod_ffn)[which], 1)
                dve.wait_ge((mod_mix, mod_ffn)[which], l + 1)

            def modulate(n):
                which = n % 2
                dve.wait_ge(turned, 4 * n + 2)
                if which == 0:
                    dve.wait_ge(bcs_read, n // 2 + 1)
                for kc in range(4):
                    TS(hT[:, kc, :], ps[:, 2 + kc // 2, 256 * (kc % 2):256 * (kc % 2) + 256],
                       mod_a[:, which, kc:kc + 1], mod_s[:, which, kc:kc + 1], ALU.mult, ALU.add).then_inc(hT_dve, 1)

            def state_scalars():
                a, b = PRM["lam_re"]
                lre = prms[:, :, a:b]
                a, b = PRM["lam_im"]
                lim = prms[:, :, a:b]
                t1, t2, t3 = sv["t1"][:], sv["t2"][:], sv["t3"][:]
                dve.wait_ge(sv_step, 1)
                TTo(sv["dec"][:], lre, sv["step"][:], ALU.mult)
                link(TTo(t1, lim, sv["step"][:], ALU.mult))
                for m in range(8):
                    ins = TS(pw_c[:, m], t1, float(1 << m), None, ALU.mult)
                link(ins)
                link(TS(pw_s[:], pw_c[:], 1.0 / (2 * math.pi), ROUND, ALU.mult, ALU.add))
                link(TS(pw_s[:], pw_s[:], -ROUND, None, ALU.add))
                for part in (TWO_PI_HI, TWO_PI_MID, TWO_PI_LO):
                    link(STT(pw_c[:], pw_s[:], -part, pw_c[:], ALU.mult, ALU.add))
                TS(pw_c[:], pw_c[:], 3.1415925, -3.1415925, ALU.min, ALU.max).then_inc(sv_angle, 1)
                dve.wait_ge(sv_trig, 1)
                link(TTo(pw_c[:], pw_c[:], pw_c[:], ALU.mult))
                link(TS(pw_c[:], pw_c[:], -2.0, 1.0, ALU.mult, ALU.add))
                dec, cr, ci = sv["dec"][:], sv["cr"][:], sv["ci"][:]
                TTo(t1, dec, pw_c[:, 0], ALU.mult)
                link(TTo(t2, dec, pw_s[:, 0], ALU.mult))
                link(TS(t1, t1, -1.0, None, ALU.add))
                TTo(cr, t1, lre, ALU.mult)
                link(TTo(t3, t2, lim, ALU.mult))
                link(TTo(cr, cr, t3, ALU.add))
                TTo(ci, t2, lre, ALU.mult)
                link(TTo(t3, t1, lim, ALU.mult))
                link(TTo(ci, ci, t3, ALU.subtract))
                TTo(t1, lre, lre, ALU.mult)
                link(TTo(t2, lim, lim, ALU.mult))
                link(TTo(t1, t1, t2, ALU.add))
                link(V.reciprocal(t1, t1))
                TTo(cr, cr, t1, ALU.mult)
                link(TTo(ci, ci, t1, ALU.mult))
                link(TS(t1, cr, -1.0, None, ALU.mult))
                TS(t2, ci, -1.0, None, ALU.mult).then_inc(sv_ready, 1)

            dve.wait_ge(c_silu, 1)
            V.tensor_copy(c_wide[:], c_act[:].unsqueeze(2).to_broadcast([P, KC, P])).then_inc(c_spread, 1)
            dve.wait_ge(params_in, 16)
            state_scalars()
            link(first_columns(V, 0, link, range(5), tab_t[0]))
            norm(0)
            link(first_columns(V, 0, link, range(5, 6), tab_t[0]))

            for l in range(DEPTH):
                if l == 0:
                    dve.wait_ge(const_in, 16)
                    take(0, 0)
                    first_columns(V, 0, link, range(6, 7), tab_t[0]).then_inc(table0, 1)
                    for cg in range(1, 4):
                        take(0, cg)
                    finish_mod(0, 0)
                modulate(2 * l)
                if l == 0:
                    dve.wait_ge(table0, 1)
                    double(V, 0, 7, "cos", link, tab_t[0]).then_inc(table0_cos, 1)
                    dve.wait_ge(table0_cos, 1)
                    dve.wait_ge(table0_sin, 1)
                if l:
                    dve.wait_ge(table1, 1)

                def skip(u):
                    dve.wait_ge(y_psum, 8 * l + 2 * u + 2)
                    d0 = PRM["d_skip"][0] + u
                    STT(yT[:, u, :], uT[:, u, :], prms[:, l, d0:d0 + 1], ps[:, Y_BANK[u % 2], 0:T],
                        ALU.mult, ALU.add).then_inc(y_skip, 1)

                for j in range(8):
                    b = 2 + 2 * (j % 2)
                    re, im = (ps[:, b + m, :].rearrange("p (q n) -> p q n", q=2) for m in (0, 1))
                    cs, sn = cos_t[:, 2 * j:2 * j + 2, :], sin_t[:, 2 * j:2 * j + 2, :]
                    zr, zi = z_re[j % 2], z_im[j % 2]
                    dve.wait_ge(bu_psum, 8 * l + j + 1)
                    if 8 * l + j >= 2:
                        dve.wait_ge(rotated, 8 * l + j - 1)
                    TTo(zr, re, cs, ALU.mult)
                    link(TTo(rot_a[:], im, sn, ALU.mult))
                    link(TTo(zr, zr, rot_a[:], ALU.add))
                    TTo(zi, im, cs, ALU.mult)
                    TTo(rot_b[:], re, sn, ALU.mult).then_inc(bu_used, 1)
                    dve.wait_ge(bu_used, 8 * l + j + 1)
                    link(TTo(zi, zi, rot_b[:], ALU.subtract))
                    for q in range(2):
                        decay = sv["dec"][:, l, 2 * j + q:2 * j + q + 1].to_broadcast([P, T])
                        for v in (zr, zi):
                            ins = V.tensor_tensor_scan(v[:, q, :], decay, v[:, q, :], 0.0, ALU.mult, ALU.add)
                    if l:
                        link(ins)
                        ins = TTo(st_t[j % 2][:], zi, cs, ALU.mult)
                    ins.then_inc(scanned, 1)
                    if j in (3, 5, 7):
                        skip((j - 3) // 2)
                    if l == 0:
                        if j in (2, 4, 6, 7):
                            take(0, {2: 4, 4: 5, 6: 6, 7: 7}[j])
                        if j in (0, 2, 4, 5, 6):
                            cg = (5, 0, 6, 0, 7, 8, 9)[j]
                            sum_mod(0, cg, range(of_dve(0, cg)))

                banks = lambda p0, p1, b: ps[p0:p1, b:b + 2, :].rearrange("p b (h n) -> p (b h) n", n=P)
                dve.wait_ge(scores, 2 * (l + 1))
                V.tensor_reduce(s_max[HD:P, 0, :], banks(HD, P, 2), AX, ALU.max)
                V.tensor_reduce(s_max[0:HD, 0, :], banks(0, HD, 2)[:, :, 0:CH], AX, ALU.max)
                link(V.tensor_reduce(s_max[:, 1, :], banks(0, P, 4), AX, ALU.max))
                sinks = par(l, "sinks").unsqueeze(1).to_broadcast([P, TT, HEADS])
                link(TTo(s_max[:], s_max[:], sinks, ALU.max))
                link(TTo(sinks_e[:], sinks, s_max[:], ALU.subtract))
                skip(3)
                for t in range(TT):
                    dve.wait_ge(rotated, 8 * l + 7 + t)
                    if t == 0:
                        V.memset(sc[0:HD, 0, :, CH:P], NEG)
                    for p0, p1, kn in ((0, HD, CH), (HD, P, P)) if t == 0 else ((0, P, P),):
                        ins = TTo(sc[p0:p1, t, :, 0:kn], banks(p0, p1, 2 + 2 * t)[:, :, 0:kn],
                                  s_max[p0:p1, t, :].unsqueeze(2).to_broadcast([p1 - p0, HEADS, kn]), ALU.subtract)
                    ins.then_inc(shifted, 1)
                for t in range(TT):
                    dve.wait_ge(exps, 3 * l + t + 1)
                    link(V.tensor_reduce(s_den[:, t, :], sc[:, t], AX, ALU.add))
                dve.wait_ge(exps, 3 * (l + 1))
                link(TTo(s_den[:], s_den[:], sinks_e[:], ALU.add))
                link(V.reciprocal(s_den[:], s_den[:]))
                for t in range(TT):
                    TTo(sc[:, t], sc[:, t], s_den[:, t, :].unsqueeze(2).to_broadcast([P, HEADS, P]),
                        ALU.mult).then_inc(probs, 1)

                dve.wait_ge(glu_sig, 4 * (l + 1))
                link(TTo(yT[:, 0:UT, :], yT[:, 0:UT, :], sig[:], ALU.mult))
                TTo(sig[:], yT[:, 0:UT, :], yT[:, 0:UT, :], ALU.mult).then_inc(ssm_sq, 1)
                dve.wait_ge(ssm_sq, 2 * l + 1)
                for u in range(UT):
                    g0 = PRM["g_ssm"][0] + u
                    ins = TS(yT[:, u, :], yT[:, u, :], prms[:, l, g0:g0 + 1], None, ALU.mult)
                ins.then_inc(ssm_sq, 1)

                if l == 0:
                    take(0, 8)
                    take(0, 9)
                    finish_mod(0, 1)
                dve.wait_ge(pv_psum, l + 1)
                for b in range(2):
                    src = ps[:, 6 + b, :].rearrange("p (c j n) -> p j c n", c=2, j=HPK)
                    dst = yT[:, UT:2 * UT, P * b:P * b + P].rearrange("p j (c n) -> p j c n", c=2)
                    ins = V.tensor_copy(dst, src)
                link(ins)
                dve.wait_ge(ss_psum, 2 * l + 1)
                TTo(sig[:], yT[:, UT:2 * UT, :], yT[:, UT:2 * UT, :], ALU.mult).then_inc(attn_sq, 1)
                dve.wait_ge(attn_sq, 2 * l + 1)
                for u in range(UT):
                    g0 = PRM["g_attn"][0] + u
                    ins = TS(yT[:, UT + u, :], yT[:, UT + u, :], prms[:, l, g0:g0 + 1], None, ALU.mult)
                ins.then_inc(attn_sq, 1)
                dve.wait_ge(ss_psum, 2 * (l + 1))
                TS(head_ss[:, 0:2], ps[:, 4, 0:2], 1.0 / D_SSM, EPS, ALU.mult, ALU.add)
                TS(head_ss[:, 2:4], ps[:, 5, 0:2], 1.0 / D_SSM, EPS, ALU.mult, ALU.add).then_inc(head_var, 1)
                dve.wait_ge(head_dev, l + 1)
                V.reciprocal(head_rs[:], head_rs[:]).then_inc(head_ready, 1)
                dve.wait_ge(head_ready, l + 1)
                def join(t, n, bank, rs):
                    part = slice(512 * n, 512 * n + 512)
                    link(STT(resid[:, n, :], ps[:, bank, :], head_rs[:, rs:rs + 1], gate_m[:, part],
                             ALU.mult, ALU.mult))
                    return TTo(xs[:, t, part], xs[:, t, part], resid[:, n, :], ALU.add)

                for n in range(2):
                    for t in range(TT):
                        dve.wait_ge(out_psum, 5 * l + (1, 1, 2, 3)[2 * n + t])
                        link(join(t, n, 2 * n + t, t))
                for t in range(TT):
                    dve.wait_ge(out_psum, 5 * l + 4 + t)
                    link(join(t, 0, 4 + 2 * t, 2 + t))
                    join(t, 1, 5 + 2 * t, 2 + t).then_inc(x_updated, 1)
                    norm_tile(2 * l + 1, t)
                if l == 0:
                    def low(g, i):
                        dve.wait_ge(e_high, 4 * g + i + 1)
                        part = ring[:, (at_gu[g] + i // 2) % SLOTS, UNIT * (i % 2):UNIT * (i % 2) + UNIT]
                        TTo(w_lo[i][:], part, w_hi[i][:].bitcast(F32), ALU.subtract).then_inc(e_low, 1)

                    low(0, 0)
                modulate(2 * l + 1)
                if l == 0:
                    low(0, 1)
                    for half in range(2):
                        dve.wait_ge(hT_high, half + 1)
                        part = slice(4 * half, 4 * half + 4)
                        TTo(hT_lo[:, part, :], hT[:, part, :], hT_hi[:, part, :].bitcast(F32),
                            ALU.subtract).then_inc(hT_split, 1)

                    def product(g):
                        dve.wait_ge(gu_silu, g + 1)
                        TTo(a_T[:, 2 * g:2 * g + 2, :].rearrange("p f n -> p (f n)"), sil[:],
                            ps[:, 3 + 2 * (g % 2), :], ALU.mult).then_inc(gu_out, 1)

                    for g in range(GG):
                        for i in range(4):
                            if g or i >= 2:
                                low(g, i)
                            if g - 1 in GU_MODS:
                                sum_mod(*FFN_MODS[GU_MODS.index(g - 1)], (2 * i, 2 * i + 1))
                            if i == 2 and g - 2 in GU_MODS:
                                take(*FFN_MODS[GU_MODS.index(g - 2)])
                        if g:
                            product(g - 1)

                    def low_down(n):
                        for i in range(2):
                            u = 4 * GG + 2 * n + i
                            dve.wait_ge(e_high, u + 1)
                            TTo(w_lo[u % SPLITS][:], ring[:, at_down[n] % SLOTS, UNIT * i:UNIT * i + UNIT],
                                w_hi[u % SPLITS][:].bitcast(F32), ALU.subtract).then_inc(e_low, 1)

                    low_down(0)
                    product(GG - 1)
                    for n in range(GG):
                        if n:
                            low_down(n)
                        dve.wait_ge(a_high, n + 1)
                        TTo(a_lo[:, n % 2], a_T[:, 2 * n:2 * n + 2, :], a_hi[:, n % 2].bitcast(F32),
                            ALU.subtract).then_inc(a_split, 1)
                        if n - 1 in DOWN_MODS:
                            sum_mod(*FFN_MODS[len(GU_MODS) + DOWN_MODS.index(n - 1)], range(KC))
                        if n - 3 in DOWN_MODS:
                            take(*FFN_MODS[len(GU_MODS) + DOWN_MODS.index(n - 3)])
                    finish_mod(1, 0)
                    finish_mod(1, 1)
                    for t in range(TT):
                        dve.wait_ge(*((down_psum, 1), (e_free, U0 + SPLITS))[t])
                        for n in range(2):
                            bank = (6, 7, 0, 1)[2 * t + n]
                            part = slice(512 * n, 512 * n + 512)
                            link(TTo(resid[:, n, :], ps[:, bank, :], gate_f[:, part], ALU.mult))
                            ins = TTo(xs[:, t, part], xs[:, t, part], resid[:, n, :], ALU.add)
                            if n == 0:
                                link(ins)
                        ins.then_inc(x_updated, 1)
                        if t == 0:
                            dve.wait_ge(table1, 1)
                        norm_tile(2, t)

            dve.wait_ge(logits, 1)
            link(V.tensor_copy(lg[:].rearrange("p t e -> p (t e)"), ps[:, 6, 0:TT * E]))
            for t in range(TT):
                link(V.max(top[:, t, :], lg[:, t, :]))
                link(V.max_index(idx[:, t, :], top[:, t, :], lg[:, t, :]))
            link(V.tensor_copy(idx_f[:], idx[:]))
            TTo(g2[:], top[:, :, 1], top[:, :, 0], ALU.subtract).then_inc(diff, 1)
            iota = const("iota")
            for t in range(TT):
                TS(oh1[:, t, :], iota[:, 0:E], idx_f[:, t, 0:1], None, ALU.is_equal)
                link(TS(oh2[:, t, :], iota[:, 0:E], idx_f[:, t, 1:2], None, ALU.is_equal))
            link(V.memset(gate_of[:, :, 0:1], 0.0))
            TTo(chosen[:, :, 0:E], oh1[:], oh2[:], ALU.add)
            TTo(chosen[:, :, E:2 * E], oh1[:], oh2[:], ALU.add)
            TTo(chosen[:, :, 2 * E:], oh1[:, :, 0:1], oh2[:, :, 0:1], ALU.add).then_inc(picked, 1)
            dve.wait_ge(diff_e, 1)
            link(TS(g1[:], g2[:], 1.0, None, ALU.add))
            link(V.reciprocal(g1[:], g1[:]))
            link(TTo(g2[:], g2[:], g1[:], ALU.mult))
            for t in range(TT):
                link(TS(oh1[:, t, :], oh1[:, t, :], g1[:, t:t + 1], None, ALU.mult))
                link(STT(gate_of[:, t, 1:E + 1], oh2[:, t, :], g2[:, t:t + 1], oh1[:, t, :], ALU.mult, ALU.add))
            link(V.tensor_copy(gate_of[:, :, E + 1:], gate_of[:, :, 1:E + 1]))
            dve.wait_ge(rank_psum, 1)
            r = ps[:, 7, 0:TT * E].rearrange("p (t e) -> p t e", t=TT)
            V.tensor_copy(rank[:, :, 0:E], r)
            TS(rank[:, :, E:2 * E], r, -float(CAP), None, ALU.add)
            V.tensor_copy(rank[:, :, 2 * E:], r[:, :, 0:1])
            link(V.tensor_reduce(over_f[:], ps[:, 7, 16:16 + E], AX, ALU.max))
            TS(over[:], over_f[:], float(CAP), None, ALU.is_gt).then_inc(routed, 1)
            dve.wait_ge(routed, 1)
            more = dve.value_load(over[0:1, 0:1], min_val=0, max_val=1)

            def choose(job):
                for t in range(TT):
                    TS(sel[:, t, :], iota, rank[:, t, bass.ds(job, 1)], chosen[:, t, bass.ds(job, 1)],
                       ALU.is_equal, ALU.mult).then_inc(sel_made, 1)

            def gathered_mod(job):
                for kc in range(KC):
                    if kc % 4 == 0:
                        dve.wait_ge(gathered, 2 * job + kc // 4 + 1)
                    TS(hg[:, kc, :], ps[:, 2 * (kc // 4), P * (kc % 4):P * (kc % 4) + P],
                       mod_a[:, 1, kc:kc + 1], mod_s[:, 1, kc:kc + 1], ALU.mult, ALU.add).then_inc(
                           hg_mod if kc % 4 == 3 else dve_job, 1)

            def gathered_low(job):
                for h in range(2):
                    dve.wait_ge(hg_high, 2 * job + h + 1)
                    TTo(hg_lo[:, 4 * h:4 * h + 4, :], hg[:, 4 * h:4 * h + 4, :],
                        hg_hi[:, 4 * h:4 * h + 4, :].bitcast(F32), ALU.subtract).then_inc(hg_ready, 1)

            def add_products(job):
                dve.wait_ge(added, 4 * job)
                for t in range(TT):
                    dve.wait_ge(scattered, 2 * job + t + 1)
                    for h in range(2):
                        part = slice(512 * h, 512 * h + 512)
                        STT(acc[:, t, part], ps[:, (4, 5, 1, 3)[2 * t + h], :], gate_of[:, t, bass.ds(job, 1)],
                            acc[:, t, part], ALU.mult, ALU.add).then_inc(added, 1)

            choose(0)

            def dve_one(job, first=False):
                for k in range(PER_JOB):
                    n = base + k
                    for u in (2 * k, 2 * k + 1):
                        dve.wait_ge(e_high, U0 + UPJ * job + u + 1)
                        TTo(w_lo[(U0 + u) % SPLITS][:], ring[:, n % SLOTS, UNIT * (u % 2):UNIT * (u % 2) + UNIT],
                            w_hi[(U0 + u) % SPLITS][:].bitcast(F32), ALU.subtract).then_inc(e_low, 1)
                    if k == 0 and first:
                        gathered_mod(0)
                        gathered_low(0)
                        link(V.memset(selT[:], 0.0))
                        link(V.memset(ps[:, 6:8, :], 0.0))
                        V.memset(acc[:], 0.0).then_inc(zeroed, 1)
                        dve.wait_ge(zeroed, 1)
                    if k == 3:
                        add_products(job)
                    g = (k - 5) // 4
                    if (k - 5) % 4 == 0 and 0 <= g < FG:
                        dve.wait_ge(e_silu, FG * job + g + 1)
                        TTo(e_act[:, 512 * g:512 * g + 512], e_sil[:], ps[:, 2 + g % 2, :], ALU.mult).then_inc(e_prod, 1)
                    g = (k - 10) // 4
                    if (k - 10) % 4 == 0 and 0 <= g < FG:
                        dve.wait_ge(eT_high, FG * job + g + 1)
                        hi = eT_hi[:, 4 * g:4 * g + 4, :].rearrange("p f n -> p (f n)").bitcast(F32)
                        TTo(eT_lo[:, 4 * g:4 * g + 4, :].rearrange("p f n -> p (f n)"), ps[:, 4 + g % 2, :], hi,
                            ALU.subtract).then_inc(eT_ready, 1)
                    if k == 31:
                        dve.wait_ge(sel_turned, job + 1)
                        choose(job + 1)
                    if k == 37:
                        gathered_mod(job + 1)
                    if k == 39:
                        gathered_low(job + 1)

            dve_one(0, first=True)
            with dve.Fori(1, E) as job:
                dve_one(job)
            with dve.If(more > 0):
                with dve.Fori(E, JOBS) as job:
                    dve_one(job)
                dve.wait_ge(added, 4 * JOBS)
            with dve.Else():
                dve.wait_ge(added, 4 * E)
            for t in range(TT):
                link(TTo(acc[:, t, :], acc[:, t, :], gate_f1[:], ALU.mult))
                link(TTo(xs[:, t, :], xs[:, t, :], acc[:, t, :], ALU.add))
            for t in range(TT):
                dve.wait_ge(last_scattered, t + 1)
                for h in range(2):
                    part = slice(512 * h, 512 * h + 512)
                    link(STT(acc[:, t, part], ps[:, (4, 5, 1, 3)[2 * t + h], :], gate_of[:, t, E:E + 1],
                             gate_f1[:, part], ALU.mult, ALU.mult))
                    ins = TTo(xs[:, t, part], xs[:, t, part], acc[:, t, part], ALU.add)
                ins.then_inc(x_updated, 1)
            norm(4)

        @block.tensor
        def _(pe):
            M = nc.tensor.matmul

            def mod_wide(l, cg):
                m = MODS.index((l, cg))
                if m >= 4:
                    pe.wait_ge(mod_taken, m)
                for half in range(2):
                    w = chunk(pe, at_mod[l, cg] + half)
                    for k in range(4):
                        ins = M(ps[:, mod_bank(m), :], c_wide[:, 4 * half + k, :], w[:, k, :],
                                start=(half == 0 and k == 0), stop=(half == 1 and k == 3))
                ins.then_inc(mod_psum, 1)

            def mod_ones(l, cg):
                m, d = MODS.index((l, cg)), ON_DVE.index((l, cg))
                pe.wait_ge(mod_taken, m if m <= 10 else m - 1)
                pe.wait_ge(mod_summed, d + 1)
                part = mod_acc[:, d % 3, :]
                k0 = of_dve(l, cg)
                rest = [(k, chunk(pe, at_mod[l, cg] + 1)[:, k - 4, :]) for k in range(k0, KC)]
                if cg // 2 in (G_M, G_F):
                    ins = M(ps[:, mod_bank(m), :], ones, part, start=True, stop=not rest)
                    for k, w in rest:
                        ins = M(ps[:, mod_bank(m), :], c_wide[:, k, :], w, start=False, stop=(k == KC - 1))
                else:
                    for i in range(4):
                        c = slice(P * i, P * i + P)
                        ins = M(ps[:, mod_bank(m), i:i + 1], part[:, c], ones[:, 0:1], start=True, stop=not rest)
                        for k, w in rest:
                            ins = M(ps[:, mod_bank(m), i:i + 1], w[:, c], c_act[:, k:k + 1],
                                    start=False, stop=(k == KC - 1))
                ins.then_inc(mod_psum, 1)

            def turn(n):
                for t in range(TT):
                    pe.wait_ge(normed, 2 * n + t + 1)
                    for kc in range(KC):
                        c0 = 256 * (kc % 2) + P * t
                        ins = nc.tensor.transpose(ps[:, 2 + kc // 2, c0:c0 + P], xn[:, t, P * kc:P * kc + P], ident)
                        if kc % 2 and t == TT - 1:
                            ins.then_inc(turned, 1)

            AS_READY = (0, 4, 1, 5, 2, 6, 3, 7)

            def wait_channels(n, kc):
                pe.wait_ge(hT_dve if kc < 4 else hT_act, 4 * n + kc % 4 + 1)

            pe.wait_ge(c_spread, 1)
            for cg in range(4):
                mod_wide(0, cg)

            pe.wait_ge(const_in, 16)
            for l in range(DEPTH):
                turn(2 * l)

                def project(n):
                    kind, which = UNITS[n]
                    chunk_at, c0 = in_chunk(kind, which)
                    w = chunk(pe, at_in[l, chunk_at])
                    if 12 * l + n:
                        pe.wait_ge(proj_out, 12 * l + n)
                    for i, kc in enumerate(AS_READY):
                        if n == 0:
                            wait_channels(2 * l, kc)
                        if kind == "v":
                            ins = M(ps[:, 7, 0:P], hT[:, kc, CH * which:CH * which + P], w[:, kc, c0:c0 + P],
                                    start=(i == 0), stop=(i == KC - 1))
                        else:
                            ins = M(ps[:, 7, 0:T], w[:, kc, c0:c0 + P], hT[:, kc, :], start=(i == 0), stop=(i == KC - 1))
                    ins.then_inc(projected, 1)

                def drive(j):
                    pe.wait_ge(proj_out, 12 * l + UNITS.index(("u", j // 2)) + 1)
                    pe.wait_ge(matrices, l + 1)
                    if j >= 2:
                        pe.wait_ge(bu_used, 8 * l + j - 1)
                    for m, mat in ((0, b_re), (1, b_im)):
                        for q in range(2):
                            ins = M(ps[:, 2 + 2 * (j % 2) + m, T * q:T * q + T], mat[:, 2 * j + q, :], uT[:, j // 2, :],
                                    start=True, stop=True)
                    ins.then_inc(bu_psum, 1)

                def read_out(j):
                    pe.wait_ge(rotated, 8 * l + j + 1)
                    if j % 2 == 0 and j >= 4:
                        pe.wait_ge(y_skip, 4 * l + j // 2 - 1)
                    for q in range(2):
                        for mat, st in ((c_re, st_re[j % 2]), (c_im, st_im[j % 2])):
                            first = j % 2 == 0 and q == 0 and mat is c_re
                            ins = M(ps[:, Y_BANK[j // 2 % 2], 0:T], mat[:, 2 * j + q, :], st[:, q, :], start=first,
                                    stop=(j % 2 == 1 and q == 1 and mat is c_im))
                    ins.then_inc(y_psum, 1)

                def score():
                    pe.wait_ge(proj_out, 12 * l + UNITS.index(("k", 0)) + 1)
                    pe.wait_ge(bu_used, 8 * (l + 1))
                    for t in range(TT):
                        for h in range(KVH):
                            for j in range(HPK):
                                for c in (2 * t, 2 * t + 1):
                                    k0 = CH * max(c - 1, 0)
                                    kn = CH if c == 0 else P
                                    p0 = CH * (c % 2)
                                    ins = M(ps[p0:p0 + CH, 2 + 2 * t + h, P * j:P * j + kn], qT[:, j, CH * c:CH * c + CH],
                                            kz[:, h, k0:k0 + kn], start=True, stop=True)
                        ins.then_inc(scores, 1)

                project(0)
                drive(0)
                project(1)
                drive(1)
                project(2)
                project(3)
                for j in range(8):
                    if j + 2 < 8:
                        drive(j + 2)
                    project(4 + j)
                    if l == 0 and j == 0:
                        mod_wide(0, 4)
                    if l == 0 and j in (2, 4, 6):
                        mod_ones(0, 4 + j // 2)
                    if j == 6:
                        score()
                    read_out(j)

                pe.wait_ge(y_gelu, 4 * (l + 1))
                pe.wait_ge(y_skip, 4 * (l + 1))
                w = chunk(pe, at_glu[l])
                for o in range(UT):
                    for k in range(UT):
                        ins = M(ps[:, 6 + o // 2, T * (o % 2):T * (o % 2) + T], w[:, k, P * o:P * o + P], yT[:, k, :],
                                start=(k == 0), stop=(k == UT - 1))
                    ins.then_inc(glu_psum, 1)

                def project_out(n, t, bank):
                    w = chunk(pe, at_out[l, n])
                    for k in range(4):
                        ins = M(ps[:, bank, :], yT[:, 4 * (n // 2) + k, P * t:P * t + P], w[:, k, :],
                                start=(k == 0), stop=(k == 3))
                    return ins

                def sum_squares(bank):
                    for t in range(TT):
                        for k in range(UT):
                            ins = M(ps[:, bank, t:t + 1], sig[:, k, P * t:P * t + P], ones[:, 0:1],
                                    start=(k == 0), stop=(k == UT - 1))
                    ins.then_inc(ss_psum, 1)

                if l == 0:
                    mod_ones(0, 8)
                for t in range(TT):
                    pe.wait_ge(probs, 2 * l + t + 1)
                    for h in range(HEADS):
                        ins = nc.tensor.transpose(ps[:, 2 + 2 * t + h // 4, P * (h % 4):P * (h % 4) + P],
                                                  sc[:, t, h, :], ident)
                    ins.then_inc(probs_T, 1)
                if l == 0:
                    mod_ones(0, 9)
                pe.wait_ge(glu_sig, 4 * (l + 1))
                pe.wait_ge(pT_act, 2 * (l + 1))
                pe.wait_ge(proj_out, 12 * (l + 1))
                for c in range(NCH):
                    window = (0, 0, 1, 2)[c]
                    for h in range(KVH):
                        o = ps[HD * h:HD * h + HD, 6 + c // 2, T * (c % 2):T * (c % 2) + T]
                        ins = M(o.rearrange("p (j n) -> p j n", j=HPK), vt[:, window, HD * h:HD * h + HD],
                                pT[:, c // 2, HPK * h:HPK * h + HPK, CH * (c % 2):CH * (c % 2) + CH],
                                start=True, stop=True)
                ins.then_inc(pv_psum, 1)

                pe.wait_ge(ssm_sq, 2 * l + 1)
                sum_squares(4)
                pe.wait_ge(ssm_sq, 2 * (l + 1))
                pe.wait_ge(mod_ffn, l + 1)
                project_out(0, 0, 0)
                project_out(0, 1, 1).then_inc(out_psum, 1)
                project_out(1, 0, 2).then_inc(out_psum, 1)
                pe.wait_ge(attn_sq, 2 * l + 1)
                sum_squares(5)
                project_out(1, 1, 3).then_inc(out_psum, 1)
                pe.wait_ge(attn_sq, 2 * (l + 1))
                for t in range(TT):
                    if t == 0:
                        pe.wait_ge(head_var, l + 1)
                    project_out(2, t, 4 + 2 * t)
                    project_out(3, t, 5 + 2 * t).then_inc(out_psum, 1)

                if l == 0:
                    pe.wait_ge(out_psum, 5)
                    pe.sem_inc(e_free, 2)
                turn(2 * l + 1)
                if l == 0:
                    pe.sem_inc(e_free, SPLITS - 2)
                    for g in range(GG):
                        if g >= 2:
                            pe.wait_ge(gu_out, g - 1)
                        for i in range(4):
                            pe.wait_ge(e_low, 4 * g + i + 1)
                            if g == 0 and i < 2:
                                pe.wait_ge(hT_split, i + 1)
                            hi, lo = (v[i][:].rearrange("p (k n) -> p k n", k=4) for v in (w_hi, w_lo))
                            for kk in range(4):
                                kc = 4 * (i % 2) + kk
                                for f in range(2):
                                    o = ps[:, 2 + 2 * (g % 2) + i // 2, T * f:T * f + T]
                                    part = slice(P * f, P * f + P)
                                    M(o, hi[:, kk, part], hT_hi[:, kc, :], start=(kc == 0 and f == 0), stop=False,
                                      skip_group_check=True)
                                    M(o, hi[:, kk, part], hT_lo[:, kc, :], start=False, stop=False,
                                      skip_group_check=True)
                                    ins = M(o, lo[:, kk, part], hT_hi[:, kc, :], start=False, stop=(kc == KC - 1),
                                            skip_group_check=True)
                            ins.then_inc(e_free, 1)
                        if g - 1 in GU_MODS:
                            mod_ones(*FFN_MODS[GU_MODS.index(g - 1)])
                    pe.wait_ge(gu_out, GG)
                    pe.wait_ge(mod_taken, 10 + len(GU_MODS))
                    for n in range(GG):
                        pe.wait_ge(a_split, n + 1)
                        for k in range(2):
                            f = 2 * n + k
                            u = 4 * GG + f
                            hi, lo = w_hi[u % SPLITS], w_lo[u % SPLITS]
                            pe.wait_ge(e_low, u + 1)
                            for t in range(TT):
                                tokens = slice(P * t, P * t + P)
                                for h in range(2):
                                    bank, part = ps[:, (6, 7, 0, 1)[2 * t + h], :], slice(512 * h, 512 * h + 512)
                                    M(bank, a_hi[:, n % 2, k, tokens], hi[:, part], start=(f == 0), stop=False)
                                    M(bank, a_lo[:, n % 2, k, tokens], hi[:, part], start=False, stop=False)
                                    ins = M(bank, a_hi[:, n % 2, k, tokens], lo[:, part],
                                            start=False, stop=(f == FT - 1))
                                if f == FT - 1 and t == 0:
                                    ins.then_inc(down_psum, 1)
                            ins.then_inc(e_free, 1)
                        if n - 2 in DOWN_MODS:
                            mod_ones(*FFN_MODS[len(GU_MODS) + DOWN_MODS.index(n - 2)])

            for t in range(TT):
                for i, kc in enumerate(AS_READY):
                    if t == 0:
                        wait_channels(3, kc)
                    ins = M(ps[:, 6, E * t:E * t + E], hT[:, kc, P * t:P * t + P], w_router[:, kc, :],
                            start=(i == 0), stop=(i == KC - 1))
            ins.then_inc(logits, 1)
            pe.wait_ge(picked, 1)
            M(ps[:, 7, 0:E], const("before"), chosen[:, 0, 0:E], start=True, stop=True)
            M(ps[:, 7, E:2 * E], const("before"), chosen[:, 1, 0:E], start=True, stop=False)
            M(ps[:, 7, E:2 * E], ones, chosen[:, 0, 0:E], start=False, stop=True)
            M(ps[:, 7, 2 * E:3 * E], ones, chosen[:, 0, 0:E], start=True, stop=False)
            M(ps[:, 7, 2 * E:3 * E], ones, chosen[:, 1, 0:E], start=False, stop=True).then_inc(rank_psum, 1)
            pe.wait_ge(routed, 1)
            more = pe.value_load(over[0:1, 0:1], min_val=0, max_val=1)

            def gather(job):
                pe.wait_ge(sel_made, TT * (job + 1))
                for kc in range(KC):
                    for t in range(TT):
                        ins = M(ps[:, 2 * (kc // 4), P * (kc % 4):P * (kc % 4) + P], xn[:, t, P * kc:P * kc + P],
                                sel[:, t, :], start=(t == 0), stop=(t == TT - 1))
                    if kc % 4 == 3:
                        ins.then_inc(gathered, 1)

            def scatter(job, done=scattered):
                pe.wait_ge(y_out, 2 * (job + 1))
                for t in range(TT):
                    for h in range(2):
                        ins = M(ps[:, (4, 5, 1, 3)[2 * t + h], :], selT[:, t, :], y_sb[:, 512 * h:512 * h + 512],
                                start=True, stop=True)
                    ins.then_inc(done, 1)

            gather(0)

            def pe_one(job):
                for k in range(PER_JOB):
                    if k < 2:
                        pe.wait_ge(hg_ready, 2 * job + k + 1)
                    if k < 4 * FG:
                        g, which, half = k // 4, k // 2 % 2, k % 2
                        bank = ps[:, 2 * which + g % 2, :]
                        if half == 0 and which == 0 and g == 1:
                            pe.wait_ge(added, 4 * (job + 1))
                        if half == 0 and which == 0 and g >= 2:
                            pe.wait_ge(e_prod, FG * job + g - 1)
                        for i in range(2):
                            u = 2 * k + i
                            hi, lo = w_hi[(U0 + u) % SPLITS], w_lo[(U0 + u) % SPLITS]
                            pe.wait_ge(e_low, U0 + UPJ * job + u + 1)
                            for kc in range(2):
                                kk = 4 * half + 2 * i + kc
                                part = slice(512 * kc, 512 * kc + 512)
                                M(bank, hg_hi[:, kk, :], hi[:, part], start=(kk == 0), stop=False)
                                M(bank, hg_lo[:, kk, :], hi[:, part], start=False, stop=False)
                                ins = M(bank, hg_hi[:, kk, :], lo[:, part], start=False, stop=(kk == KC - 1))
                            ins.then_inc(e_free, 1)
                    else:
                        for i in range(2):
                            u = 2 * k + i
                            hi, lo = w_hi[(U0 + u) % SPLITS], w_lo[(U0 + u) % SPLITS]
                            pe.wait_ge(e_low, U0 + UPJ * job + u + 1)
                            f = 2 * (k - 4 * FG) + i
                            if f % 4 == 0:
                                pe.wait_ge(eT_ready, FG * job + f // 4 + 1)
                            for h in range(2):
                                part = slice(512 * h, 512 * h + 512)
                                bank = ps[:, 6 + h, :]
                                M(bank, eT_hi[:, f, :], hi[:, part], start=(f == 0), stop=False)
                                M(bank, eT_lo[:, f, :], hi[:, part], start=False, stop=False)
                                ins = M(bank, eT_hi[:, f, :], lo[:, part], start=False, stop=(f == FE_T - 1))
                            ins.then_inc(e_free, 1)
                    if k == 1:
                        scatter(job)
                    if k == 3:
                        pe.wait_ge(sel_made, TT * (job + 1))
                        pe.wait_ge(added, 4 * job + 1)
                        for t in range(TT):
                            ins = nc.tensor.transpose(ps[:, 4, P * t:P * t + P], sel[:, t, :], ident)
                        ins.then_inc(sel_turned, 1)
                    for g in range(FG):
                        if k == (4 * g + 7 if g < FG - 1 else 30):
                            pe.wait_ge(e_prod, FG * job + g + 1)
                            if g >= 2:
                                pe.wait_ge(eT_ready, FG * job + g - 1)
                            if g == 0:
                                pe.wait_ge(selT_ready, job + 1)
                            for i in range(4):
                                f = 4 * g + i
                                ins = nc.tensor.transpose(ps[:, 4 + g % 2, P * i:P * i + P],
                                                          e_act[:, P * f:P * f + P], ident)
                            ins.then_inc(e_turned, 1)
                    if k == 34:
                        gather(job + 1)

            with pe.Fori(0, E) as job:
                pe_one(job)
            with pe.If(more > 0):
                with pe.Fori(E, JOBS) as job:
                    pe_one(job)
                scatter(JOBS, last_scattered)
            with pe.Else():
                scatter(E, last_scattered)


def kernel(x, c, norm_mix_g, norm_ffn_g, w_ada, b_ada, w_in, ssm_lam_re, ssm_lam_im,
           ssm_b_re, ssm_b_im, ssm_c_re, ssm_c_im, ssm_d, ssm_log_step, ssm_w_glu,
           attn_sinks, out_norm_ssm_g, out_norm_attn_g, w_out, ffn_w_gate, ffn_w_up,
           ffn_w_down, moe_w_router, moe_w_gate, moe_w_up, moe_w_down, final_norm_g):
    import numpy as np
    import concourse.bacc as bacc
    from concourse.bass_utils import run_bass_kernel_spmd

    f = lambda a: np.ascontiguousarray(np.asarray(a))
    cols = lambda v: np.asarray(v).reshape(-1, P).T
    order = np.arange(HEADS).reshape(KVH, HPK).T.reshape(-1)
    by_head = (order[:, None] * HD + np.arange(HD)[None, :]).reshape(-1)
    w_in, w_out = np.array(w_in), np.array(w_out)
    w_in[:, :, D_SSM:D_SSM + 512] = w_in[:, :, D_SSM + by_head]
    w_out[:, D_SSM:] = w_out[:, D_SSM + by_head]
    states = lambda v: np.asarray(v).reshape(PAIRS, P).T

    layer = lambda make: np.stack([make(l) for l in range(DEPTH)])
    prm = np.concatenate([
        layer(lambda l: cols(b_ada[l])), layer(lambda l: cols(norm_mix_g[l])), layer(lambda l: cols(norm_ffn_g[l])),
        layer(lambda l: states(ssm_lam_re[l])), layer(lambda l: states(ssm_lam_im[l])),
        layer(lambda l: states(np.repeat(np.asarray(ssm_log_step[l]), STATE))),
        layer(lambda l: cols(ssm_d[l])), layer(lambda l: cols(out_norm_ssm_g[l])),
        layer(lambda l: cols(np.asarray(out_norm_attn_g[l])[by_head])),
        layer(lambda l: np.broadcast_to(np.asarray(attn_sinks[l]), (P, HEADS))),
    ], axis=2).transpose(1, 0, 2)
    b_lay = lambda v: np.asarray(v).transpose(0, 2, 1).reshape(UT, P, STATE).transpose(1, 0, 2).reshape(P, -1)
    c_lay = lambda v: np.asarray(v).transpose(0, 2, 1).reshape(PAIRS, P, GROUP).transpose(1, 0, 2).reshape(P, -1)
    bc = np.stack([np.stack([b_lay(ssm_b_re[l]), b_lay(ssm_b_im[l]), c_lay(ssm_c_re[l]), c_lay(ssm_c_im[l])], 1)
                   for l in range(DEPTH)])
    small = np.concatenate([cols(c[0]), np.asarray(moe_w_router[0]).reshape(KC, P, E).transpose(1, 0, 2).reshape(P, -1)], 1)

    i = np.arange(P)
    cst = np.concatenate([
        np.eye(P), i[:, None] < i[None, :], np.ones((P, P)), np.broadcast_to(i, (P, P)),
        i[:, None] // GROUP == np.arange(GT)[None, :],
        (2 * np.arange(4)[None, :, None] + i[:, None, None] // STATE == np.arange(GT)).reshape(P, -1),
    ], axis=1).astype(np.float32)

    nc = bacc.Bacc("TRN2", target_bir_lowering=False, num_devices=1)
    arrays, args = {}, []
    for name, a in (("x", x), ("small", small), ("prm", prm), ("bc", bc), ("cst", cst), ("w_ada", w_ada),
                    ("b_ada", b_ada), ("w_in", w_in), ("w_glu", ssm_w_glu), ("w_out", w_out),
                    ("w_gate", ffn_w_gate), ("w_up", ffn_w_up), ("w_down", ffn_w_down), ("moe_gate", moe_w_gate),
                    ("moe_up", moe_w_up), ("moe_down", moe_w_down), ("final_g", final_norm_g)):
        arrays[name + "_dram"] = f(a)
        args.append(nc.dram_tensor(name + "_dram", arrays[name + "_dram"].shape, F32, kind="ExternalInput").ap())
    args.append(nc.dram_tensor("out_dram", (1, T, D), F32, kind="ExternalOutput").ap())
    build(nc, *args)
    r = run_bass_kernel_spmd(nc, [arrays], core_ids=[0])
    return r.results[0]["out_dram"]
```
